# Optimizing a Trainium2 kernel written in Bass

```python
import math
import jax, jax.numpy as jnp
from jax import lax
import numpy as np

D_MODEL = 1024
BATCH = 1
SEQ = 256
DEPTH = 2

N_MIXERS = 2
N_A_LAYERS = (DEPTH + 1) // 2
N_B_LAYERS = DEPTH // 2

S5_WIDTH = D_MODEL // 2
S5_GROUP = 16
S5_GROUPS = S5_WIDTH // S5_GROUP
S5_STATE = 64
DT_MIN = 0.001
DT_MAX = 0.1

SB_HEAD_DIM = 64
SB_HEADS = D_MODEL // SB_HEAD_DIM
Q_BLOCK = 128

D_FF = 7 * D_MODEL // 2
N_EXPERTS = 8
TOP_K = 2
NORM_EPS = 1e-6

kernel_name = "hybrid_s5_stickbreaking_moe_sandwich_adaln"

def rmsnorm(x, g):
    xf = x.astype(jnp.float32)
    xf = xf * lax.rsqrt(jnp.mean(xf * xf, axis=-1, keepdims=True) + NORM_EPS)
    return xf.astype(x.dtype) * g

def swiglu(h, w_gate_up, w_down):
    gate, up = jnp.split(h @ w_gate_up, 2, axis=-1)
    return (jax.nn.silu(gate) * up) @ w_down

def _complex_linear_combine(left, right):
    a1r, a1i, b1r, b1i = left
    a2r, a2i, b2r, b2i = right
    return (a2r * a1r - a2i * a1i,
            a2r * a1i + a2i * a1r,
            a2r * b1r - a2i * b1i + b2r,
            a2r * b1i + a2i * b1r + b2i)

def s5_mixer(h, w_in, lam_re, lam_im, b_re, b_im, c_re, c_im, d_skip, log_step, w_out):
    bsz, seq, _ = h.shape
    f32 = jnp.float32
    lam_re, lam_im = lam_re.astype(f32), lam_im.astype(f32)
    b_re, b_im = b_re.astype(f32), b_im.astype(f32)
    c_re, c_im = c_re.astype(f32), c_im.astype(f32)
    u = (h @ w_in).astype(f32).reshape(bsz, seq, S5_GROUPS, S5_GROUP)
    step = jnp.exp(log_step.astype(f32))[:, None]
    mag = jnp.exp(lam_re * step)
    lb_re = mag * jnp.cos(lam_im * step)
    lb_im = mag * jnp.sin(lam_im * step)
    den = lam_re * lam_re + lam_im * lam_im
    coef_re = ((lb_re - 1.0) * lam_re + lb_im * lam_im) / den
    coef_im = (lb_im * lam_re - (lb_re - 1.0) * lam_im) / den
    bb_re = coef_re[..., None] * b_re - coef_im[..., None] * b_im
    bb_im = coef_re[..., None] * b_im + coef_im[..., None] * b_re
    bu_re = jnp.einsum("blgh,gph->blgp", u, bb_re)
    bu_im = jnp.einsum("blgh,gph->blgp", u, bb_im)
    a_re = jnp.broadcast_to(lb_re, (1, seq) + lb_re.shape)
    a_im = jnp.broadcast_to(lb_im, (1, seq) + lb_im.shape)
    _, _, s_re, s_im = lax.associative_scan(
        _complex_linear_combine, (a_re, a_im, bu_re, bu_im), axis=1)
    y = (jnp.einsum("blgp,ghp->blgh", s_re, c_re)
         - jnp.einsum("blgp,ghp->blgh", s_im, c_im)
         + d_skip.astype(f32) * u)
    y = jax.nn.gelu(y.reshape(bsz, seq, S5_WIDTH)).astype(h.dtype)
    val, gate = jnp.split(y @ w_out, 2, axis=-1)
    return val * jax.nn.sigmoid(gate)

def stick_breaking_attention(h, w_qkv, w_out):
    bsz, seq, _ = h.shape
    qkv = (h @ w_qkv).reshape(bsz, seq, 3, SB_HEADS, SB_HEAD_DIM)
    q = jnp.transpose(qkv[:, :, 0], (0, 2, 1, 3))
    k = jnp.transpose(qkv[:, :, 1], (0, 2, 1, 3))
    v = jnp.transpose(qkv[:, :, 2], (0, 2, 1, 3))
    scale = 1.0 / math.sqrt(SB_HEAD_DIM)
    out_blocks = []
    for blk in range(seq // Q_BLOCK):
        t0 = blk * Q_BLOCK
        n_keys = t0 + Q_BLOCK
        z = jnp.einsum("bhqd,bhkd->bhqk", q[:, :, t0:n_keys],
                       k[:, :, :n_keys]).astype(jnp.float32) * scale
        t_pos = t0 + jnp.arange(Q_BLOCK)[:, None]
        s_pos = jnp.arange(n_keys)[None, :]
        strict = s_pos < t_pos
        log_keep = jnp.where(strict, jax.nn.log_sigmoid(-z), 0.0)
        log_keep_after = lax.cumsum(log_keep, axis=3, reverse=True) - log_keep
        weight = jnp.where(strict, jnp.exp(jax.nn.log_sigmoid(z) + log_keep_after), 0.0)
        out_blocks.append(jnp.einsum("bhqk,bhkd->bhqd", weight.astype(v.dtype),
                                     v[:, :, :n_keys]))
    o = jnp.concatenate(out_blocks, axis=2)
    o = jnp.transpose(o, (0, 2, 1, 3)).reshape(bsz, seq, D_MODEL)
    return o @ w_out

def moe_swiglu(h, w_router, b_router, w_gate_up, w_down):
    bsz, seq, d = h.shape
    tok = h.reshape(bsz * seq, d)
    logits = (tok @ w_router).astype(jnp.float32) + b_router.astype(jnp.float32)
    probs = jax.nn.softmax(logits, axis=-1)
    top_p, top_i = lax.top_k(probs, TOP_K)
    top_p = top_p / jnp.sum(top_p, axis=-1, keepdims=True)
    gates = jnp.sum(jax.nn.one_hot(top_i, N_EXPERTS, dtype=jnp.float32)
                    * top_p[..., None], axis=1)
    out = jnp.zeros_like(tok)
    for e in range(N_EXPERTS):
        out = out + gates[:, e:e + 1].astype(tok.dtype) * swiglu(tok, w_gate_up[e], w_down[e])
    return out.reshape(bsz, seq, d)

def setup_inputs(seed: int = 0) -> dict:
    key = jax.random.key(seed)
    ks = jax.random.split(key, 24)
    f32 = jnp.float32

    def nrm(k, shape, std):
        return std * jax.random.normal(k, shape, f32)

    d, w, g, p, hh = D_MODEL, S5_WIDTH, S5_GROUPS, S5_STATE, S5_GROUP
    return {
        "x": nrm(ks[0], (BATCH, SEQ, d), 1.0),
        "c": nrm(ks[1], (BATCH, d), 1.0),
        "ada_w": nrm(ks[2], (DEPTH, d, 6 * d), d ** -0.5),
        "ada_b": nrm(ks[3], (DEPTH, 6 * d), 0.02),
        "norm_g": 1.0 + nrm(ks[4], (DEPTH, 4, d), 0.02),
        "s5_w_in": nrm(ks[5], (N_A_LAYERS, d, w), d ** -0.5),
        "s5_lambda_re": -0.5 + nrm(ks[6], (N_A_LAYERS, g, p), 0.01),
        "s5_lambda_im": math.pi * jnp.arange(p, dtype=f32) + nrm(ks[7], (N_A_LAYERS, g, p), 0.01),
        "s5_b_re": nrm(ks[8], (N_A_LAYERS, g, p, hh), (2.0 * hh) ** -0.5),
        "s5_b_im": nrm(ks[9], (N_A_LAYERS, g, p, hh), (2.0 * hh) ** -0.5),
        "s5_c_re": nrm(ks[10], (N_A_LAYERS, g, hh, p), 0.5 ** 0.5),
        "s5_c_im": nrm(ks[11], (N_A_LAYERS, g, hh, p), 0.5 ** 0.5),
        "s5_d": nrm(ks[12], (N_A_LAYERS, g, hh), 1.0),
        "s5_log_step": jax.random.uniform(ks[13], (N_A_LAYERS, g), f32,
                                          math.log(DT_MIN), math.log(DT_MAX)),
        "s5_w_out": nrm(ks[14], (N_A_LAYERS, w, 2 * d), w ** -0.5),
        "sb_w_qkv": nrm(ks[15], (N_B_LAYERS, d, 3 * d), d ** -0.5),
        "sb_w_out": nrm(ks[16], (N_B_LAYERS, d, d), d ** -0.5),
        "ffn_w_gate_up": nrm(ks[17], (N_A_LAYERS, d, 2 * D_FF), d ** -0.5),
        "ffn_w_down": nrm(ks[18], (N_A_LAYERS, D_FF, d), D_FF ** -0.5),
        "moe_w_router": nrm(ks[19], (N_B_LAYERS, d, N_EXPERTS), d ** -0.5),
        "moe_b_router": nrm(ks[20], (N_B_LAYERS, N_EXPERTS), 0.01),
        "moe_w_gate_up": nrm(ks[21], (N_B_LAYERS, N_EXPERTS, d, 2 * D_FF), d ** -0.5),
        "moe_w_down": nrm(ks[22], (N_B_LAYERS, N_EXPERTS, D_FF, d), D_FF ** -0.5),
    }

def reference(x, c, ada_w, ada_b, norm_g, s5_w_in, s5_lambda_re, s5_lambda_im,
              s5_b_re, s5_b_im, s5_c_re, s5_c_im, s5_d, s5_log_step, s5_w_out,
              sb_w_qkv, sb_w_out, ffn_w_gate_up, ffn_w_down,
              moe_w_router, moe_b_router, moe_w_gate_up, moe_w_down):
    c_act = jax.nn.silu(c)
    for i in range(DEPTH):
        j = i // N_MIXERS
        mod = (c_act @ ada_w[i] + ada_b[i])[:, None, :]
        shift_m, scale_m, gate_m, shift_f, scale_f, gate_f = jnp.split(mod, 6, axis=-1)
        h = rmsnorm(x, norm_g[i, 0]) * (1.0 + scale_m) + shift_m
        if i % N_MIXERS == 0:
            y = s5_mixer(h, s5_w_in[j], s5_lambda_re[j], s5_lambda_im[j], s5_b_re[j],
                         s5_b_im[j], s5_c_re[j], s5_c_im[j], s5_d[j], s5_log_step[j],
                         s5_w_out[j])
        else:
            y = stick_breaking_attention(h, sb_w_qkv[j], sb_w_out[j])
        x = x + gate_m * rmsnorm(y, norm_g[i, 1])
        h = rmsnorm(x, norm_g[i, 2]) * (1.0 + scale_f) + shift_f
        if i % 2 == 0:
            y = swiglu(h, ffn_w_gate_up[j], ffn_w_down[j])
        else:
            y = moe_swiglu(h, moe_w_router[j], moe_b_router[j], moe_w_gate_up[j], moe_w_down[j])
        x = x + gate_f * rmsnorm(y, norm_g[i, 3])
    return x


_drawn_inputs = setup_inputs


def setup_inputs(seed=0):
    import zlib

    import numpy as np

    out = dict(_drawn_inputs(seed))
    spreads = {}
    factors = {}
    for name, (base, spread) in spreads.items():
        noise = np.random.default_rng([zlib.crc32(name.encode()), seed]).standard_normal(out[name].shape)
        drawn = base * np.exp(spread * noise) if base else spread * noise
        out[name] = __import__('jax').numpy.asarray(drawn.astype(out[name].dtype))
    for name, factor in factors.items():
        out[name] = (out[name] * factor).astype(out[name].dtype)
    return out
```

```python
import math
from contextlib import ExitStack

import concourse.bass as bass
from concourse import mybir

F32 = mybir.dt.float32
I32 = mybir.dt.int32
U32 = mybir.dt.uint32
ALU = mybir.AluOpType
ACT = mybir.ActivationFunctionType
AX = mybir.AxisListType

P = 128
D = 1024
KD = D // P
SEQ = 256
TT = SEQ // P
W5 = D // 2
NBLK = W5 // P
HG = 16
NS = 64
TPB = 4
NT = NBLK * TPB
HEADS = 16
DH = 64
FF = 7 * D // 2
FB = FF // 512
NE = 8
EPS = 1e-6
ROOT_D = 32.0
assert ROOT_D ** 2 == D
MODS = 12
RING = 7
GRAN = 4096
ARENA = 13568
MAGIC = 12582912.0
TWO_PI = 2 * math.pi
SIN_SCALE = TWO_PI * (1 - 2e-7)

G_BANK, U_BANK, T_BANK, S_BANK, Y_BANK = 0, 1, 2, 3, 4

PER_EXPERT = 3 * FB


def gate_at(f):
    return 0 if f == 0 else 3 * f - 1


def up_at(f):
    return gate_at(f) + 1


def down_at(f):
    return 3 * f + 4 if f < FB - 1 else PER_EXPERT - 1


N_ADA0A = 0
N_WIN = 4
N_ADA0B = 5
N_ADA1 = 13
N_WOUT = 25
N_FFN = 27
N_QKV = 48
N_SBOUT = 54
N_MOE = 56
assert N_MOE % RING == 0 and PER_EXPERT % RING == 0


def ada_place(layer, r):
    if layer:
        return N_ADA1 + r
    return N_ADA0A + r if r < 4 else N_ADA0B + r - 4


def program(nc, x, c, ada_w, ada_b, norm_g, s5_w_in, s5_lambda_re, s5_lambda_im, s5_b_re, s5_b_im,
            s5_c_re, s5_c_im, s5_d, s5_log_step, s5_w_out, sb_w_qkv, sb_w_out, ffn_w_gate_up,
            ffn_w_down, moe_w_router, moe_b_router, moe_w_gate_up, moe_w_down, out):
    ctx = ExitStack()
    with ctx:
        def sb(name, shape, dt=F32):
            return ctx.enter_context(nc.sbuf_tensor(name, shape, dt))

        def sem(name):
            return ctx.enter_context(nc.semaphore(name))

        ps = ctx.enter_context(nc.psum_tensor("ps", [P, 8, 512], F32))

        x_sb = sb("x_sb", [P, TT, D])
        hT = sb("hT", [P, KD, SEQ])
        hn = sb("hn", [P, TT, D])
        ring = sb("ring", [P, RING, GRAN])
        gg = sb("gg", [P, D])
        junk = sb("junk", [P, D])
        tbuf = sb("tbuf", [P, D])
        ident = sb("ident", [P, P])
        ones = sb("ones", [P, P])
        incl = sb("incl", [P, P])
        strict = sb("strict", [P, P])
        chmask = sb("chmask", [P, 8])
        steps = sb("steps", [P, SEQ])
        inv32 = sb("inv32", [P, 1])
        half = sb("half", [P, 1])
        cols = sb("cols", [P, 128])
        c32 = sb("c32", [P, KD, 32])
        adab = sb("adab", [P, 4, 24])
        modc = sb("modc", [P, 2, MODS, 4])
        scale_c = sb("scale_c", [P, 4, KD])
        gate_c = sb("gate_c", [P, 4, KD])
        stat = sb("stat", [P, 16])
        wr_sb = sb("wr_sb", [P, KD, NE])
        br_sb = sb("br_sb", [1, NE])

        arena = sb("arena", [P, ARENA])

        def view(at, shape):
            n = math.prod(shape)
            names = [f"d{i}" for i in range(len(shape))]
            ap = arena[:, at:at + n]
            if len(shape) == 1:
                return ap
            return ap.rearrange(f"p ({' '.join(names)}) -> p {' '.join(names)}",
                                **{k: v for k, v in zip(names, shape)})

        class Place:
            def __init__(self):
                self.at = 0

            def __call__(self, *shape):
                v = view(self.at, shape)
                self.at += math.prod(shape)
                assert self.at <= ARENA
                return v

        pl = Place()
        cosT, sinT = pl(2, TPB, SEQ), pl(2, TPB, SEQ)
        bT = pl(2, TPB, P)
        cT = pl(3, TPB, P)
        zst_b = pl(640)
        zst_c = pl(512)
        prod = pl(2, TPB, SEQ)
        uT = pl(NBLK, SEQ)
        b_raw = pl(2, NT, HG)
        bb = pl(2, NT, HG)
        c_raw = pl(2, NBLK, NS)
        par = pl(32, NT)
        rows = pl(640)
        v_re = hn[:, 0, :].rearrange("p (t s) -> p t s", t=TPB)
        v_im = hn[:, 1, :].rearrange("p (t s) -> p t s", t=TPB)
        prod2 = hT[:, :, :].rearrange("p (a t) s -> p a t s", a=2)

        pl = Place()
        qT, kT, oT = pl(KD, SEQ), pl(KD, SEQ), pl(KD, SEQ)
        v_sb = pl(TT, D)
        z_e = pl(2, 2, 384)
        z_p = pl(2, 2, 384)
        z_w = pl(2, 2, 384)

        pl = Place()
        a_sb = pl(2, 512)
        aT = pl(2, 4, P)
        sg = pl(512)
        xe = pl(KD, 2, P)
        ysb = pl(2, D)
        scT = pl(2, SEQ)
        g1 = pl(TT, SEQ)
        gw = pl(TT, SEQ)
        macc = pl(TT, D)
        rt = pl(TT, 96)
        rcol = pl(NE, 4)
        pick = pl(1, 4)
        cnt = pl(4, NE)
        cnt_i = sb("cnt_i", [1, 4, NE], I32)

        landed = [sem(f"landed{i}") for i in range(RING)]
        used = [sem(f"used{i}") for i in range(RING)]
        params_in, x_in, router_in = sem("params_in"), sem("x_in"), sem("router_in")
        out_written, consts_done = sem("out_written"), sem("consts_done")
        cols_ready, cols_ps, cols_done, silu_c_done, c32_done, gg_done = (
            sem("cols_ready"), sem("cols_ps"), sem("cols_done"), sem("silu_c_done"), sem("c32_done"), sem("gg_done"))
        dve_step = sem("dve_step")
        pool_step = sem("pool_step")
        part_out, mod_ps, mod_out, mod_done = sem("part_out"), sem("mod_ps"), sem("mod_out"), sem("mod_done")
        ss_done, rs_done, ry_done, xn_done, hT_ps, hT_act, hT_dve = (
            sem("ss_done"), sem("rs_done"), sem("ry_done"), sem("xn_done"), sem("hT_ps"), sem("hT_act"), sem("hT_dve"))
        x_new, ys_done, diag_done, gg_ps = sem("x_new"), sem("ys_done"), sem("diag_done"), sem("gg_ps")
        u_ps, u_done = sem("u_ps"), sem("u_done")
        turn_ready, trig1_done, frac_done = sem("turn_ready"), sem("trig1_done"), sem("frac_done")
        angle_done, table_done = sem("angle_done"), sem("table_done")
        zst_done, zt_ps, zt_done = sem("zst_done"), sem("zt_ps"), sem("zt_done")
        bu_ps, rot_done, v_done, scan_done, post_d, post_p, y5_ps, y5_done = (
            sem("bu_ps"), sem("rot_done"), sem("v_done"), sem("scan_done"), sem("post_d"), sem("post_p"),
            sem("y5_ps"), sem("y5_done"))
        gelu_done, wo_ps, sig_done, glu_done = sem("gelu_done"), sem("wo_ps"), sem("sig_done"), sem("glu_done")
        gate1_done, up1_done = sem("gate1_done"), sem("up1_done")
        silu_done, act_done, tr_done, aT_done = sem("silu_done"), sem("act_done"), sem("tr_done"), sem("aT_done")
        qk_done, v_out = sem("qk_done"), sem("v_out")
        z_ps, zabs_done, zcopy_done, exp_done, ln_done, sp_done, spm_done = (
            sem("z_ps"), sem("zabs_done"), sem("zcopy_done"), sem("exp_done"), sem("ln_done"), sem("sp_done"),
            sem("spm_done"))
        sfx_ps, arg_done, wexp_done, w_done, o_ps, o_done = (
            sem("sfx_ps"), sem("arg_done"), sem("wexp_done"), sem("w_done"), sem("o_ps"), sem("o_done"))
        lg_ps, lmax_done, pexp_done, sel_done, rank_ps, route_done = (
            sem("lg_ps"), sem("lmax_done"), sem("pexp_done"), sem("sel_done"), sem("rank_ps"), sem("route_done"))
        pick_done, onehot_done, xe_ps, xe_done, st_ps, st_done = (
            sem("pick_done"), sem("onehot_done"), sem("xe_ps"), sem("xe_done"), sem("st_ps"), sem("st_done"))
        ysb_act, ysb_dve, sc_ps, sc_done = sem("ysb_act"), sem("ysb_dve"), sem("sc_ps"), sem("sc_done")

        r_c = rows[0:KD, 0:P]
        r_lam = rows[0:NT, 128:384].rearrange("p (a n) -> p a n", a=2)
        r_ls = rows[0:NT, 384:386]
        r_lsb = rows[0:NT, 512:640].rearrange("p (a n) -> p a n", a=2)
        r_d = junk[0:NBLK, 512:640]
        r_g = tbuf[0:8, :]
        r_b = junk[0:24, 0:512]
        part = rows[:, 0:512]
        C_C, C_LRE, C_LIM, C_LS, C_D, C_G = 0, 8, 24, 40, 56, 60
        (STEP, XM, THETA, KTURN, TURN, COST, SIN1, COS1, MAG, LBR, LBI, CRE, CIM, DEN, FHI, FLO,
         T0, T1, T2, T3, T4) = range(21)
        MODS_OF = ((0, 0), (0, 6), (1, 0), (1, 6))

        def pcol(i):
            return par[:, i, :]

        def shift_col(s, k):
            layer, r = MODS_OF[s]
            return modc[:, layer, r + k // 4, k % 4:k % 4 + 1]

        def mods(s, which):
            layer, r = MODS_OF[s]
            return modc[:, layer, r + 2 * which:r + 2 * which + 2, :].rearrange("p a b -> p (a b)")

        def g_cols(s, post):
            return cols[:, C_G:C_G + 64].rearrange("p (k r) -> p k r", r=8)[:, :, 2 * s + post]

        def gran(n):
            return ring[:, n % RING, :]

        def gran8(n):
            return gran(n).rearrange("p (k n) -> p k n", k=KD)

        def gran4(n):
            return gran(n).rearrange("p (k n) -> p k n", k=4)

        def wait_landed(eng, n, turn=None):
            eng.wait_ge(landed[n % RING], 16 * (n // RING if turn is None else turn) + 16)

        def wait_used(eng, n, turn=None):
            eng.wait_ge(used[n % RING], (n // RING if turn is None else turn) + 1)

        def above(eng, s, value):
            if not isinstance(value, int) or value > 0:
                eng.wait_ge(s, value)

        def expert_counts(eng, e):
            nch = eng.value_load(cnt_i[0:1, 0, bass.ds(e, 1)], min_val=1, max_val=2)
            more = eng.value_load(cnt_i[0:1, 3, bass.ds(e, 1)], min_val=0, max_val=1)
            items2 = eng.value_load(cnt_i[0:1, 1, bass.ds(e, 1)], min_val=2 * FB - 2, max_val=2 * FB * (NE + 1))
            before1 = eng.value_load(cnt_i[0:1, 2, bass.ds(e, 1)], min_val=FB, max_val=FB * (NE + 1))
            return nch, more, items2, before1

        block = ctx.enter_context(nc.Block())

        @block.sync
        def _(sp):
            def load(n, dst, src, turn=None):
                turn = n // RING if turn is None else turn
                above(sp, used[n % RING], turn)
                sp.dma_start(dst, src).then_inc(landed[n % RING], 16)

            def cols512(w, at):
                return w[:, at:at + 512].rearrange("(k p) n -> p k n", p=P)

            def load_ada(layer, r):
                n = ada_place(layer, r)
                load(n, gran8(n), cols512(ada_w[layer], 512 * r))

            for r in range(4):
                load_ada(0, r)
            load(N_WIN, gran8(N_WIN), cols512(s5_w_in[0], 0))
            for r in range(4, MODS):
                load_ada(0, r)
            for r in range(MODS):
                load_ada(1, r)
            for h in range(2):
                load(N_WOUT + h, gran4(N_WOUT + h),
                     s5_w_out[0][:, D * h:D * h + D].rearrange("(k p) n -> p k n", p=P))

            def swiglu_weights(w_gu, w_dn, base, turn):
                def down(f):
                    g = down_at(f)
                    load(base + g, gran4(base + g),
                         w_dn[512 * f:512 * f + 512, :].rearrange("(k p) n -> p k n", p=P), turn(g))
                for f in range(FB):
                    for g, at in ((gate_at(f), 512 * f), (up_at(f), FF + 512 * f)):
                        load(base + g, gran8(base + g), cols512(w_gu, at), turn(g))
                    if f:
                        down(f - 1)
                down(FB - 1)

            swiglu_weights(ffn_w_gate_up[0], ffn_w_down[0], N_FFN, lambda g: (N_FFN + g) // RING)
            for r in range(6):
                load(N_QKV + r, gran8(N_QKV + r), cols512(sb_w_qkv[0], 512 * r))
            for r in range(2):
                load(N_SBOUT + r, gran8(N_SBOUT + r), cols512(sb_w_out[0], 512 * r))
            with sp.Fori(0, NE) as e:
                gu = moe_w_gate_up[0].rearrange("e a b -> (e a) b")[bass.ds(e * D, D), :]
                dn = moe_w_down[0].rearrange("e a b -> (e a) b")[bass.ds(e * FF, FF), :]
                swiglu_weights(gu, dn, N_MOE, lambda g: e * (PER_EXPERT // RING) + (N_MOE + g) // RING)
            sp.wait_ge(x_new, 8)
            sp.dma_start(out[0].rearrange("(t p) d -> p t d", p=P), x_sb[:, :, :]).then_inc(out_written, 16)
            sp.wait_ge(out_written, 16)

        @block.gpsimd
        def _(pool):
            count = [0]

            def link(ins):
                count[0] += 1
                ins.then_inc(pool_step, 1)
                pool.wait_ge(pool_step, count[0])

            link(pool.memset(ones[:, :], 1.0))
            pool.affine_select(out=ident[:, :], in_=ones[:, :], compare_op=ALU.is_equal, fill=0.0, base=0,
                               pattern=[[-1, P]], channel_multiplier=1).then_inc(consts_done, 1)
            pool.affine_select(out=incl[:, :], in_=ones[:, :], compare_op=ALU.is_ge, fill=0.0, base=0,
                               pattern=[[-1, P]], channel_multiplier=1).then_inc(consts_done, 1)
            pool.affine_select(out=strict[:, :], in_=ones[:, :], compare_op=ALU.is_gt, fill=0.0, base=0,
                               pattern=[[1, P]], channel_multiplier=-1).then_inc(consts_done, 1)
            link(pool.affine_select(out=chmask[:, :], in_=ones[:, 0:8], compare_op=ALU.is_ge, fill=0.0, base=0,
                                    pattern=[[-HG, 8]], channel_multiplier=1))
            pool.affine_select(out=chmask[:, :], in_=chmask[:, :], compare_op=ALU.is_ge, fill=0.0, base=HG - 1,
                               pattern=[[HG, 8]], channel_multiplier=-1).then_inc(consts_done, 1)
            pool.iota(steps[:, :], [[1, SEQ]], base=0, channel_multiplier=0,
                      allow_small_or_imprecise_dtypes=True).then_inc(consts_done, 1)
            pool.memset(inv32[:, :], 1.0 / 32).then_inc(consts_done, 1)
            link(pool.memset(half[:, :], -0.5))
            pool.wait_ge(consts_done, 6)

            scratch = junk[:, :].rearrange("p (t s) -> p t s", t=TPB)

            def angles(b):
                q = b % 2
                if b == 0:
                    pool.wait_ge(frac_done, 1)
                if b >= 2:
                    pool.wait_ge(post_d, b - 1)
                fh = par[:, FHI, TPB * b:TPB * b + TPB].unsqueeze(2).to_broadcast([P, TPB, SEQ])
                fl = par[:, FLO, TPB * b:TPB * b + TPB].unsqueeze(2).to_broadcast([P, TPB, SEQ])
                t = steps[:, :].unsqueeze(1).to_broadcast([P, TPB, SEQ])
                s, co = sinT[:, q], cosT[:, q]
                link(pool.tensor_tensor(s, t, fh, ALU.mult))
                link(pool.tensor_scalar(scratch, s, MAGIC, MAGIC, ALU.add, ALU.subtract))
                link(pool.tensor_tensor(s, s, scratch, ALU.subtract))
                link(pool.tensor_tensor(co, t, fl, ALU.mult))
                link(pool.tensor_tensor(s, s, co, ALU.add))
                link(pool.tensor_scalar(co, s, 0.25, None, ALU.add))
                for v in (s, co):
                    link(pool.tensor_scalar(scratch, v, MAGIC, MAGIC, ALU.add, ALU.subtract))
                    pool.tensor_tensor(v, v, scratch, ALU.subtract).then_inc(angle_done, 1)
                    pool.wait_ge(angle_done, 2 * b + (1 if v is s else 2))

            def add_rotated(b):
                pool.wait_ge(rot_done, 4 * b + 2)
                pool.tensor_tensor(v_re, prod[:, 0], prod[:, 1], ALU.add).then_inc(v_done, 1)
                pool.wait_ge(rot_done, 4 * b + 4)
                pool.tensor_tensor(v_im, prod2[:, 0], prod2[:, 1], ALU.subtract).then_inc(v_done, 1)

            def unrotate(b):
                q = b % 2
                pool.wait_ge(v_done, 2 * b + 2)
                pool.wait_ge(scan_done, 2 * TPB * (b + 1))
                pool.tensor_tensor(prod2[:, 0], v_re, sinT[:, q], ALU.mult).then_inc(post_p, 1)
                pool.tensor_tensor(prod2[:, 1], v_im, cosT[:, q], ALU.mult).then_inc(post_p, 1)
                pool.wait_ge(post_p, 2 * b + 2)

            def inverse_norm(s, ready, done, src, dst):
                for tt in range(TT):
                    pool.wait_ge(ready, 2 * s + tt + 1)
                    a, b = stat[:, src + tt:src + tt + 1], stat[:, dst + tt:dst + tt + 1]
                    link(pool.tensor_scalar(b, a, D * EPS, None, ALU.add))
                    pool.tensor_tensor(b, b, half[:, :], ALU.pow).then_inc(done, 1)

            inverse_norm(0, ss_done, rs_done, 0, 8)
            angles(0)
            angles(1)
            for b in range(NBLK):
                add_rotated(b)
                unrotate(b)
                if b + 2 < NBLK:
                    angles(b + 2)
            for s in range(4):
                if s:
                    inverse_norm(s, ss_done, rs_done, 0, 8)
                inverse_norm(s, ys_done, ry_done, 4, 12)

        @block.scalar
        def _(act):
            act.dma_start(r_c, c.rearrange("a (k n) -> (a k) n", n=P)).then_inc(params_in, 16)
            act.dma_start(r_lam[:, 0, :], s5_lambda_re[0].rearrange("(t g) n -> t (g n)", g=2)).then_inc(params_in, 16)
            act.dma_start(r_lam[:, 1, :], s5_lambda_im[0].rearrange("(t g) n -> t (g n)", g=2)).then_inc(params_in, 16)
            act.dma_start(r_ls, s5_log_step[0].rearrange("(t g) -> t g", g=2)).then_inc(params_in, 16)
            act.dma_start(r_d, s5_d[0].rearrange("(b g) h -> b (g h)", b=NBLK)).then_inc(params_in, 16)
            act.dma_start(r_g, norm_g.rearrange("a b n -> (a b) n")).then_inc(params_in, 16)
            act.dma_start(r_b, ada_b.rearrange("l (r n) -> (l r) n", n=512)).then_inc(params_in, 16)
            act.dma_start(x_sb[:, :, :], x[0].rearrange("(t p) d -> p t d", p=P)).then_inc(x_in, 16)
            for i, w in enumerate((s5_b_re, s5_b_im)):
                for g in range(2):
                    act.dma_start(b_raw[NS * g:NS * g + NS, i], w[0].rearrange("(t g) n h -> g n t h", g=2)[g]
                                  ).then_inc(params_in, 16)
            for i, w in enumerate((s5_c_re, s5_c_im)):
                act.dma_start(c_raw[:, i], w[0].rearrange("(b g) h n -> (g h) b n", b=NBLK)).then_inc(params_in, 16)
            act.dma_start(wr_sb[:, :, :], moe_w_router[0].rearrange("(k p) n -> p k n", p=P)).then_inc(router_in, 16)
            act.dma_start(br_sb[:, :], moe_b_router).then_inc(router_in, 16)

            def pre_stats(s):
                for tt in range(TT):
                    if s == 0:
                        act.wait_ge(x_in, 16)
                    else:
                        act.wait_ge(x_new, 2 * (s - 1) + tt + 1)
                    act.activation(hn[:, tt, :], x_sb[:, tt, :], ACT.Square,
                                   accum_out=stat[:, tt:tt + 1]).then_inc(ss_done, 1)

            def hT_evict(s):
                act.wait_ge(mod_done, s + 1)
                for k in (0, 1, 4, 5):
                    act.wait_ge(hT_ps, 4 * s + k // 2 + 1)
                    act.activation(hT[:, k, :], ps[:, Y_BANK + k // 2, 256 * (k % 2):256 * (k % 2) + 256],
                                   ACT.Identity, bias=shift_col(s, k), scale=scale_c[:, s, k:k + 1]
                                   ).then_inc(hT_act, 1)

            def y_stats(s, source):
                for tt in range(TT):
                    if s or tt:
                        act.wait_ge(ys_done, 2 * s + tt)
                    act.activation(junk[:, :], source(tt), ACT.Square,
                                   accum_out=stat[:, 4 + tt:5 + tt]).then_inc(ys_done, 1)

            def y_banks(tt):
                return ps[:, Y_BANK + 2 * tt:Y_BANK + 2 * tt + 2, :].rearrange("p a b -> p (a b)")

            def ada_parts(lo, hi):
                for i in range(lo, hi):
                    wait_used(act, ada_place(*divmod(i, MODS)))
                    above(act, mod_ps, i)
                    act.activation(part, ps[:, 0, :], ACT.Copy).then_inc(part_out, 1)

            def trig(b):
                q = b % 2
                act.wait_ge(angle_done, 2 * b + 2)
                act.activation(sinT[:, q], sinT[:, q], ACT.Sin, scale=SIN_SCALE).then_inc(table_done, 1)
                act.activation(cosT[:, q], cosT[:, q], ACT.Sin, scale=SIN_SCALE).then_inc(table_done, 1)

            def gate_out(f, q, ch, base, turn, c1):
                n = base + gate_at(f)
                if ch:
                    act.wait_ge(gate1_done, c1 + f + 1)
                else:
                    wait_used(act, n, turn(gate_at(f)))
                above(act, act_done, q)
                act.activation(sg, ps[:, G_BANK, :], ACT.Silu).then_inc(silu_done, 1)

            def aT_out(q, ch):
                act.wait_ge(tr_done, q + 1)
                act.activation(aT[:, ch].rearrange("p k n -> p (k n)"), ps[:, T_BANK, :], ACT.Copy
                               ).then_inc(aT_done, 1)

            pre_stats(0)
            act.wait_ge(cols_done, 1)
            act.activation(cols[:, 0:KD], cols[:, 0:KD], ACT.Silu).then_inc(silu_c_done, 1)
            act.wait_ge(turn_ready, 1)
            act.activation(pcol(SIN1), pcol(TURN), ACT.Sin, scale=SIN_SCALE).then_inc(trig1_done, 1)
            act.activation(pcol(COS1), pcol(COST), ACT.Sin, scale=SIN_SCALE).then_inc(trig1_done, 1)
            ada_parts(0, 4)
            hT_evict(0)
            for i in range(2):
                if i:
                    wait_used(act, N_WIN)
                else:
                    act.wait_ge(u_ps, 1)
                act.activation(uT[:, 2 * i:2 * i + 2, :].rearrange("p a b -> p (a b)"), ps[:, i, :], ACT.Copy
                               ).then_inc(u_done, 1)
            trig(0)
            trig(1)
            for b in range(NBLK):
                zt = ps[:, T_BANK, :].rearrange("p (t n) -> p t n", t=TPB)
                for i, dst, sign in ((0, bT[:, 0], 1.0), (1, bT[:, 1], 1.0), (2, cT[:, 0], 1.0), (3, cT[:, 2], -1.0)):
                    act.wait_ge(zt_ps, 4 * b + i + 1)
                    if b:
                        act.wait_ge(y5_ps, b)
                    act.activation(dst, zt, ACT.Copy, scale=sign).then_inc(zt_done, 1)
                    if i == 2:
                        act.activation(cT[:, 1], zt, ACT.Copy, scale=-1.0).then_inc(zt_done, 1)
                ada_parts(4 + 5 * b, 9 + 5 * b)
                if b + 2 < NBLK:
                    trig(b + 2)
            for b in range(NBLK):
                act.wait_ge(y5_done, b + 1)
                act.activation(uT[:, b, :], uT[:, b, :], ACT.Gelu_apprx_tanh).then_inc(gelu_done, 1)
            for i in range(4):
                if i < 3:
                    act.wait_ge(wo_ps, i + 1)
                else:
                    wait_used(act, N_WOUT + 1)
                if i >= 2:
                    act.wait_ge(glu_done, i - 1)
                act.activation(junk[:, 512 * (i % 2):512 * (i % 2) + 512], ps[:, 2 * i + 1, :],
                               ACT.Sigmoid).then_inc(sig_done, 1)
            act.wait_ge(glu_done, 4)
            y_stats(0, lambda tt: hn[:, tt, :])
            pre_stats(1)
            hT_evict(1)
            ffn_turn = lambda g: (N_FFN + g) // RING
            for f in range(FB):
                for ch, q in ((1, 2 * f), (0, 2 * f + 1)):
                    gate_out(f, q, ch, N_FFN, ffn_turn, 0)
                    if f:
                        aT_out(q - 2, ch)
            aT_out(2 * FB - 2, 1)
            aT_out(2 * FB - 1, 0)
            wait_used(act, N_FFN + PER_EXPERT - 1)
            y_stats(1, y_banks)
            pre_stats(2)
            hT_evict(2)
            for r in range(4):
                wait_used(act, N_QKV + r)
                src = ps[:, 2 * (r % 2):2 * (r % 2) + 2, :].rearrange("p a (b n) -> p (a b) n", b=2)
                act.activation((qT if r < 2 else kT)[:, 4 * (r % 2):4 * (r % 2) + 4, :], src, ACT.Copy,
                               scale=DH ** -0.5 if r < 2 else 1.0).then_inc(qk_done, 1)
            def o_out(h):
                act.wait_ge(o_ps, h + 1)
                act.activation(oT[:, h, :], ps[:, 6 + h % 2, 0:256], ACT.Copy).then_inc(o_done, 1)

            for h in range(HEADS // 2):
                b = h % 2
                act.wait_ge(z_ps, h + 1)
                if h >= 2:
                    act.wait_ge(o_ps, h - 1)
                act.activation(z_w[:, b], ps[:, 2 * b:2 * b + 2, 0:384], ACT.Copy).then_inc(zcopy_done, 1)
                act.wait_ge(zabs_done, h + 1)
                act.activation(z_e[:, b], z_e[:, b], ACT.Exp).then_inc(exp_done, 1)
                act.wait_ge(exp_done, h + 1)
                act.activation(z_e[:, b], z_e[:, b], ACT.Ln, bias=1.0).then_inc(ln_done, 1)
                act.wait_ge(arg_done, h + 1)
                act.activation(z_w[:, b], z_w[:, b], ACT.Exp).then_inc(wexp_done, 1)
                if h:
                    o_out(h - 1)
            o_out(HEADS // 2 - 1)
            wait_used(act, N_SBOUT + 1)
            y_stats(2, y_banks)
            pre_stats(3)
            hT_evict(3)
            for tt in range(TT):
                act.wait_ge(lmax_done, tt + 1)
                act.activation(rt[:, tt, 8:16], rt[:, tt, 0:8], ACT.Exp, bias=rt[:, tt, 80:81],
                               accum_out=rt[:, tt, 81:82]).then_inc(pexp_done, 1)
            act.wait_ge(route_done, 1)
            with act.Fori(0, NE) as e:
                nch, more, items2, c1 = expert_counts(act, e)
                moe_turn = lambda g: e * (PER_EXPERT // RING) + (N_MOE + g) // RING

                def xe_out(ch):
                    for k in range(KD):
                        bank = (G_BANK, T_BANK)[ch] + k // 4
                        ins = act.activation(xe[:, k, ch, :], ps[:, bank, P * (k % 4):P * (k % 4) + P],
                                             ACT.Identity, bias=shift_col(3, k), scale=scale_c[:, 3, k:k + 1])
                    return ins

                with act.If(nch > 1):
                    act.wait_ge(xe_ps, e + 1)
                    xe_out(1)
                act.wait_ge(xe_ps, e + 1)
                xe_out(0).then_inc(xe_done, 1)
                for f in range(FB):
                    q2 = items2 + f * nch
                    with act.If(nch > 1):
                        gate_out(f, q2 + 2, 1, N_MOE, moe_turn, c1)
                        if f:
                            aT_out(q2, 1)
                    gate_out(f, q2 + more + 2, 0, N_MOE, moe_turn, c1)
                    if f:
                        aT_out(q2 + 1, 0)
                q2 = items2 + FB * nch
                with act.If(nch > 1):
                    aT_out(q2, 1)
                aT_out(q2 + 1, 0)
                with act.If(nch > 1):
                    wait_used(act, N_MOE + PER_EXPERT - 1, moe_turn(PER_EXPERT - 1))
                    act.activation(ysb[:, 1, 0:512], ps[:, Y_BANK + 2, :], ACT.Copy)
                wait_used(act, N_MOE + PER_EXPERT - 1, moe_turn(PER_EXPERT - 1))
                act.activation(ysb[:, 0, 0:512], ps[:, Y_BANK, :], ACT.Copy).then_inc(ysb_act, 1)
            act.wait_ge(sc_done, 4 * NE + 4)
            y_stats(3, lambda tt: macc[:, tt, :])

        @block.vector
        def _(dve):
            count = [0]

            def link(ins):
                count[0] += 1
                ins.then_inc(dve_step, 1)
                dve.wait_ge(dve_step, count[0])

            def stt(o, a, s, b, op0, op1):
                return dve.scalar_tensor_tensor(out=o, in0=a, scalar=s, in1=b, op0=op0, op1=op1)

            def exp_small(dst, src):
                n, r, p, bits = pcol(T0), pcol(T1), pcol(T2), pcol(T3)
                link(dve.tensor_scalar(n, src, 1.0 / math.log(2), MAGIC, ALU.mult, ALU.add))
                link(dve.tensor_scalar(n, n, MAGIC, None, ALU.subtract))
                link(dve.tensor_scalar(n, n, -126.0, None, ALU.max))
                hi = 0.693145751953125
                link(stt(r, n, -hi, src, ALU.mult, ALU.add))
                link(stt(r, n, -(math.log(2) - hi), r, ALU.mult, ALU.add))
                link(dve.tensor_scalar(p, r, 1.0 / math.factorial(7), None, ALU.mult))
                for k in range(6, 0, -1):
                    link(stt(p, p, 1.0 / math.factorial(k), r, ALU.add, ALU.mult))
                link(dve.tensor_scalar(n, n, 127.0, 8388608.0, ALU.add, ALU.mult))
                link(dve.tensor_copy(bits.bitcast(I32), n))
                link(stt(dst, p, 1.0, bits, ALU.add, ALU.mult))

            def to_hT(s):
                for tt in range(TT):
                    dve.wait_ge(rs_done, 2 * s + tt + 1)
                    dve.tensor_scalar(hn[:, tt, :], x_sb[:, tt, :], stat[:, 8 + tt:9 + tt], ROOT_D, ALU.mult, ALU.mult
                                      ).then_inc(xn_done, 1)

            def hT_evict(s):
                dve.wait_ge(mod_done, s + 1)
                for k in (2, 3, 6, 7):
                    dve.wait_ge(hT_ps, 4 * s + k // 2 + 1)
                    dve.tensor_scalar(hT[:, k, :], ps[:, Y_BANK + k // 2, 256 * (k % 2):256 * (k % 2) + 256],
                                      scale_c[:, s, k:k + 1], shift_col(s, k), ALU.mult, ALU.add
                                      ).then_inc(hT_dve, 1)

            def gate_row(s):
                if s:
                    dve.wait_ge(x_new, 2 * s)
                link(stt(gate_c[:, s, :], mods(s, 2), ROOT_D, g_cols(s, 1), ALU.mult, ALU.mult))
                dve.tensor_tensor(tbuf[:, :].rearrange("p (k n) -> p k n", k=KD),
                                  ident[:, :].unsqueeze(1).to_broadcast([P, KD, P]),
                                  gate_c[:, s, :].unsqueeze(2).to_broadcast([P, KD, P]), ALU.mult
                                  ).then_inc(diag_done, 1)
                dve.wait_ge(gg_ps, s + 1)
                dve.tensor_copy(gg[:, :], ps[:, 2:4, :].rearrange("p a b -> p (a b)")).then_inc(gg_done, 1)
                dve.wait_ge(gg_done, s + 1)

            def residual(s, source):
                for tt in range(TT):
                    dve.wait_ge(ry_done, 2 * s + tt + 1)
                    link(stt(tbuf[:, :], source(tt), stat[:, 12 + tt:13 + tt], gg[:, :], ALU.mult, ALU.mult))
                    dve.tensor_tensor(x_sb[:, tt, :], x_sb[:, tt, :], tbuf[:, :], ALU.add).then_inc(x_new, 1)
                    dve.wait_ge(x_new, 2 * s + tt + 1)

            def y_banks(tt):
                return ps[:, Y_BANK + 2 * tt:Y_BANK + 2 * tt + 2, :].rearrange("p a b -> p (a b)")

            def ada_cols(lo, hi):
                for i in range(lo, hi):
                    layer, r = divmod(i, MODS)
                    dve.wait_ge(mod_ps, i + 1)
                    dve.tensor_tensor(modc[:, layer, r, :], ps[:, 1, 0:4], adab[:, :, i], ALU.add).then_inc(mod_out, 1)
                    if r in (3, 9):
                        s = 2 * layer + (r == 9)
                        dve.wait_ge(mod_out, i + 1)
                        stt(scale_c[:, s, :], mods(s, 1), 1.0, g_cols(s, 0), ALU.add, ALU.mult).then_inc(mod_done, 1)

            def swiglu_out(f, q, ch, base, turn, c1, a_free):
                dve.wait_ge(silu_done, q + 1)
                if ch:
                    dve.wait_ge(up1_done, c1 + f + 1)
                else:
                    wait_used(dve, base + up_at(f), turn(up_at(f)))
                if a_free is not None:
                    dve.wait_ge(tr_done, a_free)
                dve.tensor_tensor(a_sb[:, ch, :], sg, ps[:, U_BANK, :], ALU.mult).then_inc(act_done, 1)

            dve.wait_ge(params_in, 16 * 13)
            link(dve.tensor_copy(r_lsb, r_ls.unsqueeze(2).to_broadcast([NT, 2, NS])))
            dve.memset(zst_b, 0.0).then_inc(cols_ready, 1)
            dve.wait_ge(cols_ps, 2)
            link(dve.tensor_copy(cols[:, 0:124], ps[:, 0, 0:124]))
            dve.tensor_copy(adab[:, :, :], ps[:, 1, 0:96].rearrange("p (a b) -> p a b", a=4)).then_inc(cols_done, 1)
            dve.wait_ge(cols_done, 1)
            lre, lim, ls = (cols[:, a:a + NT] for a in (C_LRE, C_LIM, C_LS))
            exp_small(pcol(STEP), ls)
            link(dve.tensor_tensor(pcol(THETA), lim, pcol(STEP), ALU.mult))
            link(dve.tensor_scalar(pcol(KTURN), pcol(THETA), 1 / TWO_PI, MAGIC, ALU.mult, ALU.add))
            link(dve.tensor_scalar(pcol(KTURN), pcol(KTURN), MAGIC, None, ALU.subtract))
            p1 = 6.28125
            p2 = 0.0019350051879882812
            p3 = TWO_PI - p1 - p2
            for p in (p1, p2, p3):
                link(stt(pcol(THETA), pcol(KTURN), -p, pcol(THETA), ALU.mult, ALU.add))
            link(dve.tensor_scalar(pcol(TURN), pcol(THETA), 1 / TWO_PI, None, ALU.mult))
            link(dve.tensor_scalar(pcol(COST), pcol(TURN), 0.25, None, ALU.add))
            link(dve.tensor_scalar(pcol(T0), pcol(COST), MAGIC, MAGIC, ALU.add, ALU.subtract))
            dve.tensor_tensor(pcol(COST), pcol(COST), pcol(T0), ALU.subtract).then_inc(turn_ready, 1)
            dve.wait_ge(turn_ready, 1)
            link(dve.tensor_scalar(pcol(FHI), pcol(TURN), 768.0, 768.0, ALU.add, ALU.subtract))
            dve.tensor_tensor(pcol(FLO), pcol(TURN), pcol(FHI), ALU.subtract).then_inc(frac_done, 1)
            dve.wait_ge(silu_c_done, 1)
            dve.tensor_copy(c32[:, :, :], cols[:, 0:KD].unsqueeze(2).to_broadcast([P, KD, 32])).then_inc(c32_done, 1)
            link(dve.tensor_tensor(pcol(XM), lre, pcol(STEP), ALU.mult))
            exp_small(pcol(MAG), pcol(XM))
            dve.wait_ge(trig1_done, 2)
            link(dve.tensor_tensor(pcol(LBR), pcol(MAG), pcol(COS1), ALU.mult))
            link(dve.tensor_tensor(pcol(LBI), pcol(MAG), pcol(SIN1), ALU.mult))
            link(dve.tensor_tensor(pcol(DEN), lre, lre, ALU.mult))
            link(dve.tensor_tensor(pcol(T0), lim, lim, ALU.mult))
            link(dve.tensor_tensor(pcol(DEN), pcol(DEN), pcol(T0), ALU.add))
            link(dve.reciprocal(pcol(DEN), pcol(DEN)))
            link(dve.tensor_scalar(pcol(T0), pcol(LBR), 1.0, None, ALU.subtract))
            link(dve.tensor_tensor(pcol(T1), pcol(T0), lre, ALU.mult))
            link(dve.tensor_tensor(pcol(T2), pcol(LBI), lim, ALU.mult))
            link(dve.tensor_tensor(pcol(T1), pcol(T1), pcol(T2), ALU.add))
            link(dve.tensor_tensor(pcol(CRE), pcol(T1), pcol(DEN), ALU.mult))
            link(dve.tensor_tensor(pcol(T1), pcol(LBI), lre, ALU.mult))
            link(dve.tensor_tensor(pcol(T2), pcol(T0), lim, ALU.mult))
            link(dve.tensor_tensor(pcol(T1), pcol(T1), pcol(T2), ALU.subtract))
            link(dve.tensor_tensor(pcol(CIM), pcol(T1), pcol(DEN), ALU.mult))
            cre = pcol(CRE).unsqueeze(2).to_broadcast([P, NT, HG])
            cim = pcol(CIM).unsqueeze(2).to_broadcast([P, NT, HG])
            btmp = zst_c[:, 0:NT * HG].rearrange("p (t h) -> p t h", t=NT)
            link(dve.tensor_tensor(bb[:, 0], cre, b_raw[:, 0], ALU.mult))
            link(dve.tensor_tensor(btmp, cim, b_raw[:, 1], ALU.mult))
            link(dve.tensor_tensor(bb[:, 0], bb[:, 0], btmp, ALU.subtract))
            link(dve.tensor_tensor(bb[:, 1], cre, b_raw[:, 1], ALU.mult))
            link(dve.tensor_tensor(btmp, cim, b_raw[:, 0], ALU.mult))
            link(dve.tensor_tensor(bb[:, 1], bb[:, 1], btmp, ALU.add))
            to_hT(0)
            ada_cols(0, 4)
            hT_evict(0)

            def stage(b):
                diag = zst_b.rearrange("p (t n) -> p t n", n=P + 2 * HG)
                for i in range(2):
                    if b or i:
                        dve.wait_ge(zt_ps, 4 * b + (1 if i else -2))
                    link(dve.tensor_copy(diag[0:NS, :, 0:HG], bb[0:NS, i, TPB * b:TPB * b + TPB, :]))
                    dve.tensor_copy(diag[NS:P, :, HG:2 * HG], bb[NS:P, i, TPB * b:TPB * b + TPB, :]
                                    ).then_inc(zst_done, 1)
                for i in range(2):
                    if b or i:
                        dve.wait_ge(zt_ps, 4 * b + (3 if i else 0))
                    dve.tensor_tensor(zst_c.rearrange("p (j n) -> p j n", j=8),
                                      c_raw[:, i, b, :].unsqueeze(1).to_broadcast([P, 8, NS]),
                                      chmask[:, :].unsqueeze(2).to_broadcast([P, 8, NS]), ALU.mult
                                      ).then_inc(zst_done, 1)
                dve.wait_ge(zst_done, 4 * b + 4)

            def bu(i):
                return ps[:, 4 + 2 * i:6 + 2 * i, :].rearrange("p a (t s) -> p (a t) s", t=2)

            for b in range(NBLK):
                q = b % 2
                stage(b)
                dve.wait_ge(table_done, 2 * b + 2)
                dve.wait_ge(bu_ps, b + 1)
                if b:
                    dve.wait_ge(y5_ps, b)
                dve.tensor_tensor(prod[:, 0], bu(0), cosT[:, q], ALU.mult).then_inc(rot_done, 1)
                dve.tensor_tensor(prod[:, 1], bu(1), sinT[:, q], ALU.mult).then_inc(rot_done, 1)
                dve.tensor_tensor(prod2[:, 0], bu(1), cosT[:, q], ALU.mult).then_inc(rot_done, 1)
                dve.tensor_tensor(prod2[:, 1], bu(0), sinT[:, q], ALU.mult).then_inc(rot_done, 1)
                for i, v in enumerate((v_re, v_im)):
                    dve.wait_ge(v_done, 2 * b + i + 1)
                    for t in range(TPB):
                        mag = par[:, MAG, TPB * b + t:TPB * b + t + 1].to_broadcast([P, SEQ])
                        dve.tensor_tensor_scan(v[:, t, :], mag, v[:, t, :], 0.0, ALU.mult, ALU.add
                                               ).then_inc(scan_done, 1)
                dve.wait_ge(scan_done, 2 * TPB * (b + 1))
                dve.tensor_tensor(prod[:, 0], v_re, cosT[:, q], ALU.mult).then_inc(dve_step, 1)
                dve.tensor_tensor(prod[:, 1], v_im, sinT[:, q], ALU.mult).then_inc(post_d, 1)
                count[0] += 1
                ada_cols(4 + 5 * b, 9 + 5 * b)
                dve.wait_ge(y5_ps, b + 1)
                stt(uT[:, b, :], uT[:, b, :], cols[:, C_D + b:C_D + b + 1], ps[:, 3, 0:256], ALU.mult, ALU.add
                    ).then_inc(y5_done, 1)
            gate_row(0)
            for i in range(4):
                tt, n = divmod(i, 2)
                dve.wait_ge(sig_done, i + 1)
                dve.tensor_tensor(hn[:, tt, 512 * n:512 * n + 512], ps[:, 2 * i, :],
                                  junk[:, 512 * (i % 2):512 * (i % 2) + 512], ALU.mult).then_inc(glu_done, 1)
            dve.wait_ge(glu_done, 4)
            residual(0, lambda tt: hn[:, tt, :])
            to_hT(1)
            hT_evict(1)
            ffn_turn = lambda g: (N_FFN + g) // RING
            for f in range(FB):
                for ch, q in ((1, 2 * f), (0, 2 * f + 1)):
                    swiglu_out(f, q, ch, N_FFN, ffn_turn, 0, q - 1 if f else None)
            gate_row(1)
            residual(1, y_banks)
            to_hT(2)
            hT_evict(2)
            for n in range(2):
                wait_used(dve, N_QKV + 4 + n)
                for tt in range(TT):
                    dve.tensor_copy(v_sb[:, tt, 512 * n:512 * n + 512], ps[:, Y_BANK + 2 * tt + n, :]
                                    ).then_inc(v_out, 1)

            def on_diagonal(z):
                return z.rearrange("p g (b n) -> p g b n", b=3)[:, :, 0:3:2, :]

            mask = strict[:, :].unsqueeze(1).unsqueeze(1).to_broadcast([P, 2, 2, P])
            for h in range(HEADS // 2 + 1):
                if h < HEADS // 2:
                    b = h % 2
                    z = z_w[:, b]
                    dve.wait_ge(zcopy_done, h + 1)
                    if h >= 2:
                        dve.wait_ge(sp_done, h - 1)
                    stt(z_e[:, b], z, -1.0, z, ALU.mult, ALU.min).then_inc(zabs_done, 1)
                    dve.wait_ge(ln_done, h + 1)
                    if h >= 2:
                        dve.wait_ge(sfx_ps, h - 1)
                    stt(z_p[:, b], z, 0.0, z_e[:, b], ALU.max, ALU.add).then_inc(sp_done, 1)
                    dve.wait_ge(sp_done, h + 1)
                    dve.tensor_tensor(on_diagonal(z_p[:, b]), on_diagonal(z_p[:, b]), mask, ALU.mult
                                      ).then_inc(spm_done, 1)
                if h:
                    b = (h - 1) % 2
                    dve.wait_ge(wexp_done, h)
                    for g in range(2):
                        w = on_diagonal(z_w[:, b])[:, g]
                        stt(w, w, 1.0, mask[:, g], ALU.min, ALU.mult).then_inc(w_done, 1)
                if h < HEADS // 2:
                    b = h % 2
                    dve.wait_ge(sfx_ps, h + 1)
                    stt(z_w[:, b], ps[:, 4:6, 0:384], -1.0, z_w[:, b], ALU.mult, ALU.add).then_inc(arg_done, 1)
            gate_row(2)
            residual(2, y_banks)
            to_hT(3)
            hT_evict(3)
            dve.memset(macc, 0.0).then_inc(sc_done, 4)
            for tt in range(TT):
                r = rt[:, tt]
                dve.wait_ge(lg_ps, 1)
                link(dve.tensor_copy(r[:, 0:8], ps[:, S_BANK, 8 * tt:8 * tt + 8]))
                link(dve.tensor_reduce(r[:, 82:83], r[:, 0:8], AX.X, ALU.max))
                dve.tensor_scalar(r[:, 80:81], r[:, 82:83], -1.0, None, ALU.mult).then_inc(lmax_done, 1)
            for tt in range(TT):
                r = rt[:, tt]
                dve.wait_ge(pexp_done, tt + 1)
                link(dve.reciprocal(r[:, 81:82], r[:, 81:82]))
                link(dve.tensor_scalar(r[:, 8:16], r[:, 8:16], r[:, 81:82], None, ALU.mult))
                link(dve.max(r[:, 16:24], r[:, 8:16]))
                link(dve.max_index(r[:, 24:32].bitcast(U32), r[:, 16:24], r[:, 8:16]))
                link(dve.tensor_tensor(r[:, 84:85], r[:, 16:17], r[:, 17:18], ALU.add))
                link(dve.reciprocal(r[:, 84:85], r[:, 84:85]))
                link(dve.tensor_scalar(r[:, 82:84], r[:, 16:18], r[:, 84:85], None, ALU.mult))
                link(dve.tensor_copy(r[:, 86:88], r[:, 24:26].bitcast(U32)))
                for j in range(2):
                    link(dve.tensor_scalar(r[:, 32 + 8 * j:40 + 8 * j], steps[:, 0:8], r[:, 86 + j:87 + j], None,
                                           ALU.is_equal))
                link(dve.tensor_tensor(r[:, 48:56], r[:, 32:40], r[:, 40:48], ALU.add))
                link(dve.tensor_scalar(r[:, 32:40], r[:, 32:40], r[:, 82:83], None, ALU.mult))
                stt(rcol[:, :, 2 + tt], r[:, 40:48], r[:, 83:84], r[:, 32:40], ALU.mult, ALU.add).then_inc(sel_done, 1)
            dve.wait_ge(rank_ps, 1)
            for tt in range(TT):
                r = rt[:, tt]
                link(stt(r[:, 56:64], ps[:, S_BANK, 16 + 8 * tt:24 + 8 * tt], 1.0, r[:, 48:56], ALU.add, ALU.mult))
                link(dve.tensor_scalar(rcol[:, :, tt], r[:, 56:64], 1.0, None, ALU.subtract))
            one = cnt[0:1, 3, :]
            link(dve.memset(one, 1.0))
            link(dve.tensor_scalar(cnt[0:1, 1, :], ps[0:1, S_BANK, 32:40], float(P) + 0.5, None, ALU.is_gt))
            link(dve.tensor_scalar(cnt[0:1, 0, :], cnt[0:1, 1, :], 1.0, None, ALU.add))
            link(dve.tensor_tensor_scan(cnt[0:1, 2, :], one, cnt[0:1, 1, :], 0.0, ALU.mult, ALU.add))
            link(dve.tensor_copy(cnt[0:1, 3, :], cnt[0:1, 1, :]))
            link(dve.tensor_tensor(cnt[0:1, 2, :], cnt[0:1, 2, :], cnt[0:1, 1, :], ALU.subtract))
            link(dve.tensor_tensor(cnt[0:1, 1, :], cnt[0:1, 2, :], steps[0:1, 0:8], ALU.add))
            link(dve.tensor_copy(cnt_i[:, 3, :], cnt[0:1, 3, :]))
            link(dve.tensor_scalar(cnt[0:1, 1, :], cnt[0:1, 1, :], 2.0, float(FB), ALU.add, ALU.mult))
            link(dve.tensor_scalar(cnt[0:1, 1, :], cnt[0:1, 1, :], 2.0, None, ALU.subtract))
            link(dve.tensor_scalar(cnt[0:1, 2, :], cnt[0:1, 2, :], 1.0, float(FB), ALU.add, ALU.mult))
            dve.tensor_copy(cnt_i[:, 0:3, :], cnt[0:1, 0:3, :]).then_inc(route_done, 1)
            dve.wait_ge(route_done, 1)

            with dve.Fori(0, NE) as e:
                nch, more, items2, c1 = expert_counts(dve, e)
                moe_turn = lambda g: e * (PER_EXPERT // RING) + (N_MOE + g) // RING
                dve.tensor_copy(pick, rcol[:, bass.ds(e, 1), :]).then_inc(pick_done, 1)
                dve.wait_ge(pick_done, e + 1)
                for tt in range(TT):
                    dve.tensor_scalar(g1[:, tt], steps[:, :], pick[:, 0, tt:tt + 1], None, ALU.is_equal
                                      ).then_inc(onehot_done, 1)
                    dve.tensor_scalar(gw[:, tt], steps[:, :], pick[:, 0, tt:tt + 1], pick[:, 0, 2 + tt:3 + tt],
                                      ALU.is_equal, ALU.mult).then_inc(onehot_done, 1)
                with dve.If(nch > 1):
                    dve.wait_ge(st_ps, e + 1)
                    dve.tensor_copy(scT[:, 1, :], ps[:, Y_BANK + 3, 256:512])
                dve.wait_ge(st_ps, e + 1)
                dve.tensor_copy(scT[:, 0, :], ps[:, Y_BANK + 3, 0:256]).then_inc(st_done, 1)
                for f in range(FB):
                    q2 = items2 + f * nch
                    with dve.If(nch > 1):
                        swiglu_out(f, q2 + 2, 1, N_MOE, moe_turn, c1, q2 + 1)
                    swiglu_out(f, q2 + more + 2, 0, N_MOE, moe_turn, c1, q2 + 2)
                with dve.If(nch > 1):
                    wait_used(dve, N_MOE + PER_EXPERT - 1, moe_turn(PER_EXPERT - 1))
                    dve.tensor_copy(ysb[:, 1, 512:D], ps[:, Y_BANK + 3, :])
                wait_used(dve, N_MOE + PER_EXPERT - 1, moe_turn(PER_EXPERT - 1))
                dve.tensor_copy(ysb[:, 0, 512:D], ps[:, Y_BANK + 1, :]).then_inc(ysb_dve, 1)
                for i in range(4):
                    tt, n = divmod(i, 2)
                    dve.wait_ge(sc_ps, 4 * e + i + 1)
                    m = macc[:, tt, 512 * n:512 * n + 512]
                    dve.tensor_tensor(m, m, ps[:, T_BANK + i % 2, :], ALU.add).then_inc(sc_done, 1)
                dve.wait_ge(sc_done, 4 * e + 8)
            gate_row(3)
            residual(3, lambda tt: macc[:, tt, :])

        @block.tensor
        def _(pe):
            def columns(dst, src, n):
                return pe.transpose(dst, src, ident[0:n, 0:n])

            pe.wait_ge(consts_done, 6)
            pe.wait_ge(cols_ready, 1)
            columns(ps[:, 0, C_C:C_C + KD], r_c, KD)
            columns(ps[:, 0, C_LRE:C_LRE + NT], r_lam[:, 0, :], NT)
            columns(ps[:, 0, C_LIM:C_LIM + NT], r_lam[:, 1, :], NT)
            columns(ps[:, 0, C_LS:C_LS + NT], rows[0:NT, 512:640], NT)
            columns(ps[:, 0, C_D:C_D + NBLK], r_d, NBLK)
            for k in range(KD):
                ins = columns(ps[:, 0, C_G + 8 * k:C_G + 8 * k + 8], r_g[:, P * k:P * k + P], 8)
            ins.then_inc(cols_ps, 1)
            for j in range(4):
                ins = columns(ps[:, 1, 24 * j:24 * j + 24], r_b[:, P * j:P * j + P], 24)
            ins.then_inc(cols_ps, 1)

            def ada(lo, hi):
                for i in range(lo, hi):
                    n = ada_place(*divmod(i, MODS))
                    wait_landed(pe, n)
                    above(pe, part_out, i)
                    for k in range(KD):
                        j = k % 4
                        ins = pe.matmul(ps[32 * j:32 * j + 32, 0, :], c32[:, k, :], gran8(n)[:, k, :],
                                        start=k < 4, stop=k >= 4, tile_position=(0, 32 * j))
                    ins.then_inc(used[n % RING], 1)
                    pe.wait_ge(part_out, i + 1)
                    above(pe, mod_out, i)
                    for j in range(4):
                        ins = pe.matmul(ps[:, 1, j:j + 1], part[:, P * j:P * j + P], inv32[:, :],
                                        start=True, stop=True)
                    ins.then_inc(mod_ps, 1)

            def transpose_x(s):
                pe.wait_ge(xn_done, 2 * s + 2)
                for k in range(KD):
                    for tt in range(TT):
                        ins = pe.transpose(ps[:, Y_BANK + k // 2, 256 * (k % 2) + P * tt:256 * (k % 2) + P * tt + P],
                                           hn[:, tt, P * k:P * k + P], ident[:, :])
                    if k % 2:
                        ins.then_inc(hT_ps, 1)

            def wait_hT(s):
                pe.wait_ge(hT_act, 4 * s + 4)
                pe.wait_ge(hT_dve, 4 * s + 4)

            def gate_row(s):
                pe.wait_ge(diag_done, s + 1)
                for n in range(2):
                    ins = pe.matmul(ps[:, 2 + n, :], ones[:, :], tbuf[:, 512 * n:512 * n + 512], start=True, stop=True)
                ins.then_inc(gg_ps, 1)

            def gate_product(f, q2, ch, xT, base, turn):
                n = base + gate_at(f)
                wait_landed(pe, n, turn(gate_at(f)))
                above(pe, silu_done, q2 + 2)
                for k in range(KD):
                    ins = pe.matmul(ps[:, G_BANK, :], xT(k, ch), gran8(n)[:, k, :], start=k == 0, stop=k == KD - 1)
                ins.then_inc(gate1_done if ch else used[n % RING], 1)

            def up_product(f, q2, ch, xT, base, turn):
                n = base + up_at(f)
                wait_landed(pe, n, turn(up_at(f)))
                above(pe, act_done, q2 + 2)
                for k in range(KD):
                    ins = pe.matmul(ps[:, U_BANK, :], xT(k, ch), gran8(n)[:, k, :], start=k == 0, stop=k == KD - 1)
                ins.then_inc(up1_done if ch else used[n % RING], 1)

            def turn_item(q, ch):
                pe.wait_ge(act_done, q + 1)
                above(pe, aT_done, q)
                for j in range(4):
                    ins = pe.transpose(ps[:, T_BANK, P * j:P * j + P], a_sb[:, ch, P * j:P * j + P], ident[:, :])
                ins.then_inc(tr_done, 1)

            def down_product(f, q, ch, base, turn):
                n = base + down_at(f)
                wait_landed(pe, n, turn(down_at(f)))
                pe.wait_ge(aT_done, q + 1)
                for j in range(4):
                    for h in range(2):
                        ins = pe.matmul(ps[:, Y_BANK + 2 * ch + h, :], aT[:, ch, j, :],
                                        gran4(n)[:, j, 512 * h:512 * h + 512],
                                        start=f == 0 and j == 0, stop=f == FB - 1 and j == 3)
                if not ch:
                    ins.then_inc(used[n % RING], 1)

            def item(f, q2, before, ch, xT, base, turn):
                gate_product(f, q2, ch, xT, base, turn)
                if f:
                    turn_item(before, ch)
                up_product(f, q2, ch, xT, base, turn)
                if f:
                    down_product(f - 1, before, ch, base, turn)

            pe.wait_ge(cols_done, 1)
            pe.wait_ge(c32_done, 1)
            transpose_x(0)
            ada(0, 4)
            wait_hT(0)
            wait_landed(pe, N_WIN)
            for b in range(NBLK):
                for k in range(KD):
                    ins = pe.matmul(ps[:, b // 2, 256 * (b % 2):256 * (b % 2) + 256],
                                    gran8(N_WIN)[:, k, P * b:P * b + P], hT[:, k, :], start=k == 0, stop=k == KD - 1)
                if b == 1:
                    ins.then_inc(u_ps, 1)
                    pe.wait_ge(mod_out, 4)
                elif b == 3:
                    ins.then_inc(used[N_WIN % RING], 1)
            for b in range(NBLK):
                for i in range(4):
                    pe.wait_ge(zst_done, 4 * b + i + 1)
                    above(pe, zt_done, 5 * b + (0, 1, 2, 4)[i])
                    for t in range(TPB):
                        src = (zst_b if i < 2 else zst_c)[:, P * t:P * t + P]
                        ins = pe.transpose(ps[:, T_BANK, P * t:P * t + P], src, ident[:, :])
                    ins.then_inc(zt_ps, 1)
                pe.wait_ge(zt_done, 5 * b + 2)
                pe.wait_ge(u_done, 2)
                above(pe, rot_done, 4 * b)
                for i in range(2):
                    for t in range(TPB):
                        ins = pe.matmul(ps[:, 4 + 2 * i + t // 2, 256 * (t % 2):256 * (t % 2) + 256],
                                        bT[:, i, t, :], uT[:, b, :], start=True, stop=True)
                ins.then_inc(bu_ps, 1)
                ada(4 + 5 * b, 9 + 5 * b)
                pe.wait_ge(zt_done, 5 * b + 5)
                pe.wait_ge(post_d, b + 1)
                pe.wait_ge(post_p, 2 * b + 2)
                above(pe, y5_done, b)
                terms = ((0, prod[:, 0]), (1, prod[:, 1]), (2, prod2[:, 0]), (2, prod2[:, 1]))
                for j, (i, state) in enumerate(terms):
                    for t in range(TPB):
                        ins = pe.matmul(ps[:, 3, 0:256], cT[:, i, t, :], state[:, t, :],
                                        start=j == 0 and t == 0, stop=j == 3 and t == TPB - 1)
                ins.then_inc(y5_ps, 1)
            gate_row(0)
            pe.wait_ge(gelu_done, 4)
            for i in range(4):
                tt, n = divmod(i, 2)
                if i == 1:
                    pe.wait_ge(gg_done, 1)
                for half in range(2):
                    wait_landed(pe, N_WOUT + half)
                    for k in range(NBLK):
                        ins = pe.matmul(ps[:, 2 * i + half, :], uT[:, k, P * tt:P * tt + P],
                                        gran4(N_WOUT + half)[:, k, 512 * n:512 * n + 512],
                                        start=k == 0, stop=k == NBLK - 1)
                    if i == 3:
                        ins.then_inc(used[(N_WOUT + half) % RING], 1)
                    elif half:
                        ins.then_inc(wo_ps, 1)
            transpose_x(1)
            wait_hT(1)
            tokens = lambda k, ch: hT[:, k, P * ch:P * ch + P]
            ffn_turn = lambda g: (N_FFN + g) // RING
            for f in range(FB):
                item(f, 2 * f - 2, 2 * f - 2, 1, tokens, N_FFN, ffn_turn)
                item(f, 2 * f - 1, 2 * f - 1, 0, tokens, N_FFN, ffn_turn)
            for ch, q in ((1, 2 * FB - 2), (0, 2 * FB - 1)):
                turn_item(q, ch)
                down_product(FB - 1, q, ch, N_FFN, ffn_turn)
            pe.wait_ge(aT_done, 2 * FB)
            gate_row(1)
            transpose_x(2)
            wait_hT(2)
            for r in range(4):
                n = N_QKV + r
                wait_landed(pe, n)
                above(pe, qk_done, r - 1)
                if r == 1:
                    pe.wait_ge(gg_done, 2)
                for j in range(4):
                    for k in range(KD):
                        ins = pe.matmul(ps[:, 2 * (r % 2) + j // 2, 256 * (j % 2):256 * (j % 2) + 256],
                                        gran8(n)[:, k, P * j:P * j + P], hT[:, k, :], start=k == 0, stop=k == KD - 1)
                ins.then_inc(used[n % RING], 1)
            for r in range(2):
                n = N_QKV + 4 + r
                wait_landed(pe, n)
                for tt in range(TT):
                    for k in range(KD):
                        ins = pe.matmul(ps[:, Y_BANK + 2 * tt + r, :], tokens(k, tt), gran8(n)[:, k, :],
                                        start=k == 0, stop=k == KD - 1)
                ins.then_inc(used[n % RING], 1)

            def scores(h):
                b = h % 2
                pe.wait_ge(qk_done, 4)
                if h >= 2:
                    pe.wait_ge(zcopy_done, h - 1)
                for g in range(2):
                    r = slice(DH * g, DH * g + DH)
                    pe.matmul(ps[:, 2 * b + g, 0:256], kT[r, h, 0:P], qT[r, h, :], start=True, stop=True)
                    ins = pe.matmul(ps[:, 2 * b + g, 256:384], kT[r, h, P:SEQ], qT[r, h, P:SEQ], start=True, stop=True)
                ins.then_inc(z_ps, 1)

            def suffix(h):
                b = h % 2
                pe.wait_ge(spm_done, h + 1)
                if h:
                    pe.wait_ge(arg_done, h)
                else:
                    pe.wait_ge(v_out, 4)
                for g in range(2):
                    z = z_p[:, b, g]
                    pe.matmul(ps[:, 4 + g, 0:256], incl[:, :], z[:, 0:256], start=True, stop=False)
                    pe.matmul(ps[:, 4 + g, P:256], ones[:, :], z[:, 256:384], start=False, stop=True)
                    ins = pe.matmul(ps[:, 4 + g, 256:384], incl[:, :], z[:, 256:384], start=True, stop=True)
                ins.then_inc(sfx_ps, 1)

            def values(h):
                b = h % 2
                pe.wait_ge(w_done, 2 * h + 2)
                if h >= 2:
                    pe.wait_ge(o_done, h - 1)
                for g in range(2):
                    hd = slice(DH * (2 * h + g), DH * (2 * h + g) + DH)
                    o = ps[DH * g:DH * g + DH, 6 + b, :]
                    pe.matmul(o[:, 0:256], v_sb[:, 0, hd], z_w[:, b, g, 0:256], start=True, stop=False)
                    ins = pe.matmul(o[:, P:256], v_sb[:, 1, hd], z_w[:, b, g, 256:384], start=False, stop=True)
                ins.then_inc(o_ps, 1)

            for h in range(HEADS // 2 + 2):
                if h < HEADS // 2:
                    scores(h)
                if 1 <= h <= HEADS // 2:
                    suffix(h - 1)
                if h >= 2:
                    values(h - 2)
            pe.wait_ge(o_done, HEADS // 2)
            for r in range(2):
                n = N_SBOUT + r
                wait_landed(pe, n)
                for tt in range(TT):
                    for k in range(KD):
                        ins = pe.matmul(ps[:, Y_BANK + 2 * tt + r, :], oT[:, k, P * tt:P * tt + P], gran8(n)[:, k, :],
                                        start=k == 0, stop=k == KD - 1)
                ins.then_inc(used[n % RING], 1)
            gate_row(2)
            transpose_x(3)
            wait_hT(3)
            pe.wait_ge(router_in, 32)
            pe.wait_ge(gg_done, 3)
            for tt in range(TT):
                lg = ps[:, S_BANK, 8 * tt:8 * tt + 8]
                for k in range(KD):
                    pe.matmul(lg, tokens(k, tt), wr_sb[:, k, :], start=k == 0, stop=False)
                ins = pe.matmul(lg, ones[0:1, :], br_sb[:, :], start=False, stop=True)
            ins.then_inc(lg_ps, 1)
            pe.wait_ge(sel_done, 2)
            chosen = [rt[:, tt, 48:56] for tt in range(TT)]
            rank = lambda i: ps[:, S_BANK, 16 + 8 * i:24 + 8 * i]
            pe.matmul(rank(0), strict[:, :], chosen[0], start=True, stop=True)
            pe.matmul(rank(1), ones[:, :], chosen[0], start=True, stop=False)
            pe.matmul(rank(1), strict[:, :], chosen[1], start=False, stop=True)
            pe.matmul(rank(2), ones[:, :], chosen[0], start=True, stop=False)
            pe.matmul(rank(2), ones[:, :], chosen[1], start=False, stop=True).then_inc(rank_ps, 1)

            gathered = lambda k, ch: xe[:, k, ch, :]
            pe.wait_ge(route_done, 1)
            with pe.Fori(0, NE) as e:
                nch, more, items2, _ = expert_counts(pe, e)
                moe_turn = lambda g: e * (PER_EXPERT // RING) + (N_MOE + g) // RING
                pe.wait_ge(onehot_done, 4 * e + 4)
                pe.wait_ge(silu_done, items2 + 2)
                pe.wait_ge(act_done, items2 + 2)
                pe.wait_ge(aT_done, items2 + 2)
                pe.wait_ge(sc_done, 4 * e + 4)

                def gather(ch):
                    for k in range(KD):
                        bank = (G_BANK, T_BANK)[ch] + k // 4
                        for tt in range(TT):
                            ins = pe.matmul(ps[:, bank, P * (k % 4):P * (k % 4) + P], hn[:, tt, P * k:P * k + P],
                                            g1[:, tt, P * ch:P * ch + P], start=tt == 0, stop=tt == TT - 1)
                    return ins

                def scatter_weights(ch):
                    for tt in range(TT):
                        ins = pe.transpose(ps[:, Y_BANK + 3, 256 * ch + P * tt:256 * ch + P * tt + P],
                                           gw[:, tt, P * ch:P * ch + P], ident[:, :])
                    return ins

                with pe.If(nch > 1):
                    gather(1)
                gather(0).then_inc(xe_ps, 1)
                with pe.If(nch > 1):
                    scatter_weights(1)
                scatter_weights(0).then_inc(st_ps, 1)
                pe.wait_ge(xe_done, e + 1)
                pe.wait_ge(st_done, e + 1)
                for f in range(FB):
                    q2 = items2 + f * nch
                    with pe.If(nch > 1):
                        item(f, q2, q2, 1, gathered, N_MOE, moe_turn)
                    item(f, q2 + more, q2 + 1, 0, gathered, N_MOE, moe_turn)
                q2 = items2 + FB * nch
                with pe.If(nch > 1):
                    turn_item(q2, 1)
                    down_product(FB - 1, q2, 1, N_MOE, moe_turn)
                turn_item(q2 + 1, 0)
                down_product(FB - 1, q2 + 1, 0, N_MOE, moe_turn)
                pe.wait_ge(aT_done, q2 + 2)
                pe.wait_ge(ysb_act, e + 1)
                pe.wait_ge(ysb_dve, e + 1)
                for i in range(4):
                    tt, n = divmod(i, 2)
                    if i >= 2:
                        pe.wait_ge(sc_done, 4 * e + i + 3)
                    dst = ps[:, T_BANK + i % 2, :]

                    def spread(ch, start, stop):
                        return pe.matmul(dst, scT[:, ch, P * tt:P * tt + P], ysb[:, ch, 512 * n:512 * n + 512],
                                         start=start, stop=stop)

                    with pe.If(nch > 1):
                        spread(1, True, False)
                        spread(0, False, True).then_inc(sc_ps, 1)
                    with pe.Else():
                        spread(0, True, True).then_inc(sc_ps, 1)
            pe.wait_ge(sc_done, 4 * NE + 4)
            gate_row(3)


_INS = ["x", "c", "ada_w", "ada_b", "norm_g", "s5_w_in", "s5_lambda_re", "s5_lambda_im", "s5_b_re", "s5_b_im",
        "s5_c_re", "s5_c_im", "s5_d", "s5_log_step", "s5_w_out", "sb_w_qkv", "sb_w_out", "ffn_w_gate_up",
        "ffn_w_down", "moe_w_router", "moe_b_router", "moe_w_gate_up", "moe_w_down"]


def kernel(**inputs):
    import numpy as np
    import concourse.bacc as bacc
    from concourse.bass_utils import run_bass_kernel_spmd

    nc = bacc.Bacc("TRN2", target_bir_lowering=False, num_devices=1)
    arrays, args = {}, []
    for name in _INS:
        a = np.ascontiguousarray(inputs[name])
        arrays[f"in_{name}_dram"] = a
        args.append(nc.dram_tensor(f"in_{name}_dram", a.shape, mybir.dt.from_np(a.dtype), kind="ExternalInput").ap())
    args.append(nc.dram_tensor("out_dram", (1, SEQ, D), F32, kind="ExternalOutput").ap())
    program(nc, *args)
    r = run_bass_kernel_spmd(nc, [arrays], core_ids=[0])
    return r.results[0]["out_dram"]
```

```python
import math
from contextlib import ExitStack

import concourse.bass as bass
from concourse import mybir

F32 = mybir.dt.float32
I32 = mybir.dt.int32
U32 = mybir.dt.uint32
ALU = mybir.AluOpType
ACT = mybir.ActivationFunctionType
AX = mybir.AxisListType

P = 128
D = 1024
KD = D // P
SEQ = 256
TT = SEQ // P
W5 = D // 2
NBLK = W5 // P
HG = 16
NS = 64
TPB = 4
NT = NBLK * TPB
HEADS = 16
DH = 64
FF = 7 * D // 2
FB = FF // 512
NE = 8
EPS = 1e-6
ROOT_D = 32.0
assert ROOT_D ** 2 == D
MODS = 12
RING = 7
GRAN = 4096
ARENA = 13568
MAGIC = 12582912.0
TWO_PI = 2 * math.pi
SIN_SCALE = TWO_PI * (1 - 2e-7)

G_BANK, U_BANK, T_BANK, S_BANK, Y_BANK = 0, 1, 2, 3, 4

PER_EXPERT = 3 * FB


def gate_at(f):
    return 0 if f == 0 else 3 * f - 1


def up_at(f):
    return gate_at(f) + 1


def down_at(f):
    return 3 * f + 4 if f < FB - 1 else PER_EXPERT - 1


N_ADA0A = 0
N_WIN = 4
N_ADA0B = 5
N_ADA1 = 13
N_WOUT = 25
N_FFN = 27
N_QKV = 48
N_SBOUT = 54
N_MOE = 56
assert N_MOE % RING == 0 and PER_EXPERT % RING == 0


def ada_place(layer, r):
    if layer:
        return N_ADA1 + r
    return N_ADA0A + r if r < 4 else N_ADA0B + r - 4


def program(nc, x, c, ada_w, ada_b, norm_g, s5_w_in, s5_lambda_re, s5_lambda_im, s5_b_re, s5_b_im,
            s5_c_re, s5_c_im, s5_d, s5_log_step, s5_w_out, sb_w_qkv, sb_w_out, ffn_w_gate_up,
            ffn_w_down, moe_w_router, moe_b_router, moe_w_gate_up, moe_w_down, out):
    ctx = ExitStack()
    with ctx:
        def sb(name, shape, dt=F32):
            return ctx.enter_context(nc.sbuf_tensor(name, shape, dt))

        def sem(name):
            return ctx.enter_context(nc.semaphore(name))

        ps = ctx.enter_context(nc.psum_tensor("ps", [P, 8, 512], F32))

        x_sb = sb("x_sb", [P, TT, D])
        hT = sb("hT", [P, KD, SEQ])
        hn = sb("hn", [P, TT, D])
        ring = sb("ring", [P, RING, GRAN])
        gg = sb("gg", [P, D])
        junk = sb("junk", [P, D])
        tbuf = sb("tbuf", [P, D])
        ident = sb("ident", [P, P])
        ones = sb("ones", [P, P])
        incl = sb("incl", [P, P])
        strict = sb("strict", [P, P])
        chmask = sb("chmask", [P, 8])
        steps = sb("steps", [P, SEQ])
        inv32 = sb("inv32", [P, 1])
        half = sb("half", [P, 1])
        cols = sb("cols", [P, 128])
        c32 = sb("c32", [P, KD, 32])
        adab = sb("adab", [P, 4, 24])
        modc = sb("modc", [P, 2, MODS, 4])
        scale_c = sb("scale_c", [P, 4, KD])
        gate_c = sb("gate_c", [P, 4, KD])
        stat = sb("stat", [P, 16])
        wr_sb = sb("wr_sb", [P, KD, NE])
        br_sb = sb("br_sb", [1, NE])

        arena = sb("arena", [P, ARENA])

        def view(at, shape):
            n = math.prod(shape)
            names = [f"d{i}" for i in range(len(shape))]
            ap = arena[:, at:at + n]
            if len(shape) == 1:
                return ap
            return ap.rearrange(f"p ({' '.join(names)}) -> p {' '.join(names)}",
                                **{k: v for k, v in zip(names, shape)})

        class Place:
            def __init__(self):
                self.at = 0

            def __call__(self, *shape):
                v = view(self.at, shape)
                self.at += math.prod(shape)
                assert self.at <= ARENA
                return v

        pl = Place()
        cosT, sinT = pl(2, TPB, SEQ), pl(2, TPB, SEQ)
        bT = pl(2, TPB, P)
        cT = pl(3, TPB, P)
        zst_b = (pl(640), gg[:, 0:640])
        zst_c = (pl(512), tbuf[:, 0:512])
        prod = pl(2, TPB, SEQ)
        uT = pl(NBLK, SEQ)
        b_raw = pl(2, NT, HG)
        bb = pl(2, NT, HG)
        c_raw = pl(2, NBLK, NS)
        par = pl(32, NT)
        rows = pl(640)
        v_re = hn[:, 0, :].rearrange("p (t s) -> p t s", t=TPB)
        v_im = hn[:, 1, :].rearrange("p (t s) -> p t s", t=TPB)
        prod2 = hT[:, :, :].rearrange("p (a t) s -> p a t s", a=2)

        pl = Place()
        qT, kT, oT = pl(KD, SEQ), pl(KD, SEQ), pl(KD, SEQ)
        v_sb = pl(TT, D)
        z_e = pl(2, 2, 384)
        z_p = pl(2, 2, 384)
        z_w = pl(3, 2, 384)

        pl = Place()
        a_sb = pl(2, 512)
        aT = pl(2, 4, P)
        sg = pl(512)
        xe = pl(KD, 2, P)
        ysb = pl(2, D)
        scT = pl(2, SEQ)
        g1 = pl(TT, SEQ)
        gw = pl(TT, SEQ)
        macc = pl(TT, D)
        rt = pl(TT, 96)
        rcol = pl(NE, 4)
        pick = pl(1, 4)
        cnt = pl(6, NE)
        g_part = pl(2, 512)
        silu_T = pl(4, 64)
        fold = pl(2, P)
        slots = pl(3, SEQ)
        cnt_i = sb("cnt_i", [1, 6, NE], I32)

        landed = [sem(f"landed{i}") for i in range(RING)]
        used = [sem(f"used{i}") for i in range(RING)]
        params_in, x_in, router_in = sem("params_in"), sem("x_in"), sem("router_in")
        out_written, consts_done = sem("out_written"), sem("consts_done")
        cols_ready, cols_ps, cols_done, silu_c_done, c32_done, gg_done = (
            sem("cols_ready"), sem("cols_ps"), sem("cols_done"), sem("silu_c_done"), sem("c32_done"), sem("gg_done"))
        dve_step = sem("dve_step")
        pool_step = sem("pool_step")
        part_out, mod_ps, mod_out, mod_done = sem("part_out"), sem("mod_ps"), sem("mod_out"), sem("mod_done")
        ss_done, rs_done, ry_done, xn_done, hT_ps, hT_act, hT_dve = (
            sem("ss_done"), sem("rs_done"), sem("ry_done"), sem("xn_done"), sem("hT_ps"), sem("hT_act"), sem("hT_dve"))
        x_new, ys_done, diag_done, gg_ps = sem("x_new"), sem("ys_done"), sem("diag_done"), sem("gg_ps")
        u_ps, u_done = sem("u_ps"), sem("u_done")
        turn_ready, trig1_done, frac_done = sem("turn_ready"), sem("trig1_done"), sem("frac_done")
        angle_done, table_done = sem("angle_done"), sem("table_done")
        zst_done, zt_ps, zt_done = sem("zst_done"), sem("zt_ps"), sem("zt_done")
        bu_ps, rot_done, v_done, scan_done, post_d, post_p, y5_ps, y5_done = (
            sem("bu_ps"), sem("rot_done"), sem("v_done"), sem("scan_done"), sem("post_d"), sem("post_p"),
            sem("y5_ps"), sem("y5_done"))
        gelu_done, wo_ps, sig_done, glu_done = sem("gelu_done"), sem("wo_ps"), sem("sig_done"), sem("glu_done")
        gate1_done, up1_done = sem("gate1_done"), sem("up1_done")
        silu_done, act_done, tr_done, aT_done = sem("silu_done"), sem("act_done"), sem("tr_done"), sem("aT_done")
        qk_done, v_out = sem("qk_done"), sem("v_out")
        z_ps, zabs_done, zcopy_done, exp_done, ln_done, sp_done, spm_done = (
            sem("z_ps"), sem("zabs_done"), sem("zcopy_done"), sem("exp_done"), sem("ln_done"), sem("sp_done"),
            sem("spm_done"))
        sfx_ps, arg_done, wexp_done, w_done, o_ps, o_done = (
            sem("sfx_ps"), sem("arg_done"), sem("wexp_done"), sem("w_done"), sem("o_ps"), sem("o_done"))
        lg_ps, lmax_done, pexp_done, sel_done, rank_ps, route_done = (
            sem("lg_ps"), sem("lmax_done"), sem("pexp_done"), sem("sel_done"), sem("rank_ps"), sem("route_done"))
        pick_done, onehot_done, xe_ps, xe_done, st_ps, st_done = (
            sem("pick_done"), sem("onehot_done"), sem("xe_ps"), sem("xe_done"), sem("st_ps"), sem("st_done"))
        ysb_act, ysb_dve, sc_ps, sc_done = sem("ysb_act"), sem("ysb_dve"), sem("sc_ps"), sem("sc_done")

        r_c = rows[0:KD, 0:P]
        r_lam = rows[0:NT, 128:384].rearrange("p (a n) -> p a n", a=2)
        r_ls = rows[0:NT, 384:386]
        r_lsb = rows[0:NT, 512:640].rearrange("p (a n) -> p a n", a=2)
        r_d = junk[0:NBLK, 512:640]
        r_g = tbuf[0:8, :]
        r_b = junk[0:24, 0:512]
        part = rows[:, 0:512]
        C_C, C_LRE, C_LIM, C_LS, C_D, C_G = 0, 8, 24, 40, 56, 60
        (STEP, XM, THETA, KTURN, TURN, COST, SIN1, COS1, MAG, LBR, LBI, CRE, CIM, DEN, FHI, FLO,
         T0, T1, T2, T3, T4) = range(21)
        MODS_OF = ((0, 0), (0, 6), (1, 0), (1, 6))

        def pcol(i):
            return par[:, i, :]

        def shift_col(s, k):
            layer, r = MODS_OF[s]
            return modc[:, layer, r + k // 4, k % 4:k % 4 + 1]

        def mods(s, which):
            layer, r = MODS_OF[s]
            return modc[:, layer, r + 2 * which:r + 2 * which + 2, :].rearrange("p a b -> p (a b)")

        def g_cols(s, post):
            return cols[:, C_G:C_G + 64].rearrange("p (k r) -> p k r", r=8)[:, :, 2 * s + post]

        def gran(n):
            return ring[:, n % RING, :]

        def gran8(n):
            return gran(n).rearrange("p (k n) -> p k n", k=KD)

        def gran4(n):
            return gran(n).rearrange("p (k n) -> p k n", k=4)

        def wait_landed(eng, n, turn=None):
            eng.wait_ge(landed[n % RING], 16 * (n // RING if turn is None else turn) + 16)

        def wait_used(eng, n, turn=None):
            eng.wait_ge(used[n % RING], (n // RING if turn is None else turn) + 1)

        def above(eng, s, value):
            if not isinstance(value, int) or value > 0:
                eng.wait_ge(s, value)

        def expert_counts(eng, e):
            nch = eng.value_load(cnt_i[0:1, 0, bass.ds(e, 1)], min_val=1, max_val=2)
            more = eng.value_load(cnt_i[0:1, 3, bass.ds(e, 1)], min_val=0, max_val=1)
            items2 = eng.value_load(cnt_i[0:1, 1, bass.ds(e, 1)], min_val=2 * FB - 2, max_val=2 * FB * (NE + 1))
            before1 = eng.value_load(cnt_i[0:1, 2, bass.ds(e, 1)], min_val=FB, max_val=FB * (NE + 1))
            wide0 = eng.value_load(cnt_i[0:1, 4, bass.ds(e, 1)], min_val=0, max_val=2)
            narrow1 = eng.value_load(cnt_i[0:1, 5, bass.ds(e, 1)], min_val=0, max_val=1)

            def by_width(run, two):
                if two:
                    with eng.If(nch > 1):
                        with eng.If(narrow1 > 0):
                            run(1, 32)
                        with eng.Else():
                            run(1, P)
                with eng.If(wide0 > 1):
                    run(0, P)
                with eng.Else():
                    with eng.If(wide0 > 0):
                        run(0, 64)
                    with eng.Else():
                        run(0, 32)

            return nch, more, items2, before1, narrow1, wide0, by_width

        block = ctx.enter_context(nc.Block())

        @block.sync
        def _(sp):
            def load(n, dst, src, turn=None):
                turn = n // RING if turn is None else turn
                above(sp, used[n % RING], turn)
                sp.dma_start(dst, src).then_inc(landed[n % RING], 16)

            def cols512(w, at):
                return w[:, at:at + 512].rearrange("(k p) n -> p k n", p=P)

            def load_ada(layer, r):
                n = ada_place(layer, r)
                load(n, gran8(n), cols512(ada_w[layer], 512 * r))

            sp.wait_ge(params_in, 16 * 13)
            for r in range(4):
                load_ada(0, r)
            load(N_WIN, gran8(N_WIN), cols512(s5_w_in[0], 0))
            for r in range(4, MODS):
                load_ada(0, r)
            for r in range(MODS):
                load_ada(1, r)
            for h in range(2):
                load(N_WOUT + h, gran4(N_WOUT + h),
                     s5_w_out[0][:, D * h:D * h + D].rearrange("(k p) n -> p k n", p=P))

            def swiglu_weights(w_gu, w_dn, base, turn):
                def down(f):
                    g = down_at(f)
                    load(base + g, gran4(base + g),
                         w_dn[512 * f:512 * f + 512, :].rearrange("(k p) n -> p k n", p=P), turn(g))
                for f in range(FB):
                    for g, at in ((gate_at(f), 512 * f), (up_at(f), FF + 512 * f)):
                        load(base + g, gran8(base + g), cols512(w_gu, at), turn(g))
                    if f:
                        down(f - 1)
                down(FB - 1)

            swiglu_weights(ffn_w_gate_up[0], ffn_w_down[0], N_FFN, lambda g: (N_FFN + g) // RING)
            for r in range(6):
                load(N_QKV + r, gran8(N_QKV + r), cols512(sb_w_qkv[0], 512 * r))
            for r in range(2):
                load(N_SBOUT + r, gran8(N_SBOUT + r), cols512(sb_w_out[0], 512 * r))
            with sp.Fori(0, NE) as e:
                gu = moe_w_gate_up[0].rearrange("e a b -> (e a) b")[bass.ds(e * D, D), :]
                dn = moe_w_down[0].rearrange("e a b -> (e a) b")[bass.ds(e * FF, FF), :]
                swiglu_weights(gu, dn, N_MOE, lambda g: e * (PER_EXPERT // RING) + (N_MOE + g) // RING)
            sp.wait_ge(x_new, 8)
            sp.dma_start(out[0].rearrange("(t p) d -> p t d", p=P), x_sb[:, :, :]).then_inc(out_written, 16)
            sp.wait_ge(out_written, 16)

        @block.gpsimd
        def _(pool):
            count = [0]

            def link(ins):
                count[0] += 1
                ins.then_inc(pool_step, 1)
                pool.wait_ge(pool_step, count[0])

            link(pool.memset(ones[:, :], 1.0))
            pool.affine_select(out=ident[:, :], in_=ones[:, :], compare_op=ALU.is_equal, fill=0.0, base=0,
                               pattern=[[-1, P]], channel_multiplier=1).then_inc(consts_done, 1)
            pool.affine_select(out=incl[:, :], in_=ones[:, :], compare_op=ALU.is_ge, fill=0.0, base=0,
                               pattern=[[-1, P]], channel_multiplier=1).then_inc(consts_done, 1)
            pool.affine_select(out=strict[:, :], in_=ones[:, :], compare_op=ALU.is_gt, fill=0.0, base=0,
                               pattern=[[1, P]], channel_multiplier=-1).then_inc(consts_done, 1)
            link(pool.affine_select(out=chmask[:, :], in_=ones[:, 0:8], compare_op=ALU.is_ge, fill=0.0, base=0,
                                    pattern=[[-HG, 8]], channel_multiplier=1))
            pool.affine_select(out=chmask[:, :], in_=chmask[:, :], compare_op=ALU.is_ge, fill=0.0, base=HG - 1,
                               pattern=[[HG, 8]], channel_multiplier=-1).then_inc(consts_done, 1)
            pool.iota(steps[:, :], [[1, SEQ]], base=0, channel_multiplier=0,
                      allow_small_or_imprecise_dtypes=True).then_inc(consts_done, 1)
            pool.memset(inv32[:, :], 1.0 / 32).then_inc(consts_done, 1)
            link(pool.memset(half[:, :], -0.5))
            pool.wait_ge(consts_done, 6)

            def add_rotated(b):
                pool.wait_ge(rot_done, 4 * b + 2)
                pool.tensor_tensor(v_re, prod[:, 0], prod[:, 1], ALU.add).then_inc(v_done, 1)
                pool.wait_ge(rot_done, 4 * b + 4)
                pool.tensor_tensor(v_im, prod2[:, 0], prod2[:, 1], ALU.subtract).then_inc(v_done, 1)

            def unrotate(b):
                q = b % 2
                pool.wait_ge(v_done, 2 * b + 2)
                pool.wait_ge(scan_done, 2 * TPB * (b + 1))
                pool.tensor_tensor(prod2[:, 0], v_re, sinT[:, q], ALU.mult).then_inc(post_p, 1)
                pool.tensor_tensor(prod2[:, 1], v_im, cosT[:, q], ALU.mult).then_inc(post_p, 1)
                pool.wait_ge(post_p, 2 * b + 2)

            def inverse_norm(s, ready, done, src, dst):
                for tt in range(TT):
                    pool.wait_ge(ready, 2 * s + tt + 1)
                    a, b = stat[:, src + tt:src + tt + 1], stat[:, dst + tt:dst + tt + 1]
                    link(pool.tensor_scalar(b, a, D * EPS, None, ALU.add))
                    pool.tensor_tensor(b, b, half[:, :], ALU.pow).then_inc(done, 1)

            def mod_bias(layer, lo, hi, subs):
                pool.wait_ge(mod_out, MODS * layer + hi)
                m = modc[:, layer, lo:hi, :]
                link(pool.tensor_tensor(m, m, adab[:, :, MODS * layer + lo:MODS * layer + hi].rearrange("p j r -> p r j"),
                                        ALU.add))
                for s in subs:
                    link(pool.tensor_scalar(scale_c[:, s, :], mods(s, 1), 1.0, None, ALU.add))
                    pool.tensor_tensor(scale_c[:, s, :], scale_c[:, s, :], g_cols(s, 0), ALU.mult).then_inc(mod_done, 1)

            inverse_norm(0, ss_done, rs_done, 0, 8)
            mod_bias(0, 0, 4, (0,))
            for b in range(NBLK):
                add_rotated(b)
                unrotate(b)
                if b == 2:
                    mod_bias(0, 4, MODS, (1,))
            mod_bias(1, 0, MODS, (2, 3))
            for s in range(4):
                if s:
                    inverse_norm(s, ss_done, rs_done, 0, 8)
                inverse_norm(s, ys_done, ry_done, 4, 12)

        @block.scalar
        def _(act):
            act.dma_start(r_c, c.rearrange("a (k n) -> (a k) n", n=P)).then_inc(params_in, 16)
            act.dma_start(r_lam[:, 0, :], s5_lambda_re[0].rearrange("(t g) n -> t (g n)", g=2)).then_inc(params_in, 16)
            act.dma_start(r_lam[:, 1, :], s5_lambda_im[0].rearrange("(t g) n -> t (g n)", g=2)).then_inc(params_in, 16)
            act.dma_start(r_ls, s5_log_step[0].rearrange("(t g) -> t g", g=2)).then_inc(params_in, 16)
            act.dma_start(r_d, s5_d[0].rearrange("(b g) h -> b (g h)", b=NBLK)).then_inc(params_in, 16)
            act.dma_start(r_g, norm_g.rearrange("a b n -> (a b) n")).then_inc(params_in, 16)
            act.dma_start(r_b, ada_b.rearrange("l (r n) -> (l r) n", n=512)).then_inc(params_in, 16)
            act.dma_start(x_sb[:, :, :], x[0].rearrange("(t p) d -> p t d", p=P)).then_inc(x_in, 16)
            for i, w in enumerate((s5_b_re, s5_b_im)):
                for g in range(2):
                    act.dma_start(b_raw[NS * g:NS * g + NS, i], w[0].rearrange("(t g) n h -> g n t h", g=2)[g]
                                  ).then_inc(params_in, 16)
            for i, w in enumerate((s5_c_re, s5_c_im)):
                act.dma_start(c_raw[:, i], w[0].rearrange("(b g) h n -> (g h) b n", b=NBLK)).then_inc(params_in, 16)
            act.dma_start(wr_sb[:, :, :], moe_w_router[0].rearrange("(k p) n -> p k n", p=P)).then_inc(router_in, 16)
            act.dma_start(br_sb[:, :], moe_b_router).then_inc(router_in, 16)

            def pre_stats(s):
                for tt in range(TT):
                    if s == 0:
                        act.wait_ge(x_in, 16)
                    else:
                        act.wait_ge(x_new, 2 * (s - 1) + tt + 1)
                    act.activation(hn[:, tt, :], x_sb[:, tt, :], ACT.Square,
                                   accum_out=stat[:, tt:tt + 1]).then_inc(ss_done, 1)

            def hT_evict(s):
                act.wait_ge(mod_done, s + 1)
                for k in (0, 1, 4, 5):
                    act.wait_ge(hT_ps, 4 * s + k // 2 + 1)
                    act.activation(hT[:, k, :], ps[:, Y_BANK + k // 2, 256 * (k % 2):256 * (k % 2) + 256],
                                   ACT.Identity, bias=shift_col(s, k), scale=scale_c[:, s, k:k + 1]
                                   ).then_inc(hT_act, 1)

            def y_stats(s, source):
                for tt in range(TT):
                    if s or tt:
                        act.wait_ge(ys_done, 2 * s + tt)
                    act.activation(junk[:, :], source(tt), ACT.Square,
                                   accum_out=stat[:, 4 + tt:5 + tt]).then_inc(ys_done, 1)

            def y_banks(tt):
                return ps[:, Y_BANK + 2 * tt:Y_BANK + 2 * tt + 2, :].rearrange("p a b -> p (a b)")

            def ada_parts(lo, hi):
                for i in range(lo, hi):
                    wait_used(act, ada_place(*divmod(i, MODS)))
                    act.activation(part, ps[:, 0, :], ACT.Copy).then_inc(part_out, 1)
                    act.wait_ge(mod_ps, i + 1)
                    act.activation(modc[:, i // MODS, i % MODS, :], ps[:, 1, 0:4], ACT.Copy).then_inc(mod_out, 1)

            def trig(b):
                q = b % 2
                act.wait_ge(angle_done, 2 * b + 2)
                act.activation(sinT[:, q], sinT[:, q], ACT.Sin, scale=SIN_SCALE).then_inc(table_done, 1)
                act.activation(cosT[:, q], cosT[:, q], ACT.Sin, scale=SIN_SCALE).then_inc(table_done, 1)

            def gate_out(f, q, ch, base, turn, c1, width=P, prev=None):
                n = base + gate_at(f)
                if ch:
                    act.wait_ge(gate1_done, c1 + f + 1)
                else:
                    wait_used(act, n, turn(gate_at(f)))
                if width < P:
                    if f:
                        act.wait_ge(tr_done, prev + 1)
                    act.activation(g_part[:, ch, :], ps[:, G_BANK, :], ACT.Copy).then_inc(silu_done, 1)
                    return
                above(act, act_done, q)
                act.activation(sg, ps[:, G_BANK, :], ACT.Silu).then_inc(silu_done, 1)

            def aT_out(q, ch, width=P):
                act.wait_ge(tr_done, q + 1)
                if width < P:
                    src = ps[:, T_BANK, :].rearrange("p (k n) -> p k n", k=4)[:, :, 0:width]
                    act.activation(silu_T[:, :, 0:width], src, ACT.Silu).then_inc(aT_done, 1)
                else:
                    act.activation(aT[:, ch].rearrange("p k n -> p (k n)"), ps[:, T_BANK, :], ACT.Copy
                                   ).then_inc(aT_done, 2)

            pre_stats(0)
            act.wait_ge(cols_done, 1)
            act.activation(cols[:, 0:KD], cols[:, 0:KD], ACT.Silu).then_inc(silu_c_done, 1)
            act.wait_ge(turn_ready, 1)
            act.activation(pcol(SIN1), pcol(TURN), ACT.Sin, scale=SIN_SCALE).then_inc(trig1_done, 1)
            act.activation(pcol(COS1), pcol(COST), ACT.Sin, scale=SIN_SCALE).then_inc(trig1_done, 1)
            ada_parts(0, 4)
            hT_evict(0)
            for i in range(2):
                if i:
                    wait_used(act, N_WIN)
                else:
                    act.wait_ge(u_ps, 1)
                act.activation(uT[:, 2 * i:2 * i + 2, :].rearrange("p a b -> p (a b)"), ps[:, i, :], ACT.Copy
                               ).then_inc(u_done, 1)
            trig(0)
            trig(1)

            def turned_out(b, i):
                zt = ps[:, T_BANK, :].rearrange("p (t n) -> p t n", t=TPB)
                act.wait_ge(zt_ps, 4 * b + i + 1)
                act.activation((bT[:, 0], bT[:, 1], cT[:, 0], cT[:, 2])[i], zt, ACT.Copy, scale=-1.0 if i == 3 else 1.0
                               ).then_inc(zt_done, 1)
                if i == 2:
                    act.activation(cT[:, 1], zt, ACT.Copy, scale=-1.0).then_inc(zt_done, 1)

            for i in range(4):
                turned_out(0, i)
            for b in range(NBLK):
                ada_parts(4 + 5 * b, 6 + 5 * b)
                if b + 1 < NBLK:
                    turned_out(b + 1, 0)
                    turned_out(b + 1, 1)
                ada_parts(6 + 5 * b, 7 + 5 * b)
                if b + 1 < NBLK:
                    turned_out(b + 1, 2)
                    turned_out(b + 1, 3)
                ada_parts(7 + 5 * b, 9 + 5 * b)
                if b + 2 < NBLK:
                    trig(b + 2)
            for b in range(NBLK):
                act.wait_ge(y5_done, b + 1)
                act.activation(uT[:, b, :], uT[:, b, :], ACT.Gelu_apprx_tanh).then_inc(gelu_done, 1)
            for i in range(4):
                if i < 3:
                    act.wait_ge(wo_ps, i + 1)
                else:
                    wait_used(act, N_WOUT + 1)
                if i >= 2:
                    act.wait_ge(glu_done, i - 1)
                act.activation(junk[:, 512 * (i % 2):512 * (i % 2) + 512], ps[:, 2 * i + 1, :],
                               ACT.Sigmoid).then_inc(sig_done, 1)
            act.wait_ge(glu_done, 4)
            y_stats(0, lambda tt: hn[:, tt, :])
            pre_stats(1)
            hT_evict(1)
            ffn_turn = lambda g: (N_FFN + g) // RING
            for f in range(FB):
                for ch, q in ((1, 2 * f), (0, 2 * f + 1)):
                    gate_out(f, q, ch, N_FFN, ffn_turn, 0)
                    if f:
                        aT_out(q - 2, ch)
            aT_out(2 * FB - 2, 1)
            aT_out(2 * FB - 1, 0)
            wait_used(act, N_FFN + PER_EXPERT - 1)
            y_stats(1, y_banks)
            pre_stats(2)
            hT_evict(2)
            for r in range(4):
                wait_used(act, N_QKV + r)
                src = ps[:, 2 * (r % 2):2 * (r % 2) + 2, :].rearrange("p a (b n) -> p (a b) n", b=2)
                act.activation((qT if r < 2 else kT)[:, 4 * (r % 2):4 * (r % 2) + 4, :], src, ACT.Copy,
                               scale=DH ** -0.5 if r < 2 else 1.0).then_inc(qk_done, 1)
            def o_out(h):
                act.wait_ge(o_ps, h + 1)
                act.activation(oT[:, h, :], ps[:, 6 + h % 2, 0:256], ACT.Copy).then_inc(o_done, 1)

            for h in range(HEADS // 2 + 1):
                b = h % 2
                if h < HEADS // 2:
                    act.wait_ge(z_ps, h + 1)
                    if h >= 3:
                        act.wait_ge(o_ps, h - 2)
                    act.activation(z_w[:, h % 3], ps[:, 2 * b:2 * b + 2, 0:384], ACT.Copy).then_inc(zcopy_done, 1)
                    act.wait_ge(zabs_done, h + 1)
                    act.activation(z_e[:, b], z_e[:, b], ACT.Exp).then_inc(exp_done, 1)
                    act.wait_ge(exp_done, h + 1)
                    act.activation(z_e[:, b], z_e[:, b], ACT.Ln, bias=1.0).then_inc(ln_done, 1)
                if h:
                    act.wait_ge(arg_done, h)
                    act.activation(z_w[:, (h - 1) % 3], z_w[:, (h - 1) % 3], ACT.Exp).then_inc(wexp_done, 1)
                if h >= 2:
                    o_out(h - 2)
            o_out(HEADS // 2 - 1)
            wait_used(act, N_SBOUT + 1)
            y_stats(2, y_banks)
            pre_stats(3)
            hT_evict(3)
            for tt in range(TT):
                act.wait_ge(lmax_done, tt + 1)
                act.activation(rt[:, tt, 8:16], rt[:, tt, 0:8], ACT.Exp, bias=rt[:, tt, 80:81],
                               accum_out=rt[:, tt, 81:82]).then_inc(pexp_done, 1)
            act.wait_ge(route_done, 1)
            with act.Fori(0, NE) as e:
                nch, more, items2, c1, _, _, by_width = expert_counts(act, e)
                moe_turn = lambda g: e * (PER_EXPERT // RING) + (N_MOE + g) // RING

                def xe_out(ch):
                    for k in range(KD):
                        bank = (G_BANK, T_BANK)[ch] + k // 4
                        ins = act.activation(xe[:, k, ch, :], ps[:, bank, P * (k % 4):P * (k % 4) + P],
                                             ACT.Identity, bias=shift_col(3, k), scale=scale_c[:, 3, k:k + 1])
                    return ins

                with act.If(nch > 1):
                    act.wait_ge(xe_ps, e + 1)
                    xe_out(1)
                act.wait_ge(xe_ps, e + 1)
                xe_out(0).then_inc(xe_done, 1)
                for f in range(FB + 1):
                    q2 = items2 + f * nch

                    def item(ch, width):
                        before = q2 if ch else q2 + 1
                        if f < FB:
                            gate_out(f, q2 + 2 if ch else q2 + more + 2, ch, N_MOE, moe_turn, c1, width, before)
                        if f:
                            aT_out(before, ch, width)

                    by_width(item, True)
                with act.If(nch > 1):
                    wait_used(act, N_MOE + PER_EXPERT - 1, moe_turn(PER_EXPERT - 1))
                    act.activation(ysb[:, 1, 0:512], ps[:, Y_BANK + 2, :], ACT.Copy)
                wait_used(act, N_MOE + PER_EXPERT - 1, moe_turn(PER_EXPERT - 1))
                act.activation(ysb[:, 0, 0:512], ps[:, Y_BANK, :], ACT.Copy).then_inc(ysb_act, 1)
            act.wait_ge(sc_done, 4 * NE + 4)
            y_stats(3, lambda tt: macc[:, tt, :])

        @block.vector
        def _(dve):
            count = [0]

            def link(ins):
                count[0] += 1
                ins.then_inc(dve_step, 1)
                dve.wait_ge(dve_step, count[0])

            def stt(o, a, s, b, op0, op1):
                return dve.scalar_tensor_tensor(out=o, in0=a, scalar=s, in1=b, op0=op0, op1=op1)

            def exp_small(dst, src):
                n, r, p, bits = pcol(T0), pcol(T1), pcol(T2), pcol(T3)
                link(dve.tensor_scalar(n, src, 1.0 / math.log(2), MAGIC, ALU.mult, ALU.add))
                link(dve.tensor_scalar(n, n, MAGIC, None, ALU.subtract))
                link(dve.tensor_scalar(n, n, -126.0, None, ALU.max))
                hi = 0.693145751953125
                link(stt(r, n, -hi, src, ALU.mult, ALU.add))
                link(stt(r, n, -(math.log(2) - hi), r, ALU.mult, ALU.add))
                link(dve.tensor_scalar(p, r, 1.0 / math.factorial(7), None, ALU.mult))
                for k in range(6, 0, -1):
                    link(stt(p, p, 1.0 / math.factorial(k), r, ALU.add, ALU.mult))
                link(dve.tensor_scalar(n, n, 127.0, 8388608.0, ALU.add, ALU.mult))
                link(dve.tensor_copy(bits.bitcast(I32), n))
                link(stt(dst, p, 1.0, bits, ALU.add, ALU.mult))

            def to_hT(s):
                for tt in range(TT):
                    dve.wait_ge(rs_done, 2 * s + tt + 1)
                    dve.tensor_scalar(hn[:, tt, :], x_sb[:, tt, :], stat[:, 8 + tt:9 + tt], ROOT_D, ALU.mult, ALU.mult
                                      ).then_inc(xn_done, 1)

            def hT_evict(s):
                dve.wait_ge(mod_done, s + 1)
                for k in (2, 3, 6, 7):
                    dve.wait_ge(hT_ps, 4 * s + k // 2 + 1)
                    dve.tensor_scalar(hT[:, k, :], ps[:, Y_BANK + k // 2, 256 * (k % 2):256 * (k % 2) + 256],
                                      scale_c[:, s, k:k + 1], shift_col(s, k), ALU.mult, ALU.add
                                      ).then_inc(hT_dve, 1)

            def gate_row(s):
                if s:
                    dve.wait_ge(x_new, 2 * s)
                dve.wait_ge(mod_done, 2 if s < 2 else 4)
                link(stt(gate_c[:, s, :], mods(s, 2), ROOT_D, g_cols(s, 1), ALU.mult, ALU.mult))
                dve.tensor_tensor(tbuf[:, :].rearrange("p (k n) -> p k n", k=KD),
                                  ident[:, :].unsqueeze(1).to_broadcast([P, KD, P]),
                                  gate_c[:, s, :].unsqueeze(2).to_broadcast([P, KD, P]), ALU.mult
                                  ).then_inc(diag_done, 1)
                dve.wait_ge(gg_ps, s + 1)
                dve.tensor_copy(gg[:, :], ps[:, 2:4, :].rearrange("p a b -> p (a b)")).then_inc(gg_done, 1)
                dve.wait_ge(gg_done, s + 1)

            def residual(s, source):
                for tt in range(TT):
                    dve.wait_ge(ry_done, 2 * s + tt + 1)
                    link(stt(tbuf[:, :], source(tt), stat[:, 12 + tt:13 + tt], gg[:, :], ALU.mult, ALU.mult))
                    dve.tensor_tensor(x_sb[:, tt, :], x_sb[:, tt, :], tbuf[:, :], ALU.add).then_inc(x_new, 1)
                    dve.wait_ge(x_new, 2 * s + tt + 1)

            def y_banks(tt):
                return ps[:, Y_BANK + 2 * tt:Y_BANK + 2 * tt + 2, :].rearrange("p a b -> p (a b)")

            def swiglu_out(f, q, ch, base, turn, c1, a_free, width=P):
                if width == P:
                    dve.wait_ge(silu_done, q + 1)
                if ch:
                    dve.wait_ge(up1_done, c1 + f + 1)
                else:
                    wait_used(dve, base + up_at(f), turn(up_at(f)))
                if a_free is not None:
                    dve.wait_ge(tr_done, a_free)
                if width == P:
                    dve.tensor_tensor(a_sb[:, ch, :], sg, ps[:, U_BANK, :], ALU.mult).then_inc(act_done, 1)
                else:
                    dve.tensor_copy(a_sb[:, ch, :], ps[:, U_BANK, :]).then_inc(act_done, 1)

            def narrow_aT(q, ch, width):
                dve.wait_ge(aT_done, q * 2 + 1)
                up = ps[:, S_BANK, :].rearrange("p (k n) -> p k n", k=4)[:, :, 0:width]
                dve.tensor_tensor(aT[:, ch, :, 0:width], silu_T[:, :, 0:width], up, ALU.mult).then_inc(aT_done, 1)

            scratch = junk[:, :].rearrange("p (t s) -> p t s", t=TPB)

            def angles(b):
                q = b % 2
                if b == 0:
                    dve.wait_ge(frac_done, 1)
                if b >= 2:
                    dve.wait_ge(post_d, b - 1)
                    dve.wait_ge(post_p, 2 * b - 2)
                fh = par[:, FHI, TPB * b:TPB * b + TPB].unsqueeze(2).to_broadcast([P, TPB, SEQ])
                fl = par[:, FLO, TPB * b:TPB * b + TPB].unsqueeze(2).to_broadcast([P, TPB, SEQ])
                t = steps[:, :].unsqueeze(1).to_broadcast([P, TPB, SEQ])
                s, co = sinT[:, q], cosT[:, q]
                link(dve.tensor_tensor(s, t, fh, ALU.mult))
                link(dve.tensor_scalar(scratch, s, MAGIC, MAGIC, ALU.add, ALU.subtract))
                link(dve.tensor_tensor(s, s, scratch, ALU.subtract))
                link(dve.tensor_tensor(co, t, fl, ALU.mult))
                link(dve.tensor_tensor(s, s, co, ALU.add))
                link(dve.tensor_scalar(co, s, 0.25, None, ALU.add))
                for v in (s, co):
                    link(dve.tensor_scalar(scratch, v, MAGIC, MAGIC, ALU.add, ALU.subtract))
                    dve.tensor_tensor(v, v, scratch, ALU.subtract).then_inc(angle_done, 1)
                    dve.wait_ge(angle_done, 2 * b + (1 if v is s else 2))

            dve.wait_ge(params_in, 16 * 13)
            link(dve.tensor_copy(r_lsb, r_ls.unsqueeze(2).to_broadcast([NT, 2, NS])))
            dve.memset(zst_b[0], 0.0).then_inc(cols_ready, 1)
            link(dve.memset(zst_b[1], 0.0))
            dve.wait_ge(cols_ps, 2)
            link(dve.tensor_copy(cols[:, 0:124], ps[:, 0, 0:124]))
            dve.tensor_copy(adab[:, :, :], ps[:, 1, 0:96].rearrange("p (a b) -> p a b", a=4)).then_inc(cols_done, 1)
            dve.wait_ge(cols_done, 1)
            lre, lim, ls = (cols[:, a:a + NT] for a in (C_LRE, C_LIM, C_LS))
            exp_small(pcol(STEP), ls)
            link(dve.tensor_tensor(pcol(THETA), lim, pcol(STEP), ALU.mult))
            link(dve.tensor_scalar(pcol(KTURN), pcol(THETA), 1 / TWO_PI, MAGIC, ALU.mult, ALU.add))
            link(dve.tensor_scalar(pcol(KTURN), pcol(KTURN), MAGIC, None, ALU.subtract))
            p1 = 6.28125
            p2 = 0.0019350051879882812
            p3 = TWO_PI - p1 - p2
            for p in (p1, p2, p3):
                link(stt(pcol(THETA), pcol(KTURN), -p, pcol(THETA), ALU.mult, ALU.add))
            link(dve.tensor_scalar(pcol(TURN), pcol(THETA), 1 / TWO_PI, None, ALU.mult))
            link(dve.tensor_scalar(pcol(COST), pcol(TURN), 0.25, None, ALU.add))
            link(dve.tensor_scalar(pcol(T0), pcol(COST), MAGIC, MAGIC, ALU.add, ALU.subtract))
            dve.tensor_tensor(pcol(COST), pcol(COST), pcol(T0), ALU.subtract).then_inc(turn_ready, 1)
            dve.wait_ge(turn_ready, 1)
            link(dve.tensor_scalar(pcol(FHI), pcol(TURN), 768.0, 768.0, ALU.add, ALU.subtract))
            dve.tensor_tensor(pcol(FLO), pcol(TURN), pcol(FHI), ALU.subtract).then_inc(frac_done, 1)
            dve.wait_ge(silu_c_done, 1)
            dve.tensor_copy(c32[:, :, :], cols[:, 0:KD].unsqueeze(2).to_broadcast([P, KD, 32])).then_inc(c32_done, 1)
            link(dve.tensor_tensor(pcol(XM), lre, pcol(STEP), ALU.mult))
            exp_small(pcol(MAG), pcol(XM))
            dve.wait_ge(trig1_done, 2)
            link(dve.tensor_tensor(pcol(LBR), pcol(MAG), pcol(COS1), ALU.mult))
            link(dve.tensor_tensor(pcol(LBI), pcol(MAG), pcol(SIN1), ALU.mult))
            link(dve.tensor_tensor(pcol(DEN), lre, lre, ALU.mult))
            link(dve.tensor_tensor(pcol(T0), lim, lim, ALU.mult))
            link(dve.tensor_tensor(pcol(DEN), pcol(DEN), pcol(T0), ALU.add))
            link(dve.reciprocal(pcol(DEN), pcol(DEN)))
            link(dve.tensor_scalar(pcol(T0), pcol(LBR), 1.0, None, ALU.subtract))
            link(dve.tensor_tensor(pcol(T1), pcol(T0), lre, ALU.mult))
            link(dve.tensor_tensor(pcol(T2), pcol(LBI), lim, ALU.mult))
            link(dve.tensor_tensor(pcol(T1), pcol(T1), pcol(T2), ALU.add))
            link(dve.tensor_tensor(pcol(CRE), pcol(T1), pcol(DEN), ALU.mult))
            link(dve.tensor_tensor(pcol(T1), pcol(LBI), lre, ALU.mult))
            link(dve.tensor_tensor(pcol(T2), pcol(T0), lim, ALU.mult))
            link(dve.tensor_tensor(pcol(T1), pcol(T1), pcol(T2), ALU.subtract))
            link(dve.tensor_tensor(pcol(CIM), pcol(T1), pcol(DEN), ALU.mult))
            cre = pcol(CRE).unsqueeze(2).to_broadcast([P, NT, HG])
            cim = pcol(CIM).unsqueeze(2).to_broadcast([P, NT, HG])
            btmp = zst_c[0][:, 0:NT * HG].rearrange("p (t h) -> p t h", t=NT)
            link(dve.tensor_tensor(bb[:, 0], cre, b_raw[:, 0], ALU.mult))
            link(dve.tensor_tensor(btmp, cim, b_raw[:, 1], ALU.mult))
            link(dve.tensor_tensor(bb[:, 0], bb[:, 0], btmp, ALU.subtract))
            link(dve.tensor_tensor(bb[:, 1], cre, b_raw[:, 1], ALU.mult))
            link(dve.tensor_tensor(btmp, cim, b_raw[:, 0], ALU.mult))
            link(dve.tensor_tensor(bb[:, 1], bb[:, 1], btmp, ALU.add))
            to_hT(0)
            angles(0)
            angles(1)

            def stage_b(b):
                if b:
                    dve.wait_ge(zt_ps, 4 * b - 2)
                for i in range(2):
                    diag = zst_b[i].rearrange("p (t n) -> p t n", n=P + 2 * HG)
                    link(dve.tensor_copy(diag[0:NS, :, 0:HG], bb[0:NS, i, TPB * b:TPB * b + TPB, :]))
                    dve.tensor_copy(diag[NS:P, :, HG:2 * HG], bb[NS:P, i, TPB * b:TPB * b + TPB, :]
                                    ).then_inc(zst_done, 1)

            def stage_c(b):
                if b:
                    dve.wait_ge(zt_ps, 4 * b)
                for i in range(2):
                    dve.tensor_tensor(zst_c[i].rearrange("p (j n) -> p j n", j=8),
                                      c_raw[:, i, b, :].unsqueeze(1).to_broadcast([P, 8, NS]),
                                      chmask[:, :].unsqueeze(2).to_broadcast([P, 8, NS]), ALU.mult
                                      ).then_inc(zst_done, 1)
                dve.wait_ge(zst_done, 4 * b + 4)

            stage_b(0)
            stage_c(0)
            hT_evict(0)

            def bu(i):
                return ps[:, 4 + 2 * i:6 + 2 * i, :].rearrange("p a (t s) -> p (a t) s", t=2)

            for b in range(NBLK):
                q = b % 2
                dve.wait_ge(table_done, 2 * b + 2)
                dve.wait_ge(bu_ps, b + 1)
                if b:
                    dve.wait_ge(y5_ps, b)
                dve.tensor_tensor(prod[:, 0], bu(0), cosT[:, q], ALU.mult).then_inc(rot_done, 1)
                dve.tensor_tensor(prod[:, 1], bu(1), sinT[:, q], ALU.mult).then_inc(rot_done, 1)
                dve.tensor_tensor(prod2[:, 0], bu(1), cosT[:, q], ALU.mult).then_inc(rot_done, 1)
                dve.tensor_tensor(prod2[:, 1], bu(0), sinT[:, q], ALU.mult).then_inc(rot_done, 1)
                if b + 1 < NBLK:
                    stage_b(b + 1)
                for i, v in enumerate((v_re, v_im)):
                    dve.wait_ge(v_done, 2 * b + i + 1)
                    for t in range(TPB):
                        mag = par[:, MAG, TPB * b + t:TPB * b + t + 1].to_broadcast([P, SEQ])
                        dve.tensor_tensor_scan(v[:, t, :], mag, v[:, t, :], 0.0, ALU.mult, ALU.add
                                               ).then_inc(scan_done, 1)
                dve.wait_ge(scan_done, 2 * TPB * (b + 1))
                dve.tensor_tensor(prod[:, 0], v_re, cosT[:, q], ALU.mult).then_inc(dve_step, 1)
                dve.tensor_tensor(prod[:, 1], v_im, sinT[:, q], ALU.mult).then_inc(post_d, 1)
                count[0] += 1
                if b + 1 < NBLK:
                    stage_c(b + 1)
                if b + 2 < NBLK:
                    angles(b + 2)
                dve.wait_ge(y5_ps, b + 1)
                stt(uT[:, b, :], uT[:, b, :], cols[:, C_D + b:C_D + b + 1], ps[:, 3, 0:256], ALU.mult, ALU.add
                    ).then_inc(y5_done, 1)
            gate_row(0)
            for i in range(4):
                tt, n = divmod(i, 2)
                dve.wait_ge(sig_done, i + 1)
                dve.tensor_tensor(hn[:, tt, 512 * n:512 * n + 512], ps[:, 2 * i, :],
                                  junk[:, 512 * (i % 2):512 * (i % 2) + 512], ALU.mult).then_inc(glu_done, 1)
            dve.wait_ge(glu_done, 4)
            residual(0, lambda tt: hn[:, tt, :])
            to_hT(1)
            hT_evict(1)
            ffn_turn = lambda g: (N_FFN + g) // RING
            for f in range(FB):
                for ch, q in ((1, 2 * f), (0, 2 * f + 1)):
                    swiglu_out(f, q, ch, N_FFN, ffn_turn, 0, q - 1 if f else None)
            gate_row(1)
            residual(1, y_banks)
            to_hT(2)
            hT_evict(2)
            for n in range(2):
                wait_used(dve, N_QKV + 4 + n)
                for tt in range(TT):
                    dve.tensor_copy(v_sb[:, tt, 512 * n:512 * n + 512], ps[:, Y_BANK + 2 * tt + n, :]
                                    ).then_inc(v_out, 1)

            def on_diagonal(z):
                return z.rearrange("p g (b n) -> p g b n", b=3)[:, :, 0:3:2, :]

            mask = strict[:, :].unsqueeze(1).unsqueeze(1).to_broadcast([P, 2, 2, P])

            def minus_abs(h):
                z = z_w[:, h % 3]
                dve.wait_ge(zcopy_done, h + 1)
                if h >= 2:
                    dve.wait_ge(sp_done, h - 1)
                stt(z_e[:, h % 2], z, -1.0, z, ALU.mult, ALU.min).then_inc(zabs_done, 1)

            minus_abs(0)
            for h in range(HEADS // 2 + 1):
                if h < HEADS // 2:
                    b = h % 2
                    z = z_w[:, h % 3]
                    dve.wait_ge(ln_done, h + 1)
                    if h >= 2:
                        dve.wait_ge(sfx_ps, h - 1)
                    stt(z_p[:, b], z, 0.0, z_e[:, b], ALU.max, ALU.add).then_inc(sp_done, 1)
                    dve.wait_ge(sp_done, h + 1)
                    dve.tensor_tensor(on_diagonal(z_p[:, b]), on_diagonal(z_p[:, b]), mask, ALU.mult
                                      ).then_inc(spm_done, 1)
                if h + 1 < HEADS // 2:
                    minus_abs(h + 1)
                if h:
                    dve.wait_ge(wexp_done, h)
                    for g in range(2):
                        w = on_diagonal(z_w[:, (h - 1) % 3])[:, g]
                        stt(w, w, 1.0, mask[:, g], ALU.min, ALU.mult).then_inc(w_done, 1)
                if h < HEADS // 2:
                    dve.wait_ge(sfx_ps, h + 1)
                    z = z_w[:, h % 3]
                    stt(z, ps[:, 4:6, 0:384], -1.0, z, ALU.mult, ALU.add).then_inc(arg_done, 1)
            gate_row(2)
            residual(2, y_banks)
            to_hT(3)
            hT_evict(3)
            dve.memset(macc, 0.0).then_inc(sc_done, 4)
            for i, w in enumerate((32, 64)):
                link(dve.tensor_reduce(fold[:, i, 0:w], ident[:, :].rearrange("p (g s) -> p s g", s=w), AX.X, ALU.add))
                dst = fold[:, i, :].rearrange("p (g s) -> p g s", s=w)
                link(dve.tensor_copy(dst[:, 1:, :], fold[:, i, 0:w].unsqueeze(1).to_broadcast([P, P // w - 1, w])))
                link(dve.tensor_copy(slots[:, i, :].rearrange("p (g s) -> p g s", s=w),
                                     steps[:, 0:w].unsqueeze(1).to_broadcast([P, SEQ // w, w])))
            link(dve.tensor_copy(slots[:, 2, 0:P], steps[:, 0:P]))
            link(dve.tensor_copy(slots[:, 2, P:].rearrange("p (g s) -> p g s", s=32),
                                 steps[:, P:P + 32].unsqueeze(1).to_broadcast([P, 4, 32])))
            for tt in range(TT):
                r = rt[:, tt]
                dve.wait_ge(lg_ps, 1)
                link(dve.tensor_copy(r[:, 0:8], ps[:, S_BANK, 8 * tt:8 * tt + 8]))
                link(dve.tensor_reduce(r[:, 82:83], r[:, 0:8], AX.X, ALU.max))
                dve.tensor_scalar(r[:, 80:81], r[:, 82:83], -1.0, None, ALU.mult).then_inc(lmax_done, 1)
            for tt in range(TT):
                r = rt[:, tt]
                dve.wait_ge(pexp_done, tt + 1)
                link(dve.reciprocal(r[:, 81:82], r[:, 81:82]))
                link(dve.tensor_scalar(r[:, 8:16], r[:, 8:16], r[:, 81:82], None, ALU.mult))
                link(dve.max(r[:, 16:24], r[:, 8:16]))
                link(dve.max_index(r[:, 24:32].bitcast(U32), r[:, 16:24], r[:, 8:16]))
                link(dve.tensor_tensor(r[:, 84:85], r[:, 16:17], r[:, 17:18], ALU.add))
                link(dve.reciprocal(r[:, 84:85], r[:, 84:85]))
                link(dve.tensor_scalar(r[:, 82:84], r[:, 16:18], r[:, 84:85], None, ALU.mult))
                link(dve.tensor_copy(r[:, 86:88], r[:, 24:26].bitcast(U32)))
                for j in range(2):
                    link(dve.tensor_scalar(r[:, 32 + 8 * j:40 + 8 * j], steps[:, 0:8], r[:, 86 + j:87 + j], None,
                                           ALU.is_equal))
                link(dve.tensor_tensor(r[:, 48:56], r[:, 32:40], r[:, 40:48], ALU.add))
                link(dve.tensor_scalar(r[:, 32:40], r[:, 32:40], r[:, 82:83], None, ALU.mult))
                stt(rcol[:, :, 2 + tt], r[:, 40:48], r[:, 83:84], r[:, 32:40], ALU.mult, ALU.add).then_inc(sel_done, 1)
            dve.wait_ge(rank_ps, 1)
            for tt in range(TT):
                r = rt[:, tt]
                link(stt(r[:, 56:64], ps[:, S_BANK, 16 + 8 * tt:24 + 8 * tt], 1.0, r[:, 48:56], ALU.add, ALU.mult))
                link(dve.tensor_scalar(rcol[:, :, tt], r[:, 56:64], 1.0, None, ALU.subtract))
            one = cnt[0:1, 3, :]
            link(dve.memset(one, 1.0))
            total = ps[0:1, S_BANK, 32:40]
            link(dve.tensor_scalar(cnt[0:1, 4, :], total, 32.5, None, ALU.is_gt))
            link(dve.tensor_scalar(cnt[0:1, 5, :], total, 64.5, None, ALU.is_gt))
            link(dve.tensor_tensor(cnt[0:1, 4, :], cnt[0:1, 4, :], cnt[0:1, 5, :], ALU.add))
            link(dve.tensor_scalar(cnt[0:1, 5, :], total, P + 32.5, None, ALU.is_lt))
            link(dve.tensor_scalar(cnt[0:1, 1, :], ps[0:1, S_BANK, 32:40], float(P) + 0.5, None, ALU.is_gt))
            link(dve.tensor_scalar(cnt[0:1, 0, :], cnt[0:1, 1, :], 1.0, None, ALU.add))
            link(dve.tensor_tensor_scan(cnt[0:1, 2, :], one, cnt[0:1, 1, :], 0.0, ALU.mult, ALU.add))
            link(dve.tensor_copy(cnt[0:1, 3, :], cnt[0:1, 1, :]))
            link(dve.tensor_tensor(cnt[0:1, 2, :], cnt[0:1, 2, :], cnt[0:1, 1, :], ALU.subtract))
            link(dve.tensor_tensor(cnt[0:1, 1, :], cnt[0:1, 2, :], steps[0:1, 0:8], ALU.add))
            link(dve.tensor_tensor(cnt[0:1, 5, :], cnt[0:1, 5, :], cnt[0:1, 3, :], ALU.mult))
            link(dve.tensor_copy(cnt_i[:, 3:6, :], cnt[0:1, 3:6, :]))
            link(dve.tensor_scalar(cnt[0:1, 1, :], cnt[0:1, 1, :], 2.0, float(FB), ALU.add, ALU.mult))
            link(dve.tensor_scalar(cnt[0:1, 1, :], cnt[0:1, 1, :], 2.0, None, ALU.subtract))
            link(dve.tensor_scalar(cnt[0:1, 2, :], cnt[0:1, 2, :], 1.0, float(FB), ALU.add, ALU.mult))
            dve.tensor_copy(cnt_i[:, 0:3, :], cnt[0:1, 0:3, :]).then_inc(route_done, 1)
            dve.wait_ge(route_done, 1)

            with dve.Fori(0, NE) as e:
                nch, more, items2, c1, narrow1, wide0, by_width = expert_counts(dve, e)
                moe_turn = lambda g: e * (PER_EXPERT // RING) + (N_MOE + g) // RING
                dve.tensor_copy(pick, rcol[:, bass.ds(e, 1), :]).then_inc(pick_done, 1)
                dve.wait_ge(pick_done, e + 1)
                for tt in range(TT):
                    dve.tensor_scalar(g1[:, tt], steps[:, :], pick[:, 0, tt:tt + 1], None, ALU.is_equal
                                      ).then_inc(onehot_done, 1)

                def weighted(numbers):
                    for tt in range(TT):
                        dve.tensor_scalar(gw[:, tt], numbers, pick[:, 0, tt:tt + 1], pick[:, 0, 2 + tt:3 + tt],
                                          ALU.is_equal, ALU.mult).then_inc(onehot_done, 1)

                with dve.If(wide0 > 1):
                    with dve.If(narrow1 > 0):
                        weighted(slots[:, 2])
                    with dve.Else():
                        weighted(steps[:, :])
                with dve.Else():
                    with dve.If(wide0 > 0):
                        weighted(slots[:, 1])
                    with dve.Else():
                        weighted(slots[:, 0])
                with dve.If(nch > 1):
                    dve.wait_ge(st_ps, e + 1)
                    dve.tensor_copy(scT[:, 1, :], ps[:, Y_BANK + 3, 256:512])
                dve.wait_ge(st_ps, e + 1)
                dve.tensor_copy(scT[:, 0, :], ps[:, Y_BANK + 3, 0:256]).then_inc(st_done, 1)
                for f in range(FB + 1):
                    q2 = items2 + f * nch

                    def item(ch, width):
                        before = q2 if ch else q2 + 1
                        if f and width < P:
                            narrow_aT(before, ch, width)
                        if f < FB:
                            swiglu_out(f, q2 + 2 if ch else q2 + more + 2, ch, N_MOE, moe_turn, c1,
                                       before + 1 if f else None, width)

                    by_width(item, True)
                with dve.If(nch > 1):
                    wait_used(dve, N_MOE + PER_EXPERT - 1, moe_turn(PER_EXPERT - 1))
                    dve.tensor_copy(ysb[:, 1, 512:D], ps[:, Y_BANK + 3, :])
                wait_used(dve, N_MOE + PER_EXPERT - 1, moe_turn(PER_EXPERT - 1))
                dve.tensor_copy(ysb[:, 0, 512:D], ps[:, Y_BANK + 1, :]).then_inc(ysb_dve, 1)
                for i in range(4):
                    tt, n = divmod(i, 2)
                    dve.wait_ge(sc_ps, 4 * e + i + 1)
                    m = macc[:, tt, 512 * n:512 * n + 512]
                    dve.tensor_tensor(m, m, ps[:, T_BANK + i % 2, :], ALU.add).then_inc(sc_done, 1)
                dve.wait_ge(sc_done, 4 * e + 8)
            gate_row(3)
            residual(3, lambda tt: macc[:, tt, :])

        @block.tensor
        def _(pe):
            def columns(dst, src, n):
                return pe.transpose(dst, src, ident[0:n, 0:n])

            pe.wait_ge(consts_done, 6)
            pe.wait_ge(cols_ready, 1)
            columns(ps[:, 0, C_C:C_C + KD], r_c, KD)
            columns(ps[:, 0, C_LRE:C_LRE + NT], r_lam[:, 0, :], NT)
            columns(ps[:, 0, C_LIM:C_LIM + NT], r_lam[:, 1, :], NT)
            columns(ps[:, 0, C_LS:C_LS + NT], rows[0:NT, 512:640], NT)
            columns(ps[:, 0, C_D:C_D + NBLK], r_d, NBLK)
            for k in range(KD):
                ins = columns(ps[:, 0, C_G + 8 * k:C_G + 8 * k + 8], r_g[:, P * k:P * k + P], 8)
            ins.then_inc(cols_ps, 1)
            for j in range(4):
                ins = columns(ps[:, 1, 24 * j:24 * j + 24], r_b[:, P * j:P * j + P], 24)
            ins.then_inc(cols_ps, 1)

            def ada(lo, hi):
                for i in range(lo, hi):
                    n = ada_place(*divmod(i, MODS))
                    wait_landed(pe, n)
                    above(pe, part_out, i)
                    for k in range(KD):
                        j = k % 4
                        ins = pe.matmul(ps[32 * j:32 * j + 32, 0, :], c32[:, k, :], gran8(n)[:, k, :],
                                        start=k < 4, stop=k >= 4, tile_position=(0, 32 * j))
                    ins.then_inc(used[n % RING], 1)
                    pe.wait_ge(part_out, i + 1)
                    above(pe, mod_out, i)
                    for j in range(4):
                        ins = pe.matmul(ps[:, 1, j:j + 1], part[:, P * j:P * j + P], inv32[:, :],
                                        start=True, stop=True)
                    ins.then_inc(mod_ps, 1)

            def transpose_x(s):
                pe.wait_ge(xn_done, 2 * s + 2)
                for k in range(KD):
                    for tt in range(TT):
                        ins = pe.transpose(ps[:, Y_BANK + k // 2, 256 * (k % 2) + P * tt:256 * (k % 2) + P * tt + P],
                                           hn[:, tt, P * k:P * k + P], ident[:, :])
                    if k % 2:
                        ins.then_inc(hT_ps, 1)

            def wait_hT(s):
                pe.wait_ge(hT_act, 4 * s + 4)
                pe.wait_ge(hT_dve, 4 * s + 4)

            def gate_row(s):
                pe.wait_ge(diag_done, s + 1)
                for n in range(2):
                    ins = pe.matmul(ps[:, 2 + n, :], ones[:, :], tbuf[:, 512 * n:512 * n + 512], start=True, stop=True)
                ins.then_inc(gg_ps, 1)

            def product(bank, ch, xT, weights, width):
                shares = P // width
                for k in range(KD):
                    r = width * (k % shares)
                    ins = pe.matmul(ps[r:r + width, bank, :], xT(k, ch)[:, 0:width], weights[:, k, :],
                                    start=k < shares, stop=k >= KD - shares,
                                    **({} if width == P else dict(tile_position=(0, r))))
                return ins

            def gate_product(f, q2, ch, xT, base, turn, width):
                n = base + gate_at(f)
                wait_landed(pe, n, turn(gate_at(f)))
                above(pe, silu_done, q2 + 2)
                product(G_BANK, ch, xT, gran8(n), width).then_inc(gate1_done if ch else used[n % RING], 1)

            def up_product(f, q2, ch, xT, base, turn, width):
                n = base + up_at(f)
                wait_landed(pe, n, turn(up_at(f)))
                above(pe, act_done, q2 + 2)
                product(U_BANK, ch, xT, gran8(n), width).then_inc(up1_done if ch else used[n % RING], 1)

            def turn_item(q, ch, width=P):
                pe.wait_ge(act_done, q + 1)
                above(pe, aT_done, q * 2)
                if width < P:
                    pe.wait_ge(silu_done, q + 1)
                    for bank, parts in ((T_BANK, g_part), (S_BANK, a_sb)):
                        for j in range(4):
                            ins = pe.matmul(ps[:, bank, P * j:P * j + P], parts[:, ch, P * j:P * j + P],
                                            fold[:, (32, 64).index(width), :], start=True, stop=True)
                    ins.then_inc(tr_done, 1)
                    return
                for j in range(4):
                    ins = pe.transpose(ps[:, T_BANK, P * j:P * j + P], a_sb[:, ch, P * j:P * j + P], ident[:, :])
                ins.then_inc(tr_done, 1)

            def down_product(f, q, ch, base, turn, width=P):
                n = base + down_at(f)
                wait_landed(pe, n, turn(down_at(f)))
                pe.wait_ge(aT_done, q * 2 + 2)
                shares = P // width
                for j, h in [(j, h) for j in range(4) for h in range(2)] if width == P else \
                        [(j, h) for h in range(2) for j in range(4)]:
                    r = width * (j % shares)
                    ins = pe.matmul(ps[r:r + width, Y_BANK + 2 * ch + h, :], aT[:, ch, j, 0:width],
                                    gran4(n)[:, j, 512 * h:512 * h + 512],
                                    start=f == 0 and j < shares, stop=f == FB - 1 and j >= 4 - shares,
                                    **({} if width == P else dict(tile_position=(0, r))))
                if not ch:
                    ins.then_inc(used[n % RING], 1)

            def item(f, q2, before, ch, xT, base, turn, width=P):
                if f < FB:
                    gate_product(f, q2, ch, xT, base, turn, width)
                if f:
                    turn_item(before, ch, width)
                if f < FB:
                    up_product(f, q2, ch, xT, base, turn, width)
                if f:
                    down_product(f - 1, before, ch, base, turn, width)

            pe.wait_ge(cols_done, 1)
            pe.wait_ge(c32_done, 1)
            transpose_x(0)
            ada(0, 4)
            wait_hT(0)
            wait_landed(pe, N_WIN)
            for b in range(NBLK):
                for k in range(KD):
                    ins = pe.matmul(ps[:, b // 2, 256 * (b % 2):256 * (b % 2) + 256],
                                    gran8(N_WIN)[:, k, P * b:P * b + P], hT[:, k, :], start=k == 0, stop=k == KD - 1)
                if b == 1:
                    ins.then_inc(u_ps, 1)
                    pe.wait_ge(mod_out, 4)
                elif b == 3:
                    ins.then_inc(used[N_WIN % RING], 1)

            def turn_staged(b, parts):
                for i in parts:
                    pe.wait_ge(zst_done, 4 * b + i + 1)
                    above(pe, zt_done, 5 * b + (0, 1, 2, 4)[i])
                    for t in range(TPB):
                        ins = pe.transpose(ps[:, T_BANK, P * t:P * t + P],
                                           (zst_b + zst_c)[i][:, P * t:P * t + P], ident[:, :])
                    ins.then_inc(zt_ps, 1)

            def b_products(b):
                turn_staged(b, (0, 1))
                pe.wait_ge(zt_done, 5 * b + 2)
                pe.wait_ge(u_done, 2)
                above(pe, rot_done, 4 * b)
                for i in range(2):
                    for t in range(TPB):
                        ins = pe.matmul(ps[:, 4 + 2 * i + t // 2, 256 * (t % 2):256 * (t % 2) + 256],
                                        bT[:, i, t, :], uT[:, b, :], start=True, stop=True)
                ins.then_inc(bu_ps, 1)

            b_products(0)
            turn_staged(0, (2, 3))
            for b in range(NBLK):
                ada(4 + 5 * b, 6 + 5 * b)
                if b + 1 < NBLK:
                    b_products(b + 1)
                ada(6 + 5 * b, 7 + 5 * b)
                pe.wait_ge(zt_done, 5 * b + 5)
                pe.wait_ge(post_d, b + 1)
                pe.wait_ge(post_p, 2 * b + 2)
                above(pe, y5_done, b)
                terms = ((0, prod[:, 0]), (1, prod[:, 1]), (2, prod2[:, 0]), (2, prod2[:, 1]))
                for j, (i, state) in enumerate(terms):
                    for t in range(TPB):
                        ins = pe.matmul(ps[:, 3, 0:256], cT[:, i, t, :], state[:, t, :],
                                        start=j == 0 and t == 0, stop=j == 3 and t == TPB - 1)
                ins.then_inc(y5_ps, 1)
                if b + 1 < NBLK:
                    turn_staged(b + 1, (2, 3))
                ada(7 + 5 * b, 9 + 5 * b)
            gate_row(0)
            pe.wait_ge(gelu_done, 4)
            for i in range(4):
                tt, n = divmod(i, 2)
                if i == 1:
                    pe.wait_ge(gg_done, 1)
                for half in range(2):
                    wait_landed(pe, N_WOUT + half)
                    for k in range(NBLK):
                        ins = pe.matmul(ps[:, 2 * i + half, :], uT[:, k, P * tt:P * tt + P],
                                        gran4(N_WOUT + half)[:, k, 512 * n:512 * n + 512],
                                        start=k == 0, stop=k == NBLK - 1)
                    if i == 3:
                        ins.then_inc(used[(N_WOUT + half) % RING], 1)
                    elif half:
                        ins.then_inc(wo_ps, 1)
            transpose_x(1)
            wait_hT(1)
            tokens = lambda k, ch: hT[:, k, P * ch:P * ch + P]
            ffn_turn = lambda g: (N_FFN + g) // RING
            for f in range(FB):
                item(f, 2 * f - 2, 2 * f - 2, 1, tokens, N_FFN, ffn_turn)
                item(f, 2 * f - 1, 2 * f - 1, 0, tokens, N_FFN, ffn_turn)
            for ch, q in ((1, 2 * FB - 2), (0, 2 * FB - 1)):
                turn_item(q, ch)
                down_product(FB - 1, q, ch, N_FFN, ffn_turn)
            pe.wait_ge(aT_done, 4 * FB)
            gate_row(1)
            transpose_x(2)
            wait_hT(2)
            for r in range(4):
                n = N_QKV + r
                wait_landed(pe, n)
                above(pe, qk_done, r - 1)
                if r == 1:
                    pe.wait_ge(gg_done, 2)
                for j in range(4):
                    for k in range(KD):
                        ins = pe.matmul(ps[:, 2 * (r % 2) + j // 2, 256 * (j % 2):256 * (j % 2) + 256],
                                        gran8(n)[:, k, P * j:P * j + P], hT[:, k, :], start=k == 0, stop=k == KD - 1)
                ins.then_inc(used[n % RING], 1)
            for r in range(2):
                n = N_QKV + 4 + r
                wait_landed(pe, n)
                for tt in range(TT):
                    for k in range(KD):
                        ins = pe.matmul(ps[:, Y_BANK + 2 * tt + r, :], tokens(k, tt), gran8(n)[:, k, :],
                                        start=k == 0, stop=k == KD - 1)
                ins.then_inc(used[n % RING], 1)

            def scores(h):
                b = h % 2
                pe.wait_ge(qk_done, 4)
                if h >= 2:
                    pe.wait_ge(zcopy_done, h - 1)
                for g in range(2):
                    r = slice(DH * g, DH * g + DH)
                    pe.matmul(ps[:, 2 * b + g, 0:256], kT[r, h, 0:P], qT[r, h, :], start=True, stop=True)
                    ins = pe.matmul(ps[:, 2 * b + g, 256:384], kT[r, h, P:SEQ], qT[r, h, P:SEQ], start=True, stop=True)
                ins.then_inc(z_ps, 1)

            def suffix(h):
                b = h % 2
                pe.wait_ge(spm_done, h + 1)
                if h:
                    pe.wait_ge(arg_done, h)
                else:
                    pe.wait_ge(v_out, 4)
                for g in range(2):
                    z = z_p[:, b, g]
                    pe.matmul(ps[:, 4 + g, 0:256], incl[:, :], z[:, 0:256], start=True, stop=False)
                    pe.matmul(ps[:, 4 + g, P:256], ones[:, :], z[:, 256:384], start=False, stop=True)
                    ins = pe.matmul(ps[:, 4 + g, 256:384], incl[:, :], z[:, 256:384], start=True, stop=True)
                ins.then_inc(sfx_ps, 1)

            def values(h):
                b = h % 2
                pe.wait_ge(w_done, 2 * h + 2)
                if h >= 2:
                    pe.wait_ge(o_done, h - 1)
                for g in range(2):
                    hd = slice(DH * (2 * h + g), DH * (2 * h + g) + DH)
                    o = ps[DH * g:DH * g + DH, 6 + b, :]
                    pe.matmul(o[:, 0:256], v_sb[:, 0, hd], z_w[:, h % 3, g, 0:256], start=True, stop=False)
                    ins = pe.matmul(o[:, P:256], v_sb[:, 1, hd], z_w[:, h % 3, g, 256:384], start=False, stop=True)
                ins.then_inc(o_ps, 1)

            for h in range(HEADS // 2 + 2):
                if h < HEADS // 2:
                    scores(h)
                if 1 <= h <= HEADS // 2:
                    suffix(h - 1)
                if h >= 2:
                    values(h - 2)
            pe.wait_ge(o_done, HEADS // 2)
            for r in range(2):
                n = N_SBOUT + r
                wait_landed(pe, n)
                for tt in range(TT):
                    for k in range(KD):
                        ins = pe.matmul(ps[:, Y_BANK + 2 * tt + r, :], oT[:, k, P * tt:P * tt + P], gran8(n)[:, k, :],
                                        start=k == 0, stop=k == KD - 1)
                ins.then_inc(used[n % RING], 1)
            gate_row(2)
            transpose_x(3)
            wait_hT(3)
            pe.wait_ge(router_in, 32)
            pe.wait_ge(gg_done, 3)
            for tt in range(TT):
                lg = ps[:, S_BANK, 8 * tt:8 * tt + 8]
                for k in range(KD):
                    pe.matmul(lg, tokens(k, tt), wr_sb[:, k, :], start=k == 0, stop=False)
                ins = pe.matmul(lg, ones[0:1, :], br_sb[:, :], start=False, stop=True)
            ins.then_inc(lg_ps, 1)
            pe.wait_ge(sel_done, 2)
            chosen = [rt[:, tt, 48:56] for tt in range(TT)]
            rank = lambda i: ps[:, S_BANK, 16 + 8 * i:24 + 8 * i]
            pe.matmul(rank(0), strict[:, :], chosen[0], start=True, stop=True)
            pe.matmul(rank(1), ones[:, :], chosen[0], start=True, stop=False)
            pe.matmul(rank(1), strict[:, :], chosen[1], start=False, stop=True)
            pe.matmul(rank(2), ones[:, :], chosen[0], start=True, stop=False)
            pe.matmul(rank(2), ones[:, :], chosen[1], start=False, stop=True).then_inc(rank_ps, 1)

            gathered = lambda k, ch: xe[:, k, ch, :]
            pe.wait_ge(route_done, 1)
            with pe.Fori(0, NE) as e:
                nch, more, items2, _, _, _, by_width = expert_counts(pe, e)
                moe_turn = lambda g: e * (PER_EXPERT // RING) + (N_MOE + g) // RING
                pe.wait_ge(onehot_done, 4 * e + 4)
                pe.wait_ge(silu_done, items2 + 2)
                pe.wait_ge(act_done, items2 + 2)
                pe.wait_ge(aT_done, items2 * 2 + 4)
                pe.wait_ge(sc_done, 4 * e + 4)

                def gather(ch):
                    for k in range(KD):
                        bank = (G_BANK, T_BANK)[ch] + k // 4
                        for tt in range(TT):
                            ins = pe.matmul(ps[:, bank, P * (k % 4):P * (k % 4) + P], hn[:, tt, P * k:P * k + P],
                                            g1[:, tt, P * ch:P * ch + P], start=tt == 0, stop=tt == TT - 1)
                    return ins

                def scatter_weights(ch):
                    for tt in range(TT):
                        ins = pe.transpose(ps[:, Y_BANK + 3, 256 * ch + P * tt:256 * ch + P * tt + P],
                                           gw[:, tt, P * ch:P * ch + P], ident[:, :])
                    return ins

                with pe.If(nch > 1):
                    gather(1)
                gather(0).then_inc(xe_ps, 1)
                with pe.If(nch > 1):
                    scatter_weights(1)
                scatter_weights(0).then_inc(st_ps, 1)
                pe.wait_ge(xe_done, e + 1)
                pe.wait_ge(st_done, e + 1)
                for f in range(FB + 1):
                    q2 = items2 + f * nch
                    by_width(lambda ch, width: item(f, q2 if ch else q2 + more, q2 if ch else q2 + 1, ch, gathered,
                                                    N_MOE, moe_turn, width), True)
                pe.wait_ge(ysb_act, e + 1)
                pe.wait_ge(ysb_dve, e + 1)
                for i in range(4):
                    tt, n = divmod(i, 2)
                    if i >= 2:
                        pe.wait_ge(sc_done, 4 * e + i + 3)
                    dst = ps[:, T_BANK + i % 2, :]

                    def spread(ch, start, stop):
                        return pe.matmul(dst, scT[:, ch, P * tt:P * tt + P], ysb[:, ch, 512 * n:512 * n + 512],
                                         start=start, stop=stop)

                    with pe.If(nch > 1):
                        spread(1, True, False)
                        spread(0, False, True).then_inc(sc_ps, 1)
                    with pe.Else():
                        spread(0, True, True).then_inc(sc_ps, 1)
            pe.wait_ge(sc_done, 4 * NE + 4)
            gate_row(3)


_INS = ["x", "c", "ada_w", "ada_b", "norm_g", "s5_w_in", "s5_lambda_re", "s5_lambda_im", "s5_b_re", "s5_b_im",
        "s5_c_re", "s5_c_im", "s5_d", "s5_log_step", "s5_w_out", "sb_w_qkv", "sb_w_out", "ffn_w_gate_up",
        "ffn_w_down", "moe_w_router", "moe_b_router", "moe_w_gate_up", "moe_w_down"]


def kernel(**inputs):
    import numpy as np
    import concourse.bacc as bacc
    from concourse.bass_utils import run_bass_kernel_spmd

    nc = bacc.Bacc("TRN2", target_bir_lowering=False, num_devices=1)
    arrays, args = {}, []
    for name in _INS:
        a = np.ascontiguousarray(inputs[name])
        arrays[f"in_{name}_dram"] = a
        args.append(nc.dram_tensor(f"in_{name}_dram", a.shape, mybir.dt.from_np(a.dtype), kind="ExternalInput").ap())
    args.append(nc.dram_tensor("out_dram", (1, SEQ, D), F32, kind="ExternalOutput").ap())
    program(nc, *args)
    r = run_bass_kernel_spmd(nc, [arrays], core_ids=[0])
    return r.results[0]["out_dram"]
```

```python
import math
from contextlib import ExitStack

import concourse.bass as bass
from concourse import mybir

F32 = mybir.dt.float32
F32R = mybir.dt.float32r
I32 = mybir.dt.int32
U32 = mybir.dt.uint32
ALU = mybir.AluOpType
ACT = mybir.ActivationFunctionType
AX = mybir.AxisListType

P = 128
D = 1024
KD = D // P
SEQ = 256
TT = SEQ // P
W5 = D // 2
NBLK = W5 // P
HG = 16
NS = 64
TPB = 4
NT = NBLK * TPB
HEADS = 16
DH = 64
FF = 7 * D // 2
FB = FF // 512
NE = 8
EPS = 1e-6
ROOT_D = 32.0
assert ROOT_D ** 2 == D
MODS = 12
RING = 7
GRAN = 4096
ARENA = 13568
MAGIC = 12582912.0
TWO_PI = 2 * math.pi
SIN_SCALE = TWO_PI * (1 - 2e-7)

G_BANK, U_BANK, T_BANK, S_BANK, Y_BANK = 0, 1, 2, 3, 4

PER_EXPERT = 3 * FB


def gate_at(f):
    return 0 if f == 0 else 3 * f - 1


def up_at(f):
    return gate_at(f) + 1


def down_at(f):
    return 3 * f + 4 if f < FB - 1 else PER_EXPERT - 1


N_ADA0A = 0
N_WIN = 4
N_ADA0B = 5
N_ADA1 = 13
N_WOUT = 25
N_FFN = 27
N_QKV = 48
N_SBOUT = 54
N_MOE = 56
assert N_MOE % RING == 0 and PER_EXPERT % RING == 0


def ada_place(layer, r):
    if layer:
        return N_ADA1 + r
    return N_ADA0A + r if r < 4 else N_ADA0B + r - 4


def program(nc, x, c, ada_w, ada_b, norm_g, s5_w_in, s5_lambda_re, s5_lambda_im, s5_b_re, s5_b_im,
            s5_c_re, s5_c_im, s5_d, s5_log_step, s5_w_out, sb_w_qkv, sb_w_out, ffn_w_gate_up,
            ffn_w_down, moe_w_router, moe_b_router, moe_w_gate_up, moe_w_down, out):
    ctx = ExitStack()
    with ctx:
        def sb(name, shape, dt=F32):
            return ctx.enter_context(nc.sbuf_tensor(name, shape, dt))

        def sem(name):
            return ctx.enter_context(nc.semaphore(name))

        ps = ctx.enter_context(nc.psum_tensor("ps", [P, 8, 512], F32))

        x_sb = sb("x_sb", [P, TT, D])
        hn = sb("hn", [P, TT, D])
        gg = sb("gg", [P, D])
        junk = sb("junk", [P, D])
        tbuf = sb("tbuf", [P, D])
        ident = sb("ident", [P, P])
        ones = sb("ones", [P, P])
        incl = sb("incl", [P, P])
        strict = sb("strict", [P, P])
        chmask = sb("chmask", [P, 8])
        steps = sb("steps", [P, SEQ])
        inv32 = sb("inv32", [P, 1])
        half = sb("half", [P, 1])
        cols = sb("cols", [P, 128])
        c32 = sb("c32", [P, KD, 32])
        adab = sb("adab", [P, 4, 24])
        modc = sb("modc", [P, 2, MODS, 4])
        scale_c = sb("scale_c", [P, 4, KD])
        gate_c = sb("gate_c", [P, 4, KD])
        stat = sb("stat", [P, 16])
        wr_sb = sb("wr_sb", [P, KD, NE])
        br_sb = sb("br_sb", [1, NE])

        cnt_i = sb("cnt_i", [1, 3, NE], I32)
        with ExitStack() as first:
            hT, ring, arena = (first.enter_context(nc.sbuf_tensor(name, shape, F32)) for name, shape in (
                ("hT", [P, KD, SEQ]), ("ring", [P, RING, GRAN]), ("arena", [P, ARENA])))
        x_lo = sb("x_lo", [P, KD, SEQ])
        ring_lo = [sb(f"ring_lo{i}", [P, GRAN]) for i in range(RING)]
        w_hi, x_hi = sb("w_hi", [P, 2, GRAN]), sb("x_hi", [P, KD, SEQ])
        aT_hi, aT_lo = sb("aT_hi", [P, 2, 4, P]), sb("aT_lo", [P, 2, 4, P])

        def view(at, shape):
            n = math.prod(shape)
            names = [f"d{i}" for i in range(len(shape))]
            ap = arena[:, at:at + n]
            if len(shape) == 1:
                return ap
            return ap.rearrange(f"p ({' '.join(names)}) -> p {' '.join(names)}",
                                **{k: v for k, v in zip(names, shape)})

        class Place:
            def __init__(self):
                self.at = 0

            def __call__(self, *shape):
                v = view(self.at, shape)
                self.at += math.prod(shape)
                assert self.at <= ARENA
                return v

        pl = Place()
        cosT, sinT = pl(2, TPB, SEQ), pl(2, TPB, SEQ)
        bT = pl(2, TPB, P)
        cT = pl(3, TPB, P)
        zst_b = (pl(640), gg[:, 0:640])
        zst_c = (pl(512), tbuf[:, 0:512])
        prod = pl(2, TPB, SEQ)
        uT = pl(NBLK, SEQ)
        b_raw = pl(2, NT, HG)
        bb = pl(2, NT, HG)
        c_raw = pl(2, NBLK, NS)
        par = pl(32, NT)
        rows = pl(640)
        v_re = hn[:, 0, :].rearrange("p (t s) -> p t s", t=TPB)
        v_im = hn[:, 1, :].rearrange("p (t s) -> p t s", t=TPB)
        prod2 = hT[:, :, :].rearrange("p (a t) s -> p a t s", a=2)

        pl = Place()
        pl(2 * GRAN + KD * SEQ + 16 * P)
        a_ff = pl(2, 512)
        silu_ff = junk[:, :].rearrange("p (c n) -> p c n", c=2)

        pl = Place()
        qT, kT, oT = pl(KD, SEQ), pl(KD, SEQ), pl(KD, SEQ)
        v_sb = pl(TT, D)
        z_e = pl(2, 2, 384)
        z_p = pl(2, 2, 384)
        z_w = pl(3, 2, 384)

        pl = Place()
        a_sb = pl(2, 512)
        aT = pl(2, 4, P)
        sg = pl(512)
        xe = pl(KD, 2, P)
        ysb = pl(2, D)
        scT = pl(2, SEQ)
        g1 = pl(TT, SEQ)
        gw = pl(TT, SEQ)
        macc = pl(TT, D)
        rt = pl(TT, 96)
        rcol = pl(NE + 1, 4)
        pick = pl(1, 4)
        cnt = pl(4, NE)
        g_part = pl(2, 512)
        silu_T = pl(4, 64)
        fold = pl(2, P)
        slots = pl(3, SEQ)

        landed = [sem(f"landed{i}") for i in range(RING)]
        used = [sem(f"used{i}") for i in range(RING)]
        params_in, x_in, router_in = sem("params_in"), sem("x_in"), sem("router_in")
        out_written, consts_done = sem("out_written"), sem("consts_done")
        cols_ready, cols_ps, cols_done, silu_c_done, c32_done, gg_done = (
            sem("cols_ready"), sem("cols_ps"), sem("cols_done"), sem("silu_c_done"), sem("c32_done"), sem("gg_done"))
        dve_step = sem("dve_step")
        pool_step = sem("pool_step")
        part_out, mod_ps, mod_out, mod_done = sem("part_out"), sem("mod_ps"), sem("mod_out"), sem("mod_done")
        ss_done, rs_done, ry_done, xn_done, hT_ps, hT_act, hT_dve = (
            sem("ss_done"), sem("rs_done"), sem("ry_done"), sem("xn_done"), sem("hT_ps"), sem("hT_act"), sem("hT_dve"))
        x_new, ys_done, diag_done, gg_ps = sem("x_new"), sem("ys_done"), sem("diag_done"), sem("gg_ps")
        u_ps, u_done = sem("u_ps"), sem("u_done")
        turn_ready, trig1_done, frac_done = sem("turn_ready"), sem("trig1_done"), sem("frac_done")
        angle_done, table_done = sem("angle_done"), sem("table_done")
        zst_done, zt_ps, zt_done = sem("zst_done"), sem("zt_ps"), sem("zt_done")
        bu_ps, rot_done, v_done, scan_done, post_d, post_p, y5_ps, y5_done = (
            sem("bu_ps"), sem("rot_done"), sem("v_done"), sem("scan_done"), sem("post_d"), sem("post_p"),
            sem("y5_ps"), sem("y5_done"))
        gelu_done, wo_ps, sig_done, glu_done = sem("gelu_done"), sem("wo_ps"), sem("sig_done"), sem("glu_done")
        gate1_done, up1_done = sem("gate1_done"), sem("up1_done")
        silu_done, act_done, tr_done, aT_done = sem("silu_done"), sem("act_done"), sem("tr_done"), sem("aT_done")
        whi_done, wlo_done, xhi_done, xlo_done, ahi_done = (
            sem("whi_done"), sem("wlo_done"), sem("xhi_done"), sem("xlo_done"), sem("ahi_done"))
        qk_done, v_out = sem("qk_done"), sem("v_out")
        z_ps, zabs_done, zcopy_done, exp_done, ln_done, sp_done, spm_done = (
            sem("z_ps"), sem("zabs_done"), sem("zcopy_done"), sem("exp_done"), sem("ln_done"), sem("sp_done"),
            sem("spm_done"))
        sfx_ps, arg_done, wexp_done, w_done, o_ps, o_done = (
            sem("sfx_ps"), sem("arg_done"), sem("wexp_done"), sem("w_done"), sem("o_ps"), sem("o_done"))
        lg_ps, lmax_done, pexp_done, sel_done, rank_ps, route_done = (
            sem("lg_ps"), sem("lmax_done"), sem("pexp_done"), sem("sel_done"), sem("rank_ps"), sem("route_done"))
        weighted_done, xe_dve = sem("weighted_done"), sem("xe_dve")
        pick_done, onehot_done, xe_ps, xe_done, st_ps, st_done = (
            sem("pick_done"), sem("onehot_done"), sem("xe_ps"), sem("xe_done"), sem("st_ps"), sem("st_done"))
        ysb_act, ysb_dve, sc_ps, sc_done = sem("ysb_act"), sem("ysb_dve"), sem("sc_ps"), sem("sc_done")

        r_c = rows[0:KD, 0:P]
        r_lam = rows[0:NT, 128:384].rearrange("p (a n) -> p a n", a=2)
        r_ls = rows[0:NT, 384:386]
        r_lsb = rows[0:NT, 512:640].rearrange("p (a n) -> p a n", a=2)
        r_d = junk[0:NBLK, 512:640]
        r_g = tbuf[0:8, :]
        r_b = junk[0:24, 0:512]
        part = rows[:, 0:512]
        C_C, C_LRE, C_LIM, C_LS, C_D, C_G = 0, 8, 24, 40, 56, 60
        (STEP, XM, THETA, KTURN, TURN, COST, SIN1, COS1, MAG, LBR, LBI, CRE, CIM, DEN, FHI, FLO,
         T0, T1, T2, T3, T4) = range(21)
        MODS_OF = ((0, 0), (0, 6), (1, 0), (1, 6))

        def pcol(i):
            return par[:, i, :]

        def shift_col(s, k):
            layer, r = MODS_OF[s]
            return modc[:, layer, r + k // 4, k % 4:k % 4 + 1]

        def mods(s, which):
            layer, r = MODS_OF[s]
            return modc[:, layer, r + 2 * which:r + 2 * which + 2, :].rearrange("p a b -> p (a b)")

        def g_cols(s, post):
            return cols[:, C_G:C_G + 64].rearrange("p (k r) -> p k r", r=8)[:, :, 2 * s + post]

        def gran(n):
            return ring[:, n % RING, :]

        def gran8(n):
            return gran(n).rearrange("p (k n) -> p k n", k=KD)

        def gran4(n):
            return gran(n).rearrange("p (k n) -> p k n", k=4)

        def wait_landed(eng, n, turn=None):
            eng.wait_ge(landed[n % RING], 16 * (n // RING if turn is None else turn) + 16)

        def wait_used(eng, n, turn=None):
            eng.wait_ge(used[n % RING], (n // RING if turn is None else turn) + 1)

        def ff_half(buffer, half):
            return buffer[:, 2048 * half:2048 * half + 2048]

        def above(eng, s, value):
            if not isinstance(value, int) or value > 0:
                eng.wait_ge(s, value)

        def expert_counts(eng, e):
            more = eng.value_load(cnt_i[0:1, 0, bass.ds(e, 1)], min_val=0, max_val=1)
            before1 = eng.value_load(cnt_i[0:1, 1, bass.ds(e, 1)], min_val=FB, max_val=FB * (NE + 1))
            kind = eng.value_load(cnt_i[0:1, 2, bass.ds(e, 1)], min_val=0, max_val=4)

            def by_width(run):
                with eng.If(kind > 2):
                    with eng.If(kind > 3):
                        run(1, P)
                    with eng.Else():
                        run(1, 32)
                with eng.If(kind > 1):
                    run(0, P)
                with eng.Else():
                    with eng.If(kind > 0):
                        run(0, 64)
                    with eng.Else():
                        run(0, 32)

            return more + 1, more, before1 + e * FB + (FB - 2), before1, kind, by_width

        block = ctx.enter_context(nc.Block())

        @block.sync
        def _(sp):
            def load(n, dst, src, turn=None):
                turn = n // RING if turn is None else turn
                above(sp, used[n % RING], turn)
                sp.dma_start(dst, src).then_inc(landed[n % RING], 16)

            def cols512(w, at):
                return w[:, at:at + 512].rearrange("(k p) n -> p k n", p=P)

            def load_ada(layer, r):
                n = ada_place(layer, r)
                load(n, gran8(n), cols512(ada_w[layer], 512 * r))

            sp.wait_ge(params_in, 16 * 13)
            for r in range(4):
                load_ada(0, r)
            load(N_WIN, gran8(N_WIN), cols512(s5_w_in[0], 0))
            for r in range(4, MODS):
                load_ada(0, r)
            for r in range(MODS):
                load_ada(1, r)
            for h in range(2):
                load(N_WOUT + h, gran4(N_WOUT + h),
                     s5_w_out[0][:, D * h:D * h + D].rearrange("(k p) n -> p k n", p=P))

            def swiglu_weights(w_gu, w_dn, base, turn):
                def down(f):
                    g = down_at(f)
                    load(base + g, gran4(base + g),
                         w_dn[512 * f:512 * f + 512, :].rearrange("(k p) n -> p k n", p=P), turn(g))
                for f in range(FB):
                    for g, at in ((gate_at(f), 512 * f), (up_at(f), FF + 512 * f)):
                        load(base + g, gran8(base + g), cols512(w_gu, at), turn(g))
                    if f:
                        down(f - 1)
                down(FB - 1)

            swiglu_weights(ffn_w_gate_up[0], ffn_w_down[0], N_FFN, lambda g: (N_FFN + g) // RING)
            for r in range(6):
                load(N_QKV + r, gran8(N_QKV + r), cols512(sb_w_qkv[0], 512 * r))
            for r in range(2):
                load(N_SBOUT + r, gran8(N_SBOUT + r), cols512(sb_w_out[0], 512 * r))
            with sp.Fori(0, NE) as e:
                gu = moe_w_gate_up[0].rearrange("e a b -> (e a) b")[bass.ds(e * D, D), :]
                dn = moe_w_down[0].rearrange("e a b -> (e a) b")[bass.ds(e * FF, FF), :]
                swiglu_weights(gu, dn, N_MOE, lambda g: e * (PER_EXPERT // RING) + (N_MOE + g) // RING)
            sp.wait_ge(x_new, 8)
            sp.dma_start(out[0].rearrange("(t p) d -> p t d", p=P), x_sb[:, :, :]).then_inc(out_written, 16)
            sp.wait_ge(out_written, 16)

        @block.gpsimd
        def _(pool):
            count = [0]

            def link(ins):
                count[0] += 1
                ins.then_inc(pool_step, 1)
                pool.wait_ge(pool_step, count[0])

            link(pool.memset(ones[:, :], 1.0))
            pool.affine_select(out=ident[:, :], in_=ones[:, :], compare_op=ALU.is_equal, fill=0.0, base=0,
                               pattern=[[-1, P]], channel_multiplier=1).then_inc(consts_done, 1)
            pool.affine_select(out=incl[:, :], in_=ones[:, :], compare_op=ALU.is_ge, fill=0.0, base=0,
                               pattern=[[-1, P]], channel_multiplier=1).then_inc(consts_done, 1)
            pool.affine_select(out=strict[:, :], in_=ones[:, :], compare_op=ALU.is_gt, fill=0.0, base=0,
                               pattern=[[1, P]], channel_multiplier=-1).then_inc(consts_done, 1)
            link(pool.affine_select(out=chmask[:, :], in_=ones[:, 0:8], compare_op=ALU.is_ge, fill=0.0, base=0,
                                    pattern=[[-HG, 8]], channel_multiplier=1))
            pool.affine_select(out=chmask[:, :], in_=chmask[:, :], compare_op=ALU.is_ge, fill=0.0, base=HG - 1,
                               pattern=[[HG, 8]], channel_multiplier=-1).then_inc(consts_done, 1)
            pool.iota(steps[:, :], [[1, SEQ]], base=0, channel_multiplier=0,
                      allow_small_or_imprecise_dtypes=True).then_inc(consts_done, 1)
            pool.memset(inv32[:, :], 1.0 / 32).then_inc(consts_done, 1)
            link(pool.memset(half[:, :], -0.5))
            pool.wait_ge(consts_done, 6)

            def add_rotated(b):
                pool.wait_ge(rot_done, 4 * b + 2)
                pool.tensor_tensor(v_re, prod[:, 0], prod[:, 1], ALU.add).then_inc(v_done, 1)
                pool.wait_ge(rot_done, 4 * b + 4)
                pool.tensor_tensor(v_im, prod2[:, 0], prod2[:, 1], ALU.subtract).then_inc(v_done, 1)

            def unrotate(b):
                q = b % 2
                pool.wait_ge(v_done, 2 * b + 2)
                pool.wait_ge(scan_done, 2 * TPB * (b + 1))
                pool.tensor_tensor(prod2[:, 0], v_re, sinT[:, q], ALU.mult).then_inc(post_p, 1)
                pool.tensor_tensor(prod2[:, 1], v_im, cosT[:, q], ALU.mult).then_inc(post_p, 1)
                pool.wait_ge(post_p, 2 * b + 2)

            def inverse_norm(s, ready, done, src, dst):
                for tt in range(TT):
                    pool.wait_ge(ready, 2 * s + tt + 1)
                    a, b = stat[:, src + tt:src + tt + 1], stat[:, dst + tt:dst + tt + 1]
                    link(pool.tensor_scalar(b, a, D * EPS, None, ALU.add))
                    pool.tensor_tensor(b, b, half[:, :], ALU.pow).then_inc(done, 1)

            def mod_bias(layer, lo, hi, subs):
                pool.wait_ge(mod_out, MODS * layer + hi)
                m = modc[:, layer, lo:hi, :]
                link(pool.tensor_tensor(m, m, adab[:, :, MODS * layer + lo:MODS * layer + hi].rearrange("p j r -> p r j"),
                                        ALU.add))
                for s in subs:
                    link(pool.tensor_scalar(scale_c[:, s, :], mods(s, 1), 1.0, None, ALU.add))
                    pool.tensor_tensor(scale_c[:, s, :], scale_c[:, s, :], g_cols(s, 0), ALU.mult).then_inc(mod_done, 1)

            inverse_norm(0, ss_done, rs_done, 0, 8)
            mod_bias(0, 0, 4, (0,))
            for b in range(NBLK):
                add_rotated(b)
                unrotate(b)
                if b == 2:
                    mod_bias(0, 4, MODS, (1,))
            mod_bias(1, 0, MODS, (2, 3))
            for s in range(4):
                if s:
                    inverse_norm(s, ss_done, rs_done, 0, 8)
                inverse_norm(s, ys_done, ry_done, 4, 12)

        @block.scalar
        def _(act):
            act.dma_start(r_c, c.rearrange("a (k n) -> (a k) n", n=P)).then_inc(params_in, 16)
            act.dma_start(r_lam[:, 0, :], s5_lambda_re[0].rearrange("(t g) n -> t (g n)", g=2)).then_inc(params_in, 16)
            act.dma_start(r_lam[:, 1, :], s5_lambda_im[0].rearrange("(t g) n -> t (g n)", g=2)).then_inc(params_in, 16)
            act.dma_start(r_ls, s5_log_step[0].rearrange("(t g) -> t g", g=2)).then_inc(params_in, 16)
            act.dma_start(r_d, s5_d[0].rearrange("(b g) h -> b (g h)", b=NBLK)).then_inc(params_in, 16)
            act.dma_start(r_g, norm_g.rearrange("a b n -> (a b) n")).then_inc(params_in, 16)
            act.dma_start(r_b, ada_b.rearrange("l (r n) -> (l r) n", n=512)).then_inc(params_in, 16)
            act.dma_start(x_sb[:, :, :], x[0].rearrange("(t p) d -> p t d", p=P)).then_inc(x_in, 16)
            for i, w in enumerate((s5_b_re, s5_b_im)):
                for g in range(2):
                    act.dma_start(b_raw[NS * g:NS * g + NS, i], w[0].rearrange("(t g) n h -> g n t h", g=2)[g]
                                  ).then_inc(params_in, 16)
            for i, w in enumerate((s5_c_re, s5_c_im)):
                act.dma_start(c_raw[:, i], w[0].rearrange("(b g) h n -> (g h) b n", b=NBLK)).then_inc(params_in, 16)
            act.dma_start(wr_sb[:, :, :], moe_w_router[0].rearrange("(k p) n -> p k n", p=P)).then_inc(router_in, 16)
            act.dma_start(br_sb[:, :], moe_b_router).then_inc(router_in, 16)

            def pre_stats(s):
                for tt in range(TT):
                    if s == 0:
                        act.wait_ge(x_in, 16)
                    else:
                        act.wait_ge(x_new, 2 * (s - 1) + tt + 1)
                    act.activation(hn[:, tt, :], x_sb[:, tt, :], ACT.Square,
                                   accum_out=stat[:, tt:tt + 1]).then_inc(ss_done, 1)

            def hT_evict(s):
                act.wait_ge(mod_done, s + 1)
                for k in (0, 1, 4, 5):
                    act.wait_ge(hT_ps, 4 * s + k // 2 + 1)
                    act.activation(hT[:, k, :], ps[:, Y_BANK + k // 2, 256 * (k % 2):256 * (k % 2) + 256],
                                   ACT.Identity, bias=shift_col(s, k), scale=scale_c[:, s, k:k + 1]
                                   ).then_inc(hT_act, 1)

            def y_stats(s, source):
                for tt in range(TT):
                    if s or tt:
                        act.wait_ge(ys_done, 2 * s + tt)
                    act.activation(junk[:, :], source(tt), ACT.Square,
                                   accum_out=stat[:, 4 + tt:5 + tt]).then_inc(ys_done, 1)

            def y_banks(tt):
                return ps[:, Y_BANK + 2 * tt:Y_BANK + 2 * tt + 2, :].rearrange("p a b -> p (a b)")

            def ada_parts(lo, hi):
                for i in range(lo, hi):
                    wait_used(act, ada_place(*divmod(i, MODS)))
                    act.activation(part, ps[:, 0, :], ACT.Copy).then_inc(part_out, 1)
                    act.wait_ge(mod_ps, i + 1)
                    act.activation(modc[:, i // MODS, i % MODS, :], ps[:, 1, 0:4], ACT.Copy).then_inc(mod_out, 1)

            def trig(b):
                q = b % 2
                act.wait_ge(angle_done, 2 * b + 2)
                act.activation(sinT[:, q], sinT[:, q], ACT.Sin, scale=SIN_SCALE).then_inc(table_done, 1)
                act.activation(cosT[:, q], cosT[:, q], ACT.Sin, scale=SIN_SCALE).then_inc(table_done, 1)

            def gate_out(f, q, ch, base, turn, c1, width=P, prev=None):
                n = base + gate_at(f)
                if ch:
                    act.wait_ge(gate1_done, c1 + f + 1)
                else:
                    wait_used(act, n, turn(gate_at(f)))
                if width < P:
                    if f:
                        act.wait_ge(tr_done, prev + 1)
                    act.activation(g_part[:, ch, :], ps[:, G_BANK, :], ACT.Copy).then_inc(silu_done, 1)
                    return
                above(act, act_done, q)
                act.activation(sg, ps[:, G_BANK, :], ACT.Silu).then_inc(silu_done, 1)

            def aT_out(q, ch, width=P):
                act.wait_ge(tr_done, q + 1)
                if width < P:
                    src = ps[:, T_BANK, :].rearrange("p (k n) -> p k n", k=4)[:, :, 0:width]
                    act.activation(silu_T[:, :, 0:width], src, ACT.Silu).then_inc(aT_done, 1)
                else:
                    act.activation(aT[:, ch].rearrange("p k n -> p (k n)"), ps[:, T_BANK, :], ACT.Copy
                                   ).then_inc(aT_done, 2)

            pre_stats(0)
            act.wait_ge(cols_done, 1)
            act.activation(cols[:, 0:KD], cols[:, 0:KD], ACT.Silu).then_inc(silu_c_done, 1)
            act.wait_ge(turn_ready, 1)
            act.activation(pcol(SIN1), pcol(TURN), ACT.Sin, scale=SIN_SCALE).then_inc(trig1_done, 1)
            act.activation(pcol(COS1), pcol(COST), ACT.Sin, scale=SIN_SCALE).then_inc(trig1_done, 1)
            ada_parts(0, 4)
            hT_evict(0)
            for i in range(2):
                if i:
                    wait_used(act, N_WIN)
                else:
                    act.wait_ge(u_ps, 1)
                act.activation(uT[:, 2 * i:2 * i + 2, :].rearrange("p a b -> p (a b)"), ps[:, i, :], ACT.Copy
                               ).then_inc(u_done, 1)
            trig(0)
            trig(1)

            def turned_out(b, i):
                zt = ps[:, T_BANK, :].rearrange("p (t n) -> p t n", t=TPB)
                act.wait_ge(zt_ps, 4 * b + i + 1)
                act.activation((bT[:, 0], bT[:, 1], cT[:, 0], cT[:, 2])[i], zt, ACT.Copy, scale=-1.0 if i == 3 else 1.0
                               ).then_inc(zt_done, 1)
                if i == 2:
                    act.activation(cT[:, 1], zt, ACT.Copy, scale=-1.0).then_inc(zt_done, 1)

            for i in range(4):
                turned_out(0, i)
            for b in range(NBLK):
                ada_parts(4 + 5 * b, 6 + 5 * b)
                if b + 1 < NBLK:
                    turned_out(b + 1, 0)
                    turned_out(b + 1, 1)
                ada_parts(6 + 5 * b, 7 + 5 * b)
                if b + 1 < NBLK:
                    turned_out(b + 1, 2)
                    turned_out(b + 1, 3)
                ada_parts(7 + 5 * b, 9 + 5 * b)
                if b + 2 < NBLK:
                    trig(b + 2)
            for b in range(NBLK):
                act.wait_ge(y5_done, b + 1)
                act.activation(uT[:, b, :], uT[:, b, :], ACT.Gelu_apprx_tanh).then_inc(gelu_done, 1)
            for i in range(4):
                if i < 3:
                    act.wait_ge(wo_ps, i + 1)
                else:
                    wait_used(act, N_WOUT + 1)
                if i >= 2:
                    act.wait_ge(glu_done, i - 1)
                act.activation(junk[:, 512 * (i % 2):512 * (i % 2) + 512], ps[:, 2 * i + 1, :],
                               ACT.Sigmoid).then_inc(sig_done, 1)
            act.wait_ge(glu_done, 4)
            y_stats(0, lambda tt: hn[:, tt, :])
            pre_stats(1)

            def w_round(g, half):
                if g < PER_EXPERT:
                    wait_landed(act, N_FFN + g)
                    if g >= 2:
                        wait_used(act, N_FFN + g - 2)
                    act.activation(ff_half(w_hi[:, g % 2, :], half).bitcast(F32R), ff_half(gran(N_FFN + g), half),
                                   ACT.Copy).then_inc(whi_done, 1)

            def a_round(q, ch):
                act.wait_ge(tr_done, q + 1)
                act.activation(aT_hi[:, ch, :, :].rearrange("p k n -> p (k n)").bitcast(F32R),
                               ps[:, T_BANK if ch else U_BANK, :], ACT.Copy).then_inc(ahi_done, 1)

            def silu_out(f, ch):
                q = 2 * f + (0 if ch else 1)
                if ch:
                    act.wait_ge(gate1_done, f + 1)
                else:
                    wait_used(act, N_FFN + gate_at(f))
                above(act, act_done, q - 1)
                act.activation(silu_ff[:, ch, :], ps[:, G_BANK if ch else S_BANK, :], ACT.Silu
                               ).then_inc(silu_done, 1)

            w_round(0, 0)
            w_round(0, 1)
            hT_evict(1)
            act.wait_ge(hT_act, 8)
            act.wait_ge(hT_dve, 8)
            for h in range(2):
                act.activation(x_hi[:, 4 * h:4 * h + 4, :].bitcast(F32R), hT[:, 4 * h:4 * h + 4, :], ACT.Copy
                               ).then_inc(xhi_done, 1)
            for f in range(FB):
                g = gate_at(f)
                if f:
                    a_round(2 * f - 2, 1)
                w_round(g + 1, 0)
                silu_out(f, 1)
                if f:
                    a_round(2 * f - 1, 0)
                w_round(g + 1, 1)
                silu_out(f, 0)
                for n in range(g + 2, gate_at(f + 1) + 1):
                    w_round(n, 0)
                    w_round(n, 1)
            a_round(2 * FB - 2, 1)
            a_round(2 * FB - 1, 0)
            wait_used(act, N_FFN + PER_EXPERT - 1)
            y_stats(1, y_banks)
            pre_stats(2)
            hT_evict(2)
            for r in range(4):
                wait_used(act, N_QKV + r)
                src = ps[:, 2 * (r % 2):2 * (r % 2) + 2, :].rearrange("p a (b n) -> p (a b) n", b=2)
                act.activation((qT if r < 2 else kT)[:, 4 * (r % 2):4 * (r % 2) + 4, :], src, ACT.Copy,
                               scale=DH ** -0.5 if r < 2 else 1.0).then_inc(qk_done, 1)
            def o_out(h):
                act.wait_ge(o_ps, h + 1)
                act.activation(oT[:, h, :], ps[:, 6 + h % 2, 0:256], ACT.Copy).then_inc(o_done, 1)

            for h in range(HEADS // 2 + 1):
                b = h % 2
                if h < HEADS // 2:
                    act.wait_ge(z_ps, h + 1)
                    if h >= 3:
                        act.wait_ge(o_ps, h - 2)
                    act.activation(z_w[:, h % 3], ps[:, 2 * b:2 * b + 2, 0:384], ACT.Copy).then_inc(zcopy_done, 1)
                    act.wait_ge(zabs_done, h + 1)
                    act.activation(z_e[:, b], z_e[:, b], ACT.Exp).then_inc(exp_done, 1)
                    act.wait_ge(exp_done, h + 1)
                    act.activation(z_e[:, b], z_e[:, b], ACT.Ln, bias=1.0).then_inc(ln_done, 1)
                if h:
                    act.wait_ge(arg_done, h)
                    act.activation(z_w[:, (h - 1) % 3], z_w[:, (h - 1) % 3], ACT.Exp).then_inc(wexp_done, 1)
                if h >= 2:
                    o_out(h - 2)
            o_out(HEADS // 2 - 1)
            wait_used(act, N_SBOUT + 1)
            y_stats(2, y_banks)
            pre_stats(3)
            hT_evict(3)
            for tt in range(TT):
                act.wait_ge(lmax_done, tt + 1)
                act.activation(rt[:, tt, 8:16], rt[:, tt, 0:8], ACT.Exp, bias=rt[:, tt, 80:81],
                               accum_out=rt[:, tt, 81:82]).then_inc(pexp_done, 1)
            act.wait_ge(route_done, 1)
            with act.Fori(0, NE) as e:
                nch, more, items2, c1, _, by_width = expert_counts(act, e)
                moe_turn = lambda g: e * (PER_EXPERT // RING) + (N_MOE + g) // RING

                def xe_out(ch):
                    bank = (G_BANK, T_BANK)[ch]
                    for k in range(KD // 2):
                        ins = act.activation(xe[:, k, ch, :], ps[:, bank, P * (k % 4):P * (k % 4) + P],
                                             ACT.Identity, bias=shift_col(3, k), scale=scale_c[:, 3, k:k + 1])
                    return ins

                with act.If(nch > 1):
                    act.wait_ge(xe_ps, 2 * e + 1)
                    xe_out(1)
                act.wait_ge(xe_ps, 2 * e + 1)
                xe_out(0).then_inc(xe_done, 1)
                for f in range(FB + 1):
                    q2 = items2 + f * nch

                    def item(ch, width):
                        before = q2 if ch else q2 + 1
                        if f < FB:
                            gate_out(f, q2 + 2 if ch else q2 + more + 2, ch, N_MOE, moe_turn, c1, width, before)
                        if f:
                            aT_out(before, ch, width)

                    by_width(item)
                with act.If(nch > 1):
                    wait_used(act, N_MOE + PER_EXPERT - 1, moe_turn(PER_EXPERT - 1))
                    act.activation(ysb[:, 1, 0:512], ps[:, Y_BANK + 2, :], ACT.Copy)
                wait_used(act, N_MOE + PER_EXPERT - 1, moe_turn(PER_EXPERT - 1))
                act.activation(ysb[:, 0, 0:512], ps[:, Y_BANK, :], ACT.Copy).then_inc(ysb_act, 1)
            act.wait_ge(sc_done, 4 * NE + 4)
            y_stats(3, lambda tt: macc[:, tt, :])

        @block.vector
        def _(dve):
            count = [0]

            def link(ins):
                count[0] += 1
                ins.then_inc(dve_step, 1)
                dve.wait_ge(dve_step, count[0])

            def stt(o, a, s, b, op0, op1):
                return dve.scalar_tensor_tensor(out=o, in0=a, scalar=s, in1=b, op0=op0, op1=op1)

            def exp_small(dst, src):
                n, r, p, bits = pcol(T0), pcol(T1), pcol(T2), pcol(T3)
                link(dve.tensor_scalar(n, src, 1.0 / math.log(2), MAGIC, ALU.mult, ALU.add))
                link(dve.tensor_scalar(n, n, MAGIC, None, ALU.subtract))
                link(dve.tensor_scalar(n, n, -126.0, None, ALU.max))
                hi = 0.693145751953125
                link(stt(r, n, -hi, src, ALU.mult, ALU.add))
                link(stt(r, n, -(math.log(2) - hi), r, ALU.mult, ALU.add))
                link(dve.tensor_scalar(p, r, 1.0 / math.factorial(7), None, ALU.mult))
                for k in range(6, 0, -1):
                    link(stt(p, p, 1.0 / math.factorial(k), r, ALU.add, ALU.mult))
                link(dve.tensor_scalar(n, n, 127.0, 8388608.0, ALU.add, ALU.mult))
                link(dve.tensor_copy(bits.bitcast(I32), n))
                link(stt(dst, p, 1.0, bits, ALU.add, ALU.mult))

            def to_hT(s):
                for tt in range(TT):
                    dve.wait_ge(rs_done, 2 * s + tt + 1)
                    dve.tensor_scalar(hn[:, tt, :], x_sb[:, tt, :], stat[:, 8 + tt:9 + tt], ROOT_D, ALU.mult, ALU.mult
                                      ).then_inc(xn_done, 1)

            def hT_evict(s):
                dve.wait_ge(mod_done, s + 1)
                for k in (2, 3, 6, 7):
                    dve.wait_ge(hT_ps, 4 * s + k // 2 + 1)
                    dve.tensor_scalar(hT[:, k, :], ps[:, Y_BANK + k // 2, 256 * (k % 2):256 * (k % 2) + 256],
                                      scale_c[:, s, k:k + 1], shift_col(s, k), ALU.mult, ALU.add
                                      ).then_inc(hT_dve, 1)

            def gate_row(s):
                if s:
                    dve.wait_ge(x_new, 2 * s)
                dve.wait_ge(mod_done, 2 if s < 2 else 4)
                link(stt(gate_c[:, s, :], mods(s, 2), ROOT_D, g_cols(s, 1), ALU.mult, ALU.mult))
                dve.tensor_tensor(tbuf[:, :].rearrange("p (k n) -> p k n", k=KD),
                                  ident[:, :].unsqueeze(1).to_broadcast([P, KD, P]),
                                  gate_c[:, s, :].unsqueeze(2).to_broadcast([P, KD, P]), ALU.mult
                                  ).then_inc(diag_done, 1)
                dve.wait_ge(gg_ps, s + 1)
                dve.tensor_copy(gg[:, :], ps[:, 2:4, :].rearrange("p a b -> p (a b)")).then_inc(gg_done, 1)
                dve.wait_ge(gg_done, s + 1)

            def residual(s, source):
                for tt in range(TT):
                    dve.wait_ge(ry_done, 2 * s + tt + 1)
                    link(stt(tbuf[:, :], source(tt), stat[:, 12 + tt:13 + tt], gg[:, :], ALU.mult, ALU.mult))
                    dve.tensor_tensor(x_sb[:, tt, :], x_sb[:, tt, :], tbuf[:, :], ALU.add).then_inc(x_new, 1)
                    dve.wait_ge(x_new, 2 * s + tt + 1)

            def y_banks(tt):
                return ps[:, Y_BANK + 2 * tt:Y_BANK + 2 * tt + 2, :].rearrange("p a b -> p (a b)")

            def swiglu_out(f, q, ch, base, turn, c1, a_free, width=P):
                if width == P:
                    dve.wait_ge(silu_done, q + 1)
                if ch:
                    dve.wait_ge(up1_done, c1 + f + 1)
                else:
                    wait_used(dve, base + up_at(f), turn(up_at(f)))
                if a_free is not None:
                    dve.wait_ge(tr_done, a_free)
                if width == P:
                    dve.tensor_tensor(a_sb[:, ch, :], sg, ps[:, U_BANK, :], ALU.mult).then_inc(act_done, 1)
                else:
                    dve.tensor_copy(a_sb[:, ch, :], ps[:, U_BANK, :]).then_inc(act_done, 1)

            def narrow_aT(q, ch, width):
                dve.wait_ge(aT_done, q * 2 + 1)
                up = ps[:, S_BANK, :].rearrange("p (k n) -> p k n", k=4)[:, :, 0:width]
                dve.tensor_tensor(aT[:, ch, :, 0:width], silu_T[:, :, 0:width], up, ALU.mult).then_inc(aT_done, 1)

            scratch = junk[:, :].rearrange("p (t s) -> p t s", t=TPB)

            def angles(b):
                q = b % 2
                if b == 0:
                    dve.wait_ge(frac_done, 1)
                if b >= 2:
                    dve.wait_ge(post_d, b - 1)
                    dve.wait_ge(post_p, 2 * b - 2)
                fh = par[:, FHI, TPB * b:TPB * b + TPB].unsqueeze(2).to_broadcast([P, TPB, SEQ])
                fl = par[:, FLO, TPB * b:TPB * b + TPB].unsqueeze(2).to_broadcast([P, TPB, SEQ])
                t = steps[:, :].unsqueeze(1).to_broadcast([P, TPB, SEQ])
                s, co = sinT[:, q], cosT[:, q]
                link(dve.tensor_tensor(s, t, fh, ALU.mult))
                link(dve.tensor_scalar(scratch, s, MAGIC, MAGIC, ALU.add, ALU.subtract))
                link(dve.tensor_tensor(s, s, scratch, ALU.subtract))
                link(dve.tensor_tensor(co, t, fl, ALU.mult))
                link(dve.tensor_tensor(s, s, co, ALU.add))
                link(dve.tensor_scalar(co, s, 0.25, None, ALU.add))
                for v in (s, co):
                    link(dve.tensor_scalar(scratch, v, MAGIC, MAGIC, ALU.add, ALU.subtract))
                    dve.tensor_tensor(v, v, scratch, ALU.subtract).then_inc(angle_done, 1)
                    dve.wait_ge(angle_done, 2 * b + (1 if v is s else 2))

            dve.wait_ge(params_in, 16 * 13)
            link(dve.tensor_copy(r_lsb, r_ls.unsqueeze(2).to_broadcast([NT, 2, NS])))
            dve.memset(zst_b[0], 0.0).then_inc(cols_ready, 1)
            link(dve.memset(zst_b[1], 0.0))
            dve.wait_ge(cols_ps, 2)
            link(dve.tensor_copy(cols[:, 0:124], ps[:, 0, 0:124]))
            dve.tensor_copy(adab[:, :, :], ps[:, 1, 0:96].rearrange("p (a b) -> p a b", a=4)).then_inc(cols_done, 1)
            dve.wait_ge(cols_done, 1)
            lre, lim, ls = (cols[:, a:a + NT] for a in (C_LRE, C_LIM, C_LS))
            exp_small(pcol(STEP), ls)
            link(dve.tensor_tensor(pcol(THETA), lim, pcol(STEP), ALU.mult))
            link(dve.tensor_scalar(pcol(KTURN), pcol(THETA), 1 / TWO_PI, MAGIC, ALU.mult, ALU.add))
            link(dve.tensor_scalar(pcol(KTURN), pcol(KTURN), MAGIC, None, ALU.subtract))
            p1 = 6.28125
            p2 = 0.0019350051879882812
            p3 = TWO_PI - p1 - p2
            for p in (p1, p2, p3):
                link(stt(pcol(THETA), pcol(KTURN), -p, pcol(THETA), ALU.mult, ALU.add))
            link(dve.tensor_scalar(pcol(TURN), pcol(THETA), 1 / TWO_PI, None, ALU.mult))
            link(dve.tensor_scalar(pcol(COST), pcol(TURN), 0.25, None, ALU.add))
            link(dve.tensor_scalar(pcol(T0), pcol(COST), MAGIC, MAGIC, ALU.add, ALU.subtract))
            dve.tensor_tensor(pcol(COST), pcol(COST), pcol(T0), ALU.subtract).then_inc(turn_ready, 1)
            dve.wait_ge(turn_ready, 1)
            link(dve.tensor_scalar(pcol(FHI), pcol(TURN), 768.0, 768.0, ALU.add, ALU.subtract))
            dve.tensor_tensor(pcol(FLO), pcol(TURN), pcol(FHI), ALU.subtract).then_inc(frac_done, 1)
            dve.wait_ge(silu_c_done, 1)
            dve.tensor_copy(c32[:, :, :], cols[:, 0:KD].unsqueeze(2).to_broadcast([P, KD, 32])).then_inc(c32_done, 1)
            link(dve.tensor_tensor(pcol(XM), lre, pcol(STEP), ALU.mult))
            exp_small(pcol(MAG), pcol(XM))
            dve.wait_ge(trig1_done, 2)
            link(dve.tensor_tensor(pcol(LBR), pcol(MAG), pcol(COS1), ALU.mult))
            link(dve.tensor_tensor(pcol(LBI), pcol(MAG), pcol(SIN1), ALU.mult))
            link(dve.tensor_tensor(pcol(DEN), lre, lre, ALU.mult))
            link(dve.tensor_tensor(pcol(T0), lim, lim, ALU.mult))
            link(dve.tensor_tensor(pcol(DEN), pcol(DEN), pcol(T0), ALU.add))
            link(dve.reciprocal(pcol(DEN), pcol(DEN)))
            link(dve.tensor_scalar(pcol(T0), pcol(LBR), 1.0, None, ALU.subtract))
            link(dve.tensor_tensor(pcol(T1), pcol(T0), lre, ALU.mult))
            link(dve.tensor_tensor(pcol(T2), pcol(LBI), lim, ALU.mult))
            link(dve.tensor_tensor(pcol(T1), pcol(T1), pcol(T2), ALU.add))
            link(dve.tensor_tensor(pcol(CRE), pcol(T1), pcol(DEN), ALU.mult))
            link(dve.tensor_tensor(pcol(T1), pcol(LBI), lre, ALU.mult))
            link(dve.tensor_tensor(pcol(T2), pcol(T0), lim, ALU.mult))
            link(dve.tensor_tensor(pcol(T1), pcol(T1), pcol(T2), ALU.subtract))
            link(dve.tensor_tensor(pcol(CIM), pcol(T1), pcol(DEN), ALU.mult))
            cre = pcol(CRE).unsqueeze(2).to_broadcast([P, NT, HG])
            cim = pcol(CIM).unsqueeze(2).to_broadcast([P, NT, HG])
            btmp = zst_c[0][:, 0:NT * HG].rearrange("p (t h) -> p t h", t=NT)
            link(dve.tensor_tensor(bb[:, 0], cre, b_raw[:, 0], ALU.mult))
            link(dve.tensor_tensor(btmp, cim, b_raw[:, 1], ALU.mult))
            link(dve.tensor_tensor(bb[:, 0], bb[:, 0], btmp, ALU.subtract))
            link(dve.tensor_tensor(bb[:, 1], cre, b_raw[:, 1], ALU.mult))
            link(dve.tensor_tensor(btmp, cim, b_raw[:, 0], ALU.mult))
            link(dve.tensor_tensor(bb[:, 1], bb[:, 1], btmp, ALU.add))
            to_hT(0)
            angles(0)
            angles(1)

            def stage_b(b):
                if b:
                    dve.wait_ge(zt_ps, 4 * b - 2)
                for i in range(2):
                    diag = zst_b[i].rearrange("p (t n) -> p t n", n=P + 2 * HG)
                    link(dve.tensor_copy(diag[0:NS, :, 0:HG], bb[0:NS, i, TPB * b:TPB * b + TPB, :]))
                    dve.tensor_copy(diag[NS:P, :, HG:2 * HG], bb[NS:P, i, TPB * b:TPB * b + TPB, :]
                                    ).then_inc(zst_done, 1)

            def stage_c(b):
                if b:
                    dve.wait_ge(zt_ps, 4 * b)
                for i in range(2):
                    dve.tensor_tensor(zst_c[i].rearrange("p (j n) -> p j n", j=8),
                                      c_raw[:, i, b, :].unsqueeze(1).to_broadcast([P, 8, NS]),
                                      chmask[:, :].unsqueeze(2).to_broadcast([P, 8, NS]), ALU.mult
                                      ).then_inc(zst_done, 1)
                dve.wait_ge(zst_done, 4 * b + 4)

            stage_b(0)
            stage_c(0)
            hT_evict(0)

            def bu(i):
                return ps[:, 4 + 2 * i:6 + 2 * i, :].rearrange("p a (t s) -> p (a t) s", t=2)

            for b in range(NBLK):
                q = b % 2
                dve.wait_ge(table_done, 2 * b + 2)
                dve.wait_ge(bu_ps, b + 1)
                if b:
                    dve.wait_ge(y5_ps, b)
                dve.tensor_tensor(prod[:, 0], bu(0), cosT[:, q], ALU.mult).then_inc(rot_done, 1)
                dve.tensor_tensor(prod[:, 1], bu(1), sinT[:, q], ALU.mult).then_inc(rot_done, 1)
                dve.tensor_tensor(prod2[:, 0], bu(1), cosT[:, q], ALU.mult).then_inc(rot_done, 1)
                dve.tensor_tensor(prod2[:, 1], bu(0), sinT[:, q], ALU.mult).then_inc(rot_done, 1)
                if b + 1 < NBLK:
                    stage_b(b + 1)
                for i, v in enumerate((v_re, v_im)):
                    dve.wait_ge(v_done, 2 * b + i + 1)
                    for t in range(TPB):
                        mag = par[:, MAG, TPB * b + t:TPB * b + t + 1].to_broadcast([P, SEQ])
                        dve.tensor_tensor_scan(v[:, t, :], mag, v[:, t, :], 0.0, ALU.mult, ALU.add
                                               ).then_inc(scan_done, 1)
                dve.wait_ge(scan_done, 2 * TPB * (b + 1))
                dve.tensor_tensor(prod[:, 0], v_re, cosT[:, q], ALU.mult).then_inc(dve_step, 1)
                dve.tensor_tensor(prod[:, 1], v_im, sinT[:, q], ALU.mult).then_inc(post_d, 1)
                count[0] += 1
                if b + 1 < NBLK:
                    stage_c(b + 1)
                if b + 2 < NBLK:
                    angles(b + 2)
                dve.wait_ge(y5_ps, b + 1)
                stt(uT[:, b, :], uT[:, b, :], cols[:, C_D + b:C_D + b + 1], ps[:, 3, 0:256], ALU.mult, ALU.add
                    ).then_inc(y5_done, 1)
            gate_row(0)
            for i in range(4):
                tt, n = divmod(i, 2)
                dve.wait_ge(sig_done, i + 1)
                dve.tensor_tensor(hn[:, tt, 512 * n:512 * n + 512], ps[:, 2 * i, :],
                                  junk[:, 512 * (i % 2):512 * (i % 2) + 512], ALU.mult).then_inc(glu_done, 1)
            dve.wait_ge(glu_done, 4)
            residual(0, lambda tt: hn[:, tt, :])
            to_hT(1)

            def w_rest(g, half):
                if g < PER_EXPERT:
                    dve.wait_ge(whi_done, 2 * g + half + 1)
                    w = ff_half(gran(N_FFN + g), half)
                    dve.tensor_tensor(ff_half(ring_lo[(N_FFN + g) % RING][:, :], half).bitcast(F32R), w, ff_half(w_hi[:, g % 2, :], half), ALU.subtract
                                      ).then_inc(wlo_done, 1)

            def a_rest(q, ch):
                dve.wait_ge(ahi_done, q + 1)
                dve.tensor_tensor(aT_lo[:, ch, :, :].rearrange("p k n -> p (k n)").bitcast(F32R),
                                  ps[:, T_BANK if ch else U_BANK, :], aT_hi[:, ch, :, :].rearrange("p k n -> p (k n)"),
                                  ALU.subtract).then_inc(aT_done, 2)

            def product_out(f, ch):
                q = 2 * f + (0 if ch else 1)
                dve.wait_ge(silu_done, q + 1)
                if ch:
                    dve.wait_ge(up1_done, f + 1)
                else:
                    wait_used(dve, N_FFN + up_at(f))
                above(dve, tr_done, q - 1)
                dve.tensor_tensor(a_ff[:, ch, :], silu_ff[:, ch, :], ps[:, U_BANK if ch else T_BANK, :], ALU.mult
                                  ).then_inc(act_done, 1)

            w_rest(0, 0)
            w_rest(0, 1)
            hT_evict(1)
            for h in range(2):
                dve.wait_ge(xhi_done, h + 1)
                x = hT[:, 4 * h:4 * h + 4, :]
                dve.tensor_tensor(x_lo[:, 4 * h:4 * h + 4, :].bitcast(F32R), x, x_hi[:, 4 * h:4 * h + 4, :], ALU.subtract).then_inc(xlo_done, 1)
            for f in range(FB):
                g = gate_at(f)
                if f:
                    a_rest(2 * f - 2, 1)
                w_rest(g + 1, 0)
                w_rest(g + 1, 1)
                if f:
                    a_rest(2 * f - 1, 0)
                w_rest(g + 2, 0)
                product_out(f, 1)
                w_rest(g + 2, 1)
                product_out(f, 0)
                for n in range(g + 3, gate_at(f + 1) + 1):
                    w_rest(n, 0)
                    w_rest(n, 1)
            a_rest(2 * FB - 2, 1)
            a_rest(2 * FB - 1, 0)
            gate_row(1)
            residual(1, y_banks)
            to_hT(2)
            hT_evict(2)
            for n in range(2):
                wait_used(dve, N_QKV + 4 + n)
                for tt in range(TT):
                    dve.tensor_copy(v_sb[:, tt, 512 * n:512 * n + 512], ps[:, Y_BANK + 2 * tt + n, :]
                                    ).then_inc(v_out, 1)

            def on_diagonal(z):
                return z.rearrange("p g (b n) -> p g b n", b=3)[:, :, 0:3:2, :]

            mask = strict[:, :].unsqueeze(1).unsqueeze(1).to_broadcast([P, 2, 2, P])

            def minus_abs(h):
                z = z_w[:, h % 3]
                dve.wait_ge(zcopy_done, h + 1)
                if h >= 2:
                    dve.wait_ge(sp_done, h - 1)
                stt(z_e[:, h % 2], z, -1.0, z, ALU.mult, ALU.min).then_inc(zabs_done, 1)

            minus_abs(0)
            for h in range(HEADS // 2 + 1):
                if h < HEADS // 2:
                    b = h % 2
                    z = z_w[:, h % 3]
                    dve.wait_ge(ln_done, h + 1)
                    if h >= 2:
                        dve.wait_ge(sfx_ps, h - 1)
                    stt(z_p[:, b], z, 0.0, z_e[:, b], ALU.max, ALU.add).then_inc(sp_done, 1)
                    dve.wait_ge(sp_done, h + 1)
                    dve.tensor_tensor(on_diagonal(z_p[:, b]), on_diagonal(z_p[:, b]), mask, ALU.mult
                                      ).then_inc(spm_done, 1)
                if h + 1 < HEADS // 2:
                    minus_abs(h + 1)
                if h:
                    dve.wait_ge(wexp_done, h)
                    for g in range(2):
                        w = on_diagonal(z_w[:, (h - 1) % 3])[:, g]
                        stt(w, w, 1.0, mask[:, g], ALU.min, ALU.mult).then_inc(w_done, 1)
                if h < HEADS // 2:
                    dve.wait_ge(sfx_ps, h + 1)
                    z = z_w[:, h % 3]
                    stt(z, ps[:, 4:6, 0:384], -1.0, z, ALU.mult, ALU.add).then_inc(arg_done, 1)
            gate_row(2)
            residual(2, y_banks)
            to_hT(3)
            hT_evict(3)
            dve.memset(macc, 0.0).then_inc(sc_done, 4)
            for i, w in enumerate((32, 64)):
                link(dve.tensor_reduce(fold[:, i, 0:w], ident[:, :].rearrange("p (g s) -> p s g", s=w), AX.X, ALU.add))
                dst = fold[:, i, :].rearrange("p (g s) -> p g s", s=w)
                link(dve.tensor_copy(dst[:, 1:, :], fold[:, i, 0:w].unsqueeze(1).to_broadcast([P, P // w - 1, w])))
                link(dve.tensor_copy(slots[:, i, :].rearrange("p (g s) -> p g s", s=w),
                                     steps[:, 0:w].unsqueeze(1).to_broadcast([P, SEQ // w, w])))
            link(dve.tensor_copy(slots[:, 2, 0:P], steps[:, 0:P]))
            link(dve.memset(rcol[:, NE, :], -1.0))
            link(dve.tensor_copy(slots[:, 2, P:].rearrange("p (g s) -> p g s", s=32),
                                 steps[:, P:P + 32].unsqueeze(1).to_broadcast([P, 4, 32])))
            for tt in range(TT):
                r = rt[:, tt]
                dve.wait_ge(lg_ps, 1)
                link(dve.tensor_copy(r[:, 0:8], ps[:, S_BANK, 8 * tt:8 * tt + 8]))
                link(dve.tensor_reduce(r[:, 82:83], r[:, 0:8], AX.X, ALU.max))
                dve.tensor_scalar(r[:, 80:81], r[:, 82:83], -1.0, None, ALU.mult).then_inc(lmax_done, 1)
            for tt in range(TT):
                r = rt[:, tt]
                dve.wait_ge(pexp_done, tt + 1)
                link(dve.reciprocal(r[:, 81:82], r[:, 81:82]))
                link(dve.tensor_scalar(r[:, 8:16], r[:, 8:16], r[:, 81:82], None, ALU.mult))
                link(dve.max(r[:, 16:24], r[:, 8:16]))
                link(dve.max_index(r[:, 24:32].bitcast(U32), r[:, 16:24], r[:, 8:16]))
                link(dve.tensor_tensor(r[:, 84:85], r[:, 16:17], r[:, 17:18], ALU.add))
                link(dve.reciprocal(r[:, 84:85], r[:, 84:85]))
                link(dve.tensor_scalar(r[:, 82:84], r[:, 16:18], r[:, 84:85], None, ALU.mult))
                link(dve.tensor_copy(r[:, 86:88], r[:, 24:26].bitcast(U32)))
                for j in range(2):
                    link(dve.tensor_scalar(r[:, 32 + 8 * j:40 + 8 * j], steps[:, 0:8], r[:, 86 + j:87 + j], None,
                                           ALU.is_equal))
                link(dve.tensor_tensor(r[:, 48:56], r[:, 32:40], r[:, 40:48], ALU.add))
                link(dve.tensor_scalar(r[:, 32:40], r[:, 32:40], r[:, 82:83], None, ALU.mult))
                stt(rcol[:, 0:NE, 2 + tt], r[:, 40:48], r[:, 83:84], r[:, 32:40], ALU.mult, ALU.add).then_inc(sel_done, 1)
            dve.wait_ge(rank_ps, 1)
            for tt in range(TT):
                r = rt[:, tt]
                link(stt(r[:, 56:64], ps[:, S_BANK, 16 + 8 * tt:24 + 8 * tt], 1.0, r[:, 48:56], ALU.add, ALU.mult))
                link(dve.tensor_scalar(rcol[:, 0:NE, tt], r[:, 56:64], 1.0, None, ALU.subtract))
            one, two, before, kinds = (cnt[0:1, i, :] for i in range(4))
            total = ps[0:1, S_BANK, 32:40]
            link(dve.memset(one, 1.0))
            link(dve.tensor_scalar(two, total, P + 0.5, None, ALU.is_gt))
            link(dve.tensor_scalar(kinds, total, P + 32.5, None, ALU.is_gt))
            for limit in (64.5, 32.5):
                link(stt(kinds, total, limit, kinds, ALU.is_gt, ALU.add))
            link(dve.tensor_tensor(kinds, kinds, two, ALU.add))
            link(dve.tensor_tensor_scan(before, one, two, 0.0, ALU.mult, ALU.add))
            link(dve.tensor_tensor(before, before, two, ALU.subtract))
            link(dve.tensor_scalar(before, before, 1.0, float(FB), ALU.add, ALU.mult))
            dve.tensor_copy(cnt_i[:, :, :], cnt[0:1, 1:4, :]).then_inc(route_done, 1)
            dve.wait_ge(route_done, 1)

            def one_hot(e):
                dve.tensor_copy(pick, rcol[:, bass.ds(e, 1), :]).then_inc(pick_done, 1)
                dve.wait_ge(pick_done, e + 1)
                for tt in range(TT):
                    dve.tensor_scalar(g1[:, tt], steps[:, :], pick[:, 0, tt:tt + 1], None, ALU.is_equal
                                      ).then_inc(onehot_done, 1)

            one_hot(0)
            with dve.Fori(0, NE) as e:
                nch, more, items2, c1, kind, by_width = expert_counts(dve, e)
                moe_turn = lambda g: e * (PER_EXPERT // RING) + (N_MOE + g) // RING

                def weighted(numbers):
                    for tt in range(TT):
                        dve.tensor_scalar(gw[:, tt], numbers, pick[:, 0, tt:tt + 1], pick[:, 0, 2 + tt:3 + tt],
                                          ALU.is_equal, ALU.mult).then_inc(weighted_done, 1)

                with dve.If(kind > 3):
                    weighted(steps[:, :])
                with dve.Else():
                    with dve.If(kind > 1):
                        weighted(slots[:, 2])
                    with dve.Else():
                        with dve.If(kind > 0):
                            weighted(slots[:, 1])
                        with dve.Else():
                            weighted(slots[:, 0])

                def xe_out(ch):
                    bank = (U_BANK, S_BANK)[ch]
                    for k in range(KD // 2, KD):
                        ins = dve.tensor_scalar(xe[:, k, ch, :], ps[:, bank, P * (k % 4):P * (k % 4) + P],
                                                scale_c[:, 3, k:k + 1], shift_col(3, k), ALU.mult, ALU.add)
                    return ins

                with dve.If(nch > 1):
                    dve.wait_ge(xe_ps, 2 * e + 2)
                    xe_out(1)
                dve.wait_ge(xe_ps, 2 * e + 2)
                xe_out(0).then_inc(xe_dve, 1)
                with dve.If(nch > 1):
                    dve.wait_ge(st_ps, e + 1)
                    dve.tensor_copy(scT[:, 1, :], ps[:, Y_BANK + 3, 256:512])
                dve.wait_ge(st_ps, e + 1)
                dve.tensor_copy(scT[:, 0, :], ps[:, Y_BANK + 3, 0:256]).then_inc(st_done, 1)
                for f in range(FB + 1):
                    q2 = items2 + f * nch

                    def item(ch, width):
                        before = q2 if ch else q2 + 1
                        if f and width < P:
                            narrow_aT(before, ch, width)
                        if f < FB:
                            swiglu_out(f, q2 + 2 if ch else q2 + more + 2, ch, N_MOE, moe_turn, c1,
                                       before + 1 if f else None, width)

                    by_width(item)
                one_hot(e + 1)
                with dve.If(nch > 1):
                    wait_used(dve, N_MOE + PER_EXPERT - 1, moe_turn(PER_EXPERT - 1))
                    dve.tensor_copy(ysb[:, 1, 512:D], ps[:, Y_BANK + 3, :])
                wait_used(dve, N_MOE + PER_EXPERT - 1, moe_turn(PER_EXPERT - 1))
                dve.tensor_copy(ysb[:, 0, 512:D], ps[:, Y_BANK + 1, :]).then_inc(ysb_dve, 1)
                for i in range(4):
                    tt, n = divmod(i, 2)
                    dve.wait_ge(sc_ps, 4 * e + i + 1)
                    m = macc[:, tt, 512 * n:512 * n + 512]
                    dve.tensor_tensor(m, m, ps[:, T_BANK + i % 2, :], ALU.add).then_inc(sc_done, 1)
                dve.wait_ge(sc_done, 4 * e + 8)
            gate_row(3)
            residual(3, lambda tt: macc[:, tt, :])

        @block.tensor
        def _(pe):
            def columns(dst, src, n):
                return pe.transpose(dst, src, ident[0:n, 0:n])

            pe.wait_ge(consts_done, 6)
            pe.wait_ge(cols_ready, 1)
            columns(ps[:, 0, C_C:C_C + KD], r_c, KD)
            columns(ps[:, 0, C_LRE:C_LRE + NT], r_lam[:, 0, :], NT)
            columns(ps[:, 0, C_LIM:C_LIM + NT], r_lam[:, 1, :], NT)
            columns(ps[:, 0, C_LS:C_LS + NT], rows[0:NT, 512:640], NT)
            columns(ps[:, 0, C_D:C_D + NBLK], r_d, NBLK)
            for k in range(KD):
                ins = columns(ps[:, 0, C_G + 8 * k:C_G + 8 * k + 8], r_g[:, P * k:P * k + P], 8)
            ins.then_inc(cols_ps, 1)
            for j in range(4):
                ins = columns(ps[:, 1, 24 * j:24 * j + 24], r_b[:, P * j:P * j + P], 24)
            ins.then_inc(cols_ps, 1)

            def ada(lo, hi):
                for i in range(lo, hi):
                    n = ada_place(*divmod(i, MODS))
                    wait_landed(pe, n)
                    above(pe, part_out, i)
                    for k in range(KD):
                        j = k % 4
                        ins = pe.matmul(ps[32 * j:32 * j + 32, 0, :], c32[:, k, :], gran8(n)[:, k, :],
                                        start=k < 4, stop=k >= 4, tile_position=(0, 32 * j))
                    ins.then_inc(used[n % RING], 1)
                    pe.wait_ge(part_out, i + 1)
                    above(pe, mod_out, i)
                    for j in range(4):
                        ins = pe.matmul(ps[:, 1, j:j + 1], part[:, P * j:P * j + P], inv32[:, :],
                                        start=True, stop=True)
                    ins.then_inc(mod_ps, 1)

            def transpose_x(s):
                pe.wait_ge(xn_done, 2 * s + 2)
                for k in range(KD):
                    for tt in range(TT):
                        ins = pe.transpose(ps[:, Y_BANK + k // 2, 256 * (k % 2) + P * tt:256 * (k % 2) + P * tt + P],
                                           hn[:, tt, P * k:P * k + P], ident[:, :])
                    if k % 2:
                        ins.then_inc(hT_ps, 1)

            def wait_hT(s):
                pe.wait_ge(hT_act, 4 * s + 4)
                pe.wait_ge(hT_dve, 4 * s + 4)

            def gate_row(s):
                pe.wait_ge(diag_done, s + 1)
                for n in range(2):
                    ins = pe.matmul(ps[:, 2 + n, :], ones[:, :], tbuf[:, 512 * n:512 * n + 512], start=True, stop=True)
                ins.then_inc(gg_ps, 1)

            def product(bank, ch, xT, weights, width):
                shares = P // width
                for k in range(KD):
                    r = width * (k % shares)
                    ins = pe.matmul(ps[r:r + width, bank, :], xT(k, ch)[:, 0:width], weights[:, k, :],
                                    start=k < shares, stop=k >= KD - shares,
                                    **({} if width == P else dict(tile_position=(0, r))))
                return ins

            def gate_product(f, q2, ch, xT, base, turn, width):
                n = base + gate_at(f)
                wait_landed(pe, n, turn(gate_at(f)))
                above(pe, silu_done, q2 + 2)
                product(G_BANK, ch, xT, gran8(n), width).then_inc(gate1_done if ch else used[n % RING], 1)

            def up_product(f, q2, ch, xT, base, turn, width):
                n = base + up_at(f)
                wait_landed(pe, n, turn(up_at(f)))
                above(pe, act_done, q2 + 2)
                product(U_BANK, ch, xT, gran8(n), width).then_inc(up1_done if ch else used[n % RING], 1)

            def turn_item(q, ch, width=P):
                pe.wait_ge(act_done, q + 1)
                above(pe, aT_done, q * 2)
                if width < P:
                    pe.wait_ge(silu_done, q + 1)
                    for bank, parts in ((T_BANK, g_part), (S_BANK, a_sb)):
                        for j in range(4):
                            ins = pe.matmul(ps[:, bank, P * j:P * j + P], parts[:, ch, P * j:P * j + P],
                                            fold[:, (32, 64).index(width), :], start=True, stop=True)
                    ins.then_inc(tr_done, 1)
                    return
                for j in range(4):
                    ins = pe.transpose(ps[:, T_BANK, P * j:P * j + P], a_sb[:, ch, P * j:P * j + P], ident[:, :])
                ins.then_inc(tr_done, 1)

            def down_product(f, q, ch, base, turn, width=P):
                n = base + down_at(f)
                wait_landed(pe, n, turn(down_at(f)))
                pe.wait_ge(aT_done, q * 2 + 2)
                shares = P // width
                for j, h in [(j, h) for j in range(4) for h in range(2)] if width == P else \
                        [(j, h) for h in range(2) for j in range(4)]:
                    r = width * (j % shares)
                    ins = pe.matmul(ps[r:r + width, Y_BANK + 2 * ch + h, :], aT[:, ch, j, 0:width],
                                    gran4(n)[:, j, 512 * h:512 * h + 512],
                                    start=f == 0 and j < shares, stop=f == FB - 1 and j >= 4 - shares,
                                    **({} if width == P else dict(tile_position=(0, r))))
                if not ch:
                    ins.then_inc(used[n % RING], 1)

            def item(f, q2, before, ch, xT, base, turn, width=P):
                if f < FB:
                    gate_product(f, q2, ch, xT, base, turn, width)
                if f:
                    turn_item(before, ch, width)
                if f < FB:
                    up_product(f, q2, ch, xT, base, turn, width)
                if f:
                    down_product(f - 1, before, ch, base, turn, width)

            pe.wait_ge(cols_done, 1)
            pe.wait_ge(c32_done, 1)
            transpose_x(0)
            ada(0, 4)
            wait_hT(0)
            wait_landed(pe, N_WIN)
            for b in range(NBLK):
                for k in range(KD):
                    ins = pe.matmul(ps[:, b // 2, 256 * (b % 2):256 * (b % 2) + 256],
                                    gran8(N_WIN)[:, k, P * b:P * b + P], hT[:, k, :], start=k == 0, stop=k == KD - 1)
                if b == 1:
                    ins.then_inc(u_ps, 1)
                    pe.wait_ge(mod_out, 4)
                elif b == 3:
                    ins.then_inc(used[N_WIN % RING], 1)

            def turn_staged(b, parts):
                for i in parts:
                    pe.wait_ge(zst_done, 4 * b + i + 1)
                    above(pe, zt_done, 5 * b + (0, 1, 2, 4)[i])
                    for t in range(TPB):
                        ins = pe.transpose(ps[:, T_BANK, P * t:P * t + P],
                                           (zst_b + zst_c)[i][:, P * t:P * t + P], ident[:, :])
                    ins.then_inc(zt_ps, 1)

            def b_products(b):
                turn_staged(b, (0, 1))
                pe.wait_ge(zt_done, 5 * b + 2)
                pe.wait_ge(u_done, 2)
                above(pe, rot_done, 4 * b)
                for i in range(2):
                    for t in range(TPB):
                        ins = pe.matmul(ps[:, 4 + 2 * i + t // 2, 256 * (t % 2):256 * (t % 2) + 256],
                                        bT[:, i, t, :], uT[:, b, :], start=True, stop=True)
                ins.then_inc(bu_ps, 1)

            b_products(0)
            turn_staged(0, (2, 3))
            for b in range(NBLK):
                ada(4 + 5 * b, 6 + 5 * b)
                if b + 1 < NBLK:
                    b_products(b + 1)
                ada(6 + 5 * b, 7 + 5 * b)
                pe.wait_ge(zt_done, 5 * b + 5)
                pe.wait_ge(post_d, b + 1)
                pe.wait_ge(post_p, 2 * b + 2)
                above(pe, y5_done, b)
                terms = ((0, prod[:, 0]), (1, prod[:, 1]), (2, prod2[:, 0]), (2, prod2[:, 1]))
                for j, (i, state) in enumerate(terms):
                    for t in range(TPB):
                        ins = pe.matmul(ps[:, 3, 0:256], cT[:, i, t, :], state[:, t, :],
                                        start=j == 0 and t == 0, stop=j == 3 and t == TPB - 1)
                ins.then_inc(y5_ps, 1)
                if b + 1 < NBLK:
                    turn_staged(b + 1, (2, 3))
                ada(7 + 5 * b, 9 + 5 * b)
            gate_row(0)
            pe.wait_ge(gelu_done, 4)
            for i in range(4):
                tt, n = divmod(i, 2)
                if i == 1:
                    pe.wait_ge(gg_done, 1)
                for half in range(2):
                    wait_landed(pe, N_WOUT + half)
                    for k in range(NBLK):
                        ins = pe.matmul(ps[:, 2 * i + half, :], uT[:, k, P * tt:P * tt + P],
                                        gran4(N_WOUT + half)[:, k, 512 * n:512 * n + 512],
                                        start=k == 0, stop=k == NBLK - 1)
                    if i == 3:
                        ins.then_inc(used[(N_WOUT + half) % RING], 1)
                    elif half:
                        ins.then_inc(wo_ps, 1)
            transpose_x(1)
            wait_hT(1)
            tokens = lambda k, ch: hT[:, k, P * ch:P * ch + P]

            def split_product(dst, stationary, moving, start, stop):
                for i, (a, b) in enumerate(((0, 0), (0, 1), (1, 0))):
                    ins = pe.matmul(dst, stationary[a].bitcast(F32R), moving[b].bitcast(F32R),
                                    start=start and i == 0, stop=stop and i == 2)
                return ins

            def ff_weights(g, k, cols):
                return tuple(w.rearrange("p (k n) -> p k n", n=cols)[:, k, :] for w in
                             (w_hi[:, g % 2, :], ring_lo[(N_FFN + g) % RING][:, :]))

            def ff_in(g, bank, ch):
                for k in range(KD):
                    if k % 4 == 0:
                        pe.wait_ge(wlo_done, 2 * g + k // 4 + 1)
                    x = slice(P * ch, P * ch + P)
                    ins = split_product(ps[:, bank, :], (x_hi[:, k, x], x_lo[:, k, x]), ff_weights(g, k, 512),
                                        k == 0, k == KD - 1)
                return ins

            def ff_turn(q, ch, bank):
                for j in range(4):
                    ins = pe.transpose(ps[:, bank, P * j:P * j + P], a_ff[:, ch, P * j:P * j + P], ident[:, :])
                ins.then_inc(tr_done, 1)

            def ff_down(f):
                g = down_at(f)
                pe.wait_ge(wlo_done, 2 * g + 2)
                for ch in (1, 0):
                    pe.wait_ge(aT_done, 4 * f + (2 if ch else 4))
                    for j in range(4):
                        w = ff_weights(g, j, D)
                        for h in range(2):
                            ins = split_product(ps[:, Y_BANK + 2 * ch + h, :], (aT_hi[:, ch, j, :], aT_lo[:, ch, j, :]),
                                                [x[:, 512 * h:512 * h + 512] for x in w],
                                                f == 0 and j == 0, f == FB - 1 and j == 3)
                ins.then_inc(used[(N_FFN + g) % RING], 1)

            pe.wait_ge(xlo_done, 2)
            for f in range(FB):
                g = gate_at(f)
                if f:
                    pe.wait_ge(act_done, 2 * f)
                    ff_turn(2 * f - 2, 1, T_BANK)
                    pe.wait_ge(silu_done, 2 * f - 1)
                ff_in(g, G_BANK, 1).then_inc(gate1_done, 1)
                if f:
                    ff_turn(2 * f - 1, 0, U_BANK)
                    pe.wait_ge(silu_done, 2 * f)
                ff_in(g, S_BANK, 0).then_inc(used[(N_FFN + g) % RING], 1)
                above(pe, aT_done, 4 * f)
                ff_in(g + 1, U_BANK, 1).then_inc(up1_done, 1)
                ff_in(g + 1, T_BANK, 0).then_inc(used[(N_FFN + g + 1) % RING], 1)
                if f:
                    ff_down(f - 1)
            pe.wait_ge(act_done, 2 * FB)
            ff_turn(2 * FB - 2, 1, T_BANK)
            ff_turn(2 * FB - 1, 0, U_BANK)
            ff_down(FB - 1)
            pe.wait_ge(aT_done, 4 * FB)
            gate_row(1)
            transpose_x(2)
            wait_hT(2)
            for r in range(4):
                n = N_QKV + r
                wait_landed(pe, n)
                above(pe, qk_done, r - 1)
                if r == 1:
                    pe.wait_ge(gg_done, 2)
                for j in range(4):
                    for k in range(KD):
                        ins = pe.matmul(ps[:, 2 * (r % 2) + j // 2, 256 * (j % 2):256 * (j % 2) + 256],
                                        gran8(n)[:, k, P * j:P * j + P], hT[:, k, :], start=k == 0, stop=k == KD - 1)
                ins.then_inc(used[n % RING], 1)
            for r in range(2):
                n = N_QKV + 4 + r
                wait_landed(pe, n)
                for tt in range(TT):
                    for k in range(KD):
                        ins = pe.matmul(ps[:, Y_BANK + 2 * tt + r, :], tokens(k, tt), gran8(n)[:, k, :],
                                        start=k == 0, stop=k == KD - 1)
                ins.then_inc(used[n % RING], 1)

            def scores(h):
                b = h % 2
                pe.wait_ge(qk_done, 4)
                if h >= 2:
                    pe.wait_ge(zcopy_done, h - 1)
                for g in range(2):
                    r = slice(DH * g, DH * g + DH)
                    pe.matmul(ps[:, 2 * b + g, 0:256], kT[r, h, 0:P], qT[r, h, :], start=True, stop=True)
                    ins = pe.matmul(ps[:, 2 * b + g, 256:384], kT[r, h, P:SEQ], qT[r, h, P:SEQ], start=True, stop=True)
                ins.then_inc(z_ps, 1)

            def suffix(h):
                b = h % 2
                pe.wait_ge(spm_done, h + 1)
                if h:
                    pe.wait_ge(arg_done, h)
                else:
                    pe.wait_ge(v_out, 4)
                for g in range(2):
                    z = z_p[:, b, g]
                    pe.matmul(ps[:, 4 + g, 0:256], incl[:, :], z[:, 0:256], start=True, stop=False)
                    pe.matmul(ps[:, 4 + g, P:256], ones[:, :], z[:, 256:384], start=False, stop=True)
                    ins = pe.matmul(ps[:, 4 + g, 256:384], incl[:, :], z[:, 256:384], start=True, stop=True)
                ins.then_inc(sfx_ps, 1)

            def values(h):
                b = h % 2
                pe.wait_ge(w_done, 2 * h + 2)
                if h >= 2:
                    pe.wait_ge(o_done, h - 1)
                for g in range(2):
                    hd = slice(DH * (2 * h + g), DH * (2 * h + g) + DH)
                    o = ps[DH * g:DH * g + DH, 6 + b, :]
                    pe.matmul(o[:, 0:256], v_sb[:, 0, hd], z_w[:, h % 3, g, 0:256], start=True, stop=False)
                    ins = pe.matmul(o[:, P:256], v_sb[:, 1, hd], z_w[:, h % 3, g, 256:384], start=False, stop=True)
                ins.then_inc(o_ps, 1)

            for h in range(HEADS // 2 + 2):
                if h < HEADS // 2:
                    scores(h)
                if 1 <= h <= HEADS // 2:
                    suffix(h - 1)
                if h >= 2:
                    values(h - 2)
            pe.wait_ge(o_done, HEADS // 2)
            for r in range(2):
                n = N_SBOUT + r
                wait_landed(pe, n)
                for tt in range(TT):
                    for k in range(KD):
                        ins = pe.matmul(ps[:, Y_BANK + 2 * tt + r, :], oT[:, k, P * tt:P * tt + P], gran8(n)[:, k, :],
                                        start=k == 0, stop=k == KD - 1)
                ins.then_inc(used[n % RING], 1)
            gate_row(2)
            transpose_x(3)
            wait_hT(3)
            pe.wait_ge(router_in, 32)
            pe.wait_ge(gg_done, 3)
            for tt in range(TT):
                lg = ps[:, S_BANK, 8 * tt:8 * tt + 8]
                for k in range(KD):
                    pe.matmul(lg, tokens(k, tt), wr_sb[:, k, :], start=k == 0, stop=False)
                ins = pe.matmul(lg, ones[0:1, :], br_sb[:, :], start=False, stop=True)
            ins.then_inc(lg_ps, 1)
            pe.wait_ge(sel_done, 2)
            chosen = [rt[:, tt, 48:56] for tt in range(TT)]
            rank = lambda i: ps[:, S_BANK, 16 + 8 * i:24 + 8 * i]
            pe.matmul(rank(0), strict[:, :], chosen[0], start=True, stop=True)
            pe.matmul(rank(1), ones[:, :], chosen[0], start=True, stop=False)
            pe.matmul(rank(1), strict[:, :], chosen[1], start=False, stop=True)
            pe.matmul(rank(2), ones[:, :], chosen[0], start=True, stop=False)
            pe.matmul(rank(2), ones[:, :], chosen[1], start=False, stop=True).then_inc(rank_ps, 1)

            gathered = lambda k, ch: xe[:, k, ch, :]
            pe.wait_ge(route_done, 1)
            with pe.Fori(0, NE) as e:
                nch, more, items2, _, _, by_width = expert_counts(pe, e)
                moe_turn = lambda g: e * (PER_EXPERT // RING) + (N_MOE + g) // RING
                pe.wait_ge(onehot_done, 2 * e + 2)
                pe.wait_ge(silu_done, items2 + 2)
                pe.wait_ge(act_done, items2 + 2)
                pe.wait_ge(aT_done, items2 * 2 + 4)
                pe.wait_ge(sc_done, 4 * e + 4)

                def gather(ch):
                    for k in range(KD):
                        bank = (G_BANK, T_BANK)[ch] + k // 4
                        for tt in range(TT):
                            ins = pe.matmul(ps[:, bank, P * (k % 4):P * (k % 4) + P], hn[:, tt, P * k:P * k + P],
                                            g1[:, tt, P * ch:P * ch + P], start=tt == 0, stop=tt == TT - 1)
                        if not ch and k % 4 == 3:
                            ins.then_inc(xe_ps, 1)

                def scatter_weights(ch):
                    for tt in range(TT):
                        ins = pe.transpose(ps[:, Y_BANK + 3, 256 * ch + P * tt:256 * ch + P * tt + P],
                                           gw[:, tt, P * ch:P * ch + P], ident[:, :])
                    return ins

                with pe.If(nch > 1):
                    gather(1)
                gather(0)
                pe.wait_ge(weighted_done, 2 * e + 2)
                with pe.If(nch > 1):
                    scatter_weights(1)
                scatter_weights(0).then_inc(st_ps, 1)
                pe.wait_ge(xe_done, e + 1)
                pe.wait_ge(xe_dve, e + 1)
                pe.wait_ge(st_done, e + 1)
                for f in range(FB + 1):
                    q2 = items2 + f * nch
                    by_width(lambda ch, width: item(f, q2 if ch else q2 + more, q2 if ch else q2 + 1, ch, gathered,
                                                    N_MOE, moe_turn, width))
                pe.wait_ge(ysb_act, e + 1)
                pe.wait_ge(ysb_dve, e + 1)
                for i in range(4):
                    tt, n = divmod(i, 2)
                    if i >= 2:
                        pe.wait_ge(sc_done, 4 * e + i + 3)
                    dst = ps[:, T_BANK + i % 2, :]

                    def spread(ch, start, stop):
                        return pe.matmul(dst, scT[:, ch, P * tt:P * tt + P], ysb[:, ch, 512 * n:512 * n + 512],
                                         start=start, stop=stop)

                    with pe.If(nch > 1):
                        spread(1, True, False)
                        spread(0, False, True).then_inc(sc_ps, 1)
                    with pe.Else():
                        spread(0, True, True).then_inc(sc_ps, 1)
            pe.wait_ge(sc_done, 4 * NE + 4)
            gate_row(3)


_INS = ["x", "c", "ada_w", "ada_b", "norm_g", "s5_w_in", "s5_lambda_re", "s5_lambda_im", "s5_b_re", "s5_b_im",
        "s5_c_re", "s5_c_im", "s5_d", "s5_log_step", "s5_w_out", "sb_w_qkv", "sb_w_out", "ffn_w_gate_up",
        "ffn_w_down", "moe_w_router", "moe_b_router", "moe_w_gate_up", "moe_w_down"]


def kernel(**inputs):
    import numpy as np
    import concourse.bacc as bacc
    from concourse.bass_utils import run_bass_kernel_spmd

    nc = bacc.Bacc("TRN2", target_bir_lowering=False, num_devices=1)
    arrays, args = {}, []
    for name in _INS:
        a = np.ascontiguousarray(inputs[name])
        arrays[f"in_{name}_dram"] = a
        args.append(nc.dram_tensor(f"in_{name}_dram", a.shape, mybir.dt.from_np(a.dtype), kind="ExternalInput").ap())
    args.append(nc.dram_tensor("out_dram", (1, SEQ, D), F32, kind="ExternalOutput").ap())
    program(nc, *args)
    r = run_bass_kernel_spmd(nc, [arrays], core_ids=[0])
    return r.results[0]["out_dram"]
```
